# Optimizing a Trainium2 kernel written in Bass

```python
import math
import jax, jax.numpy as jnp
from jax import lax
import numpy as np

D_MODEL = 1024
BATCH = 1
SEQ = 512
DEPTH = 1
DEC_BATCH = 1
DEC_SEQ = 32
PAST_LEN = 1024

CHUNK = 64
Q_BLOCK = 128
EPS = 1e-6
GLA_HEADS = 4
GLA_DK = D_MODEL // 2 // GLA_HEADS
GLA_DV = D_MODEL // GLA_HEADS
GLA_RANK = 16
GLA_TAU = 16.0
GLA_CHUNK = 64
DIFF_HEADS = 8
DIFF_DH = D_MODEL // DIFF_HEADS // 2
DIFF_DV = 2 * DIFF_DH
N_GROUPS = 4
EXPERTS_PER_GROUP = 4
N_EXPERTS = N_GROUPS * EXPERTS_PER_GROUP
TOP_K = 2
D_EXPERT = 512
EXPERT_BLOCK = 128
GLA_QK = GLA_HEADS * GLA_DK
GLA_V = GLA_HEADS * GLA_DV
DIFF_QK = DIFF_HEADS * 2 * DIFF_DH
DIFF_V = DIFF_HEADS * DIFF_DV
IN_SIZES = (GLA_QK, GLA_QK, GLA_V, GLA_V, GLA_RANK, DIFF_QK, DIFF_QK, DIFF_V, D_MODEL, D_MODEL)
D_IN = sum(IN_SIZES)

kernel_name = "gla_diffattn_hmoe_streaming_step"

def rms_norm(x, g):
    xf = x.astype(jnp.float32)
    y = xf * lax.rsqrt(jnp.mean(xf * xf, axis=-1, keepdims=True) + EPS)
    return (y * g.astype(jnp.float32)).astype(x.dtype)

def alibi_slopes(n):
    return jnp.asarray([2.0 ** (-8.0 * (h + 1) / n) for h in range(n)], jnp.float32)

def gla_scan(q, k, v, log_a, s0, chunk):
    B, L, H, dk = q.shape
    dv = v.shape[-1]
    n = L // chunk

    def to_chunks(t):
        return t.astype(jnp.float32).reshape(B, n, chunk, H, t.shape[-1]).transpose(1, 0, 3, 2, 4)

    qc = to_chunks(q) * (dk ** -0.5)
    kc, vc, gc = to_chunks(k), to_chunks(v), to_chunks(log_a)
    causal = jnp.tril(jnp.ones((chunk, chunk), dtype=bool))

    def step(S, inp):
        qi, ki, vi, gi = inp
        b = jnp.cumsum(gi, axis=-2)
        b_last = b[..., -1:, :]
        q_t = qi * jnp.exp(b)
        k_t = ki * jnp.exp(-b)
        o = jnp.einsum('bhcd,bhde->bhce', q_t, S)
        att = jnp.where(causal, jnp.einsum('bhcd,bhsd->bhcs', q_t, k_t), 0.0)
        o = o + jnp.einsum('bhcs,bhse->bhce', att, vi)
        k_end = ki * jnp.exp(b_last - b)
        S = jnp.exp(b_last[..., 0, :])[..., None] * S + jnp.einsum('bhcd,bhce->bhde', k_end, vi)
        return S, o

    S, o = lax.scan(step, s0.astype(jnp.float32), (qc, kc, vc, gc))
    o = o.transpose(1, 0, 3, 2, 4).reshape(B, L, H, dv)
    return o, S

def diff_attention(q, k, v, q_pos, k_pos, lam, slopes):
    qf = q.astype(jnp.float32) * (DIFF_DH ** -0.5)
    kf = k.astype(jnp.float32)
    allowed = (k_pos[None, :] // CHUNK) <= (q_pos[:, None] // CHUNK)
    dist = jnp.abs(q_pos[:, None] - k_pos[None, :]).astype(jnp.float32)
    bias = jnp.where(allowed[None], -slopes[:, None, None] * dist[None], -jnp.inf)
    s1 = jnp.einsum('bqhd,bshd->bhqs', qf[..., :DIFF_DH], kf[..., :DIFF_DH]) + bias
    s2 = jnp.einsum('bqhd,bshd->bhqs', qf[..., DIFF_DH:], kf[..., DIFF_DH:]) + bias
    attn = jax.nn.softmax(s1, axis=-1) - lam * jax.nn.softmax(s2, axis=-1)
    return jnp.einsum('bhqs,bshe->bqhe', attn, v.astype(jnp.float32))

def hmoe(h, w_rg, b_rg, w_re, b_re, w_gate, w_up, w_down):
    B, L, D = h.shape
    T = B * L
    hf = h.reshape(T, D)
    g_logits = (hf @ w_rg + b_rg).astype(jnp.float32)
    g_prob = jax.nn.softmax(g_logits, axis=-1)
    g_sel = jnp.argmax(g_logits, axis=-1)
    p_g = jnp.take_along_axis(g_prob, g_sel[:, None], axis=-1)
    e_logits = (hf @ w_re + b_re).astype(jnp.float32).reshape(T, N_GROUPS, EXPERTS_PER_GROUP)
    idx = jnp.broadcast_to(g_sel[:, None, None], (T, 1, EXPERTS_PER_GROUP))
    e_logits = jnp.take_along_axis(e_logits, idx, axis=1)[:, 0]
    top_v, top_i = lax.top_k(e_logits, TOP_K)
    wts = jax.nn.softmax(top_v, axis=-1) * p_g
    eid = g_sel[:, None] * EXPERTS_PER_GROUP + top_i

    A = T * TOP_K
    flat_e = eid.reshape(A)
    flat_t = jnp.repeat(jnp.arange(T, dtype=jnp.int32), TOP_K)
    flat_w = wts.reshape(A)
    order = jnp.argsort(flat_e)
    se, st, sw = flat_e[order], flat_t[order], flat_w[order]
    counts = jnp.bincount(flat_e, length=N_EXPERTS)
    padded = ((counts + EXPERT_BLOCK - 1) // EXPERT_BLOCK) * EXPERT_BLOCK
    starts = jnp.cumsum(counts) - counts
    pad_ends = jnp.cumsum(padded)
    pad_starts = pad_ends - padded
    dest = pad_starts[se] + jnp.arange(A) - starts[se]
    n_blocks = -(-A // EXPERT_BLOCK) + N_EXPERTS
    P = n_blocks * EXPERT_BLOCK
    slot_tok = jnp.full((P,), T, jnp.int32).at[dest].set(st)
    slot_w = jnp.zeros((P,), jnp.float32).at[dest].set(sw)
    block_e = jnp.searchsorted(pad_ends, jnp.arange(n_blocks) * EXPERT_BLOCK, side='right')
    block_e = jnp.minimum(block_e, N_EXPERTS - 1)
    x_pad = jnp.concatenate([hf, jnp.zeros((1, D), hf.dtype)], axis=0)
    xb = x_pad[slot_tok].reshape(n_blocks, EXPERT_BLOCK, D)

    def expert_block(args):
        xi, e = args
        return (jax.nn.silu(xi @ w_gate[e]) * (xi @ w_up[e])) @ w_down[e]

    yb = lax.map(expert_block, (xb, block_e)).reshape(P, D)
    y = jnp.zeros((T + 1, D), jnp.float32).at[slot_tok].add(yb.astype(jnp.float32) * slot_w[:, None])
    return y[:T].astype(h.dtype).reshape(B, L, D)

def trunk_layer(x, p, s0, k_past, v_past, lam_init):
    B, L, _ = x.shape
    h = rms_norm(x, p['norm_mix'])
    z = h @ p['w_in']
    offsets = [int(o) for o in np.cumsum(IN_SIZES)[:-1]]
    qa, ka, va, ra, da, qb, kb, vb, ga, gb = jnp.split(z, offsets, axis=-1)

    log_a = jax.nn.log_sigmoid((da @ p['w_decay'] + p['b_decay']).astype(jnp.float32)) / GLA_TAU
    qa = qa.reshape(B, L, GLA_HEADS, GLA_DK)
    ka = ka.reshape(B, L, GLA_HEADS, GLA_DK)
    va = va.reshape(B, L, GLA_HEADS, GLA_DV)
    log_a = log_a.reshape(B, L, GLA_HEADS, GLA_DK)
    o_a, s_new = gla_scan(qa, ka, va, log_a, s0, min(GLA_CHUNK, L))
    o_a = rms_norm(o_a, p['gla_norm']).astype(x.dtype) * jax.nn.silu(ra.reshape(B, L, GLA_HEADS, GLA_DV))
    u_a = o_a.reshape(B, L, GLA_V) @ p['w_proj_a']

    qb = qb.reshape(B, L, DIFF_HEADS, 2 * DIFF_DH)
    kb = kb.reshape(B, L, DIFF_HEADS, 2 * DIFF_DH)
    vb = vb.reshape(B, L, DIFF_HEADS, DIFF_DV)
    lq1, lk1 = p['lambda_q1'].astype(jnp.float32), p['lambda_k1'].astype(jnp.float32)
    lq2, lk2 = p['lambda_q2'].astype(jnp.float32), p['lambda_k2'].astype(jnp.float32)
    lam = jnp.exp(jnp.sum(lq1 * lk1)) - jnp.exp(jnp.sum(lq2 * lk2)) + lam_init
    slopes = alibi_slopes(DIFF_HEADS)
    if k_past is None:
        pos = jnp.arange(L, dtype=jnp.int32)
        nqb = L // Q_BLOCK
        q_blocks = qb.reshape(B, nqb, Q_BLOCK, DIFF_HEADS, 2 * DIFF_DH).swapaxes(0, 1)
        pos_blocks = pos.reshape(nqb, Q_BLOCK)
        o_b = lax.map(lambda a: diff_attention(a[0], kb, vb, a[1], pos, lam, slopes), (q_blocks, pos_blocks))
        o_b = o_b.swapaxes(0, 1).reshape(B, L, DIFF_HEADS, DIFF_DV)
    else:
        past = k_past.shape[1]
        k_all = jnp.concatenate([k_past.astype(kb.dtype), kb], axis=1)
        v_all = jnp.concatenate([v_past.astype(vb.dtype), vb], axis=1)
        q_pos = past + jnp.arange(L, dtype=jnp.int32)
        k_pos = jnp.arange(past + L, dtype=jnp.int32)
        o_b = diff_attention(qb, k_all, v_all, q_pos, k_pos, lam, slopes)
    o_b = rms_norm(o_b, p['diff_norm']) * (1.0 - lam_init)
    u_b = o_b.astype(x.dtype).reshape(B, L, DIFF_V) @ p['w_proj_b']

    mix = jax.nn.sigmoid(ga) * u_a + jax.nn.sigmoid(gb) * u_b
    x = x + mix @ p['w_out']
    x = x + hmoe(rms_norm(x, p['norm_ffn']), p['w_router_group'], p['b_router_group'],
                 p['w_router_expert'], p['b_router_expert'], p['w_gate'], p['w_up'], p['w_down'])
    return x, s_new, kb, vb

def setup_inputs(seed: int = 0) -> dict:
    key = jax.random.key(seed)
    ks = jax.random.split(key, 32)
    f32 = jnp.float32

    def nrm(k, shape, s):
        return jax.random.normal(k, shape, f32) * s

    def gain(k, shape):
        return 1.0 + 0.02 * jax.random.normal(k, shape, f32)

    return {
        "x_prompt": nrm(ks[0], (BATCH, SEQ, D_MODEL), 1.0),
        "x_sample": nrm(ks[1], (DEC_BATCH, DEC_SEQ, D_MODEL), 1.0),
        "cache_k": nrm(ks[2], (DEPTH, DEC_BATCH, PAST_LEN, DIFF_HEADS, 2 * DIFF_DH), 1.0),
        "cache_v": nrm(ks[3], (DEPTH, DEC_BATCH, PAST_LEN, DIFF_HEADS, DIFF_DV), 1.0),
        "state_gla": nrm(ks[4], (DEPTH, DEC_BATCH, GLA_HEADS, GLA_DK, GLA_DV), 1.0),
        "norm_mix": gain(ks[5], (DEPTH, D_MODEL)),
        "w_in": nrm(ks[6], (DEPTH, D_MODEL, D_IN), D_MODEL ** -0.5),
        "w_decay": nrm(ks[7], (DEPTH, GLA_RANK, GLA_QK), GLA_RANK ** -0.5),
        "b_decay": nrm(ks[8], (DEPTH, GLA_QK), 0.1),
        "gla_norm": gain(ks[9], (DEPTH, GLA_DV)),
        "w_proj_a": nrm(ks[10], (DEPTH, GLA_V, D_MODEL), GLA_V ** -0.5),
        "lambda_q1": nrm(ks[11], (DEPTH, DIFF_DH), 0.1),
        "lambda_k1": nrm(ks[12], (DEPTH, DIFF_DH), 0.1),
        "lambda_q2": nrm(ks[13], (DEPTH, DIFF_DH), 0.1),
        "lambda_k2": nrm(ks[14], (DEPTH, DIFF_DH), 0.1),
        "diff_norm": gain(ks[15], (DEPTH, DIFF_DV)),
        "w_proj_b": nrm(ks[16], (DEPTH, DIFF_V, D_MODEL), DIFF_V ** -0.5),
        "w_out": nrm(ks[17], (DEPTH, D_MODEL, D_MODEL), D_MODEL ** -0.5),
        "norm_ffn": gain(ks[18], (DEPTH, D_MODEL)),
        "w_router_group": nrm(ks[19], (DEPTH, D_MODEL, N_GROUPS), D_MODEL ** -0.5),
        "b_router_group": nrm(ks[20], (DEPTH, N_GROUPS), 0.01),
        "w_router_expert": nrm(ks[21], (DEPTH, D_MODEL, N_EXPERTS), D_MODEL ** -0.5),
        "b_router_expert": nrm(ks[22], (DEPTH, N_EXPERTS), 0.01),
        "w_gate": nrm(ks[23], (DEPTH, N_EXPERTS, D_MODEL, D_EXPERT), D_MODEL ** -0.5),
        "w_up": nrm(ks[24], (DEPTH, N_EXPERTS, D_MODEL, D_EXPERT), D_MODEL ** -0.5),
        "w_down": nrm(ks[25], (DEPTH, N_EXPERTS, D_EXPERT, D_MODEL), D_EXPERT ** -0.5),
        "norm_final": gain(ks[26], (D_MODEL,)),
    }

def reference(x_prompt, x_sample, cache_k, cache_v, state_gla, norm_mix, w_in, w_decay, b_decay,
              gla_norm, w_proj_a, lambda_q1, lambda_k1, lambda_q2, lambda_k2, diff_norm, w_proj_b,
              w_out, norm_ffn, w_router_group, b_router_group, w_router_expert, b_router_expert,
              w_gate, w_up, w_down, norm_final):
    yp, ys = x_prompt, x_sample
    kp_l, vp_l, sp_l, ks_l, vs_l, ss_l = [], [], [], [], [], []
    for l in range(DEPTH):
        p = dict(norm_mix=norm_mix[l], w_in=w_in[l], w_decay=w_decay[l], b_decay=b_decay[l],
                 gla_norm=gla_norm[l], w_proj_a=w_proj_a[l], lambda_q1=lambda_q1[l],
                 lambda_k1=lambda_k1[l], lambda_q2=lambda_q2[l], lambda_k2=lambda_k2[l],
                 diff_norm=diff_norm[l], w_proj_b=w_proj_b[l], w_out=w_out[l], norm_ffn=norm_ffn[l],
                 w_router_group=w_router_group[l], b_router_group=b_router_group[l],
                 w_router_expert=w_router_expert[l], b_router_expert=b_router_expert[l],
                 w_gate=w_gate[l], w_up=w_up[l], w_down=w_down[l])
        lam_init = 0.8 - 0.6 * math.exp(-0.3 * l)
        s0 = jnp.zeros((yp.shape[0], GLA_HEADS, GLA_DK, GLA_DV), jnp.float32)
        yp, sp, kp, vp = trunk_layer(yp, p, s0, None, None, lam_init)
        ys, ss, kss, vss = trunk_layer(ys, p, state_gla[l], cache_k[l], cache_v[l], lam_init)
        kp_l.append(kp)
        vp_l.append(vp)
        sp_l.append(sp.astype(x_prompt.dtype))
        ks_l.append(kss)
        vs_l.append(vss)
        ss_l.append(ss.astype(state_gla.dtype))
    y_prompt = rms_norm(yp, norm_final)
    y_sample = rms_norm(ys, norm_final)
    return (y_prompt, y_sample, jnp.stack(kp_l), jnp.stack(vp_l), jnp.stack(sp_l),
            jnp.stack(ks_l), jnp.stack(vs_l), jnp.stack(ss_l))


_drawn_inputs = setup_inputs


def setup_inputs(seed=0):
    import zlib

    import numpy as np

    out = dict(_drawn_inputs(seed))
    spreads = {}
    factors = {'diff_norm': 12.152,
     'b_router_expert': 14.607,
     'norm_final': 7.759,
     'gla_norm': 8.0,
     'norm_ffn': 3.136,
     'b_router_group': 6.771}
    for name, (base, spread) in spreads.items():
        noise = np.random.default_rng([zlib.crc32(name.encode()), seed]).standard_normal(out[name].shape)
        drawn = base * np.exp(spread * noise) if base else spread * noise
        out[name] = __import__('jax').numpy.asarray(drawn.astype(out[name].dtype))
    for name, factor in factors.items():
        out[name] = (out[name] * factor).astype(out[name].dtype)
    return out
```

```python
from contextlib import ExitStack

import concourse.bass as bass
from concourse import mybir

ALU = mybir.AluOpType
ACT = mybir.ActivationFunctionType
F32 = mybir.dt.float32
F16 = mybir.dt.float16
I32 = mybir.dt.int32
AX_X = mybir.AxisListType.X

P = 128
D = 1024
KC = D // P
TP = 512
TS = 32
NT = TP + TS
TILES = [(i * P, P) for i in range(TP // P)] + [(TP, TS)]
NTILE = len(TILES)
HALF = NT // 2
PAST = 1024
EPS = 1e-6
CHUNK = 64
GH, DK, DV = 4, 128, 256
RANK = 16
TAU = 16.0
NCH = TP // CHUNK + 1
DH, DVB = 8, 128
DQ = 64
LAM_INIT = 0.2
NG, EG = 4, 4
NE = NG * EG
FE = 512
CAP = 128
MORE = (NT - 1) // CAP
NOVF = 2 * NT // CAP
NBLK = NE + NOVF
BIG = 1e30
WC = 512
RING = 3

C_QA, C_KA, C_VA, C_RA, C_CODE = 0, 512, 1024, 2048, 3072
C_QB, C_KB, C_VB, C_GA, C_GB = 3088, 4112, 5136, 6160, 7184


def layout_of_units():
    tiles = [("w_in", C_QA), ("w_in", C_KA), ("w_in", C_VA), ("w_in", C_VA + WC), ("w_in", C_RA), ("w_in", C_RA + WC),
             ("w_in", C_GA), ("w_in", C_GA + WC), ("w_proj_a", 0), ("w_proj_a", WC)]
    tiles += [("w_in", c + n * WC) for c in (C_QB, C_KB, C_VB) for n in range(2)]
    tiles += [("w_in", C_GB), ("w_proj_b", 0), ("w_in", C_GB + WC), ("w_proj_b", WC), ("w_out", 0), ("w_out", WC)]
    kinds = ["qa", "ka", "va", "va", "ra", "ra", "ga", "ga", "pa", "pa", "qb", "qb", "kb", "kb", "vb", "vb",
             "gb", "pb", "gb", "pb", "wo", "wo"]
    nth = [0, 0, 0, 1, 0, 1, 0, 1, 0, 1, 0, 1, 0, 1, 0, 1, 0, 0, 1, 1, 0, 1]
    units, emptied = [], {"A": 0, "D": 0}
    for n, kind in enumerate(kinds):
        token_major = kind in ("va", "ra", "vb", "wo")
        parts = [(i, 0) for i in range(NTILE)] if token_major else [(f, h) for f in range(4) for h in range(2)]
        for m, (a, b) in enumerate(parts):
            if kind in ("ra", "ga", "gb"):
                eng = "A"
            elif kind in ("pa", "pb", "wo"):
                eng = "D"
            else:
                eng = "AD"[len(units) % 2]
            emptied[eng] += 1
            units.append(dict(tile=n, kind=kind, nth=nth[n], a=a, b=b, first=m == 0, last=m == len(parts) - 1,
                              eng=eng, count=emptied[eng], token_major=token_major))
    return tiles, kinds, units


def build(nc, x_prompt, x_sample, cache_k, cache_v, state_gla, norm_mix, w_in, w_decay, b_decay, gla_norm, w_proj_a,
          lambda_q1, lambda_k1, lambda_q2, lambda_k2, diff_norm, w_proj_b, w_out, norm_ffn, w_router_group,
          b_router_group, w_router_expert, b_router_expert, w_gate, w_up, w_down, norm_final,
          y_prompt, y_sample, new_k_p, new_v_p, new_s_p, new_k_s, new_v_s, new_s_s):
    wtiles, wkinds, units = layout_of_units()
    bank_of = [u % 3 for u in range(len(units))]
    stage_units = {}
    for u, d in enumerate(units):
        stage_units.setdefault(d["tile"], []).append(u)
    tiles_of = {k: [n for n, kk in enumerate(wkinds) if kk == k] for k in set(wkinds)}

    h2_rows = nc.dram_tensor("h2_rows", (NT, D), F32)
    y_rows = nc.dram_tensor("y_rows", (NBLK * CAP, D), F32)
    h2_rows, y_rows = h2_rows.ap(), y_rows.ap()

    ctx = ExitStack()
    with ctx:
        def sem(name):
            return ctx.enter_context(nc.semaphore(name))

        def sb(name, shape, dt=F32, stack=ctx):
            return stack.enter_context(nc.sbuf_tensor(name, shape, dt))

        ps = ctx.enter_context(nc.psum_tensor("ps", [P, 8, 512], F32))

        ident = sb("ident", [P, P])
        trimask = sb("trimask", [P, CHUNK], I32)
        trif = sb("trif", [P, CHUNK])
        eps = sb("eps", [P, 1])
        ones = sb("ones", [P, P])
        small = sb("small", [P, 64])
        g_mix, g_gla, g_diff, b_dec = small[:, 0:8], small[:, 8:16], small[:, 16:17], small[:, 17:21]
        g_diff_s = small[:, 21:22]
        lamt = sb("lamt", [P, 4, DQ])
        lam = sb("lam", [P, 8])
        stat = sb("stat", [P, 64])
        wr = sb("wr", [P, KC, NG + NE])
        br = sb("br", [P, NG + NE])
        w_code = sb("w_code", [P, KC, RANK])
        w_dec = sb("w_dec", [RANK, GH * DK])

        dense = ExitStack()
        ring = sb("ring", [P, RING, KC * WC], stack=dense)
        hT = sb("hT", [P, KC, NT], stack=dense)
        mixT = sb("mixT", [P, KC, NT], stack=dense)

        gla = ExitStack()
        fmA = sb("fmA", [P, 8, NT], stack=gla)
        code = sb("code", [RANK, NT], stack=gla)
        va = sb("va", [P, NTILE, GH * DV], stack=gla)
        ra = sb("ra", [P, NTILE, GH * DV], stack=gla)
        kend = sb("kend", [P, NTILE, GH, DK], stack=gla)
        S = sb("S", [P, 2, GH, DV], stack=gla)
        att = sb("att", [P, GH, CHUNK], stack=gla)
        ebl = sb("ebl", [P, GH, NCH], stack=gla)
        xa = ExitStack()
        x0 = sb("x0", [P, NTILE, D], stack=xa)
        sq0 = sb("sq0", [P, D], stack=xa)
        xa.close()
        bT = sb("bT", [P, GH, NT], stack=gla)
        t1 = sb("t1", [P, GH, NT], stack=gla)
        t2 = sb("t2", [P, GH, NT], stack=gla)
        t3 = sb("t3", [P, GH, NT], stack=gla)
        keep = sb("keep", [P, NT], stack=gla)
        sqa = sb("sqa", [P, DV], stack=gla)
        S_in = sb("S_in", [P, GH, DV], stack=gla)
        gla.close()

        dif = ExitStack()
        qbT = sb("qbT", [P, DH, NT], stack=dif)
        kbT = sb("kbT", [P, DH, NT], stack=dif)
        vb = sb("vb", [P, NTILE, DH * DVB], stack=dif)
        kb_rows = sb("kb_rows", [P, 2, D], stack=dif)
        dist = sb("dist", [P, TP], stack=dif)
        dist_s = sb("dist_s", [P, PAST + TS], stack=dif)
        bias = sb("bias", [P, 2, TP + TS // 2], stack=dif)
        slope = sb("slope", [P, 2], stack=dif)
        kraw = sb("kraw", [P, 2, PAST // P, P], stack=dif)
        kcT = sb("kcT", [P, 2, PAST], stack=dif)
        vc = sb("vc", [P, 4, PAST // P, P], stack=dif)
        sc = sb("sc", [P, 2, 2, TP + 16], stack=dif)
        pT = sb("pT", [P, 2, TP], stack=dif)
        att_st = sb("att_st", [P, 2, 8], stack=dif)
        ob = sb("ob", [P, TP], stack=dif)
        dif.close()

        merge = ExitStack()
        sb("qbT_kept", [P, DH, NT], stack=merge)
        obT = qbT
        sgb = sb("sgb", [P, 4, NT], stack=merge)
        tmpm = sb("tmpm", [P, 2, HALF], stack=merge)
        h2 = sb("h2", [P, 2, D], stack=merge)
        h2T = sb("h2T", [P, KC, P], stack=merge)
        sq2 = sb("sq2", [P, D], stack=merge)
        merge.close()
        dense.close()

        ex = ExitStack()
        wg = sb("wg", [P, 2, KC, FE], stack=ex)
        wu = sb("wu", [P, 2, KC, FE], stack=ex)
        wd = sb("wd", [P, 2, FE // P, D], stack=ex)
        xg = sb("xg", [P, 2, D], stack=ex)
        xgT = sb("xgT", [P, 2, KC, P], stack=ex)
        sg = sb("sg", [P, FE], stack=ex)
        hh = sb("hh", [P, 2, FE], stack=ex)
        hhT = sb("hhT", [P, FE // P, P], stack=ex)
        yo = sb("yo", [P, 2, D], stack=ex)
        x2 = sb("x2", [P, NTILE, D], stack=ex)
        gffn = sb("gffn", [P, D], stack=ex)
        gfin = sb("gfin", [P, D], stack=ex)
        lg = sb("lg", [P, NTILE, NG + NE], stack=ex)
        rt = sb("rt", [P, 12, NTILE * NE], stack=ex)
        rs = sb("rs", [P, 16, NTILE], stack=ex)
        iota_e = sb("iota_e", [P, NE], stack=ex)
        ov = sb("ov", [P, 8, NE], stack=ex)
        iota_s = sb("iota_s", [P, CAP], stack=ex)
        tok_id = sb("tok_id", [P, NTILE], F16, stack=ex)
        upper = sb("upper", [P, P], stack=ex)
        rsel = sb("rsel", [P, NTILE, NBLK], stack=ex)
        slot_i = sb("slot_i", [P, NBLK], I32, stack=ex)
        ysl = sb("ysl", [P, 2, NTILE], I32, stack=ex)
        ovb = sb("ovb", [P, NOVF, 2], stack=ex)
        ovi = sb("ovi", [P, 2 * NOVF + 2], I32, stack=ex)
        ovm = sb("ovm", [P, NOVF, 3, NE], stack=ex)
        onehot = sb("onehot", [P, 2, NBLK, CAP], F16, stack=ex)

        ex.close()
        fin = ExitStack()
        yg = sb("yg", [P, 2, 2, D], stack=fin)
        fo = sb("fo", [P, 2, D], stack=fin)
        sqf = sb("sqf", [P, D], stack=fin)
        fin.close()
        def rep(ap, axis, n):
            a = ap.unsqueeze(axis)
            shape = list(a.shape)
            shape[axis] = n
            return a.broadcast_to(shape)

        def after(eng, s, value):
            if not (isinstance(value, int) and value <= 0):
                eng.wait_ge(s, value)

        bias_s = bias[:].rearrange("p a n -> p (a n)")
        scs = sc[:].rearrange("p k a n -> p k (a n)")
        pTs_v = kb_rows[:].rearrange("p a n -> p (a n)")[:, 0:(PAST // P + 1) * P].rearrange("p (c q) -> p c q", q=P)

        def u_of(kind, nth, a, b):
            return next(u for u, d in enumerate(units) if (d["kind"], d["nth"], d["a"], d["b"]) == (kind, nth, a, b))

        s_x = [sem(f"s_x{i}") for i in range(NTILE)]
        s_small = sem("s_small")
        s_wcode = sem("s_wcode")
        s_const = sem("s_const")
        s_pool = sem("s_pool")
        s_dve = sem("s_dve")
        s_act = sem("s_act")
        s_lamp, s_lame = sem("s_lamp"), sem("s_lame")
        s_xsq, s_xrs = sem("s_xsq"), sem("s_xrs")
        s_h = sem("s_h")
        s_hx = sem("s_hx")
        s_hT = sem("s_hT")
        s_w = [sem(f"s_w{i}") for i in range(RING)]
        s_unit = sem("s_unit")
        s_ev = {"A": sem("s_evA"), "D": sem("s_evD")}
        s_code_mm, s_code = sem("s_code_mm"), sem("s_code")
        s_dec_mm, s_dec_rd = sem("s_dec_mm"), sem("s_dec_rd")
        s_abs, s_ln, s_delta, s_exps = sem("s_abs"), sem("s_ln"), sem("s_delta"), sem("s_exps")
        s_qk = sem("s_qk")
        s_ke_mm, s_ke = sem("s_ke_mm"), sem("s_ke")
        s_sin = sem("s_sin")
        s_att_mm, s_att = sem("s_att_mm"), sem("s_att")
        s_dS, s_S, s_o = sem("s_dS"), sem("s_S"), sem("s_o")
        s_osq, s_og = sem("s_osq"), sem("s_og")
        s_ox, s_oaT = sem("s_ox"), sem("s_oaT")
        s_Sst = sem("s_Sst")
        s_mz = sem("s_mz")
        s_dist = sem("s_dist")
        s_bs = sem("s_bs")
        s_bias = sem("s_bias")
        s_kx, s_krow, s_kst, s_vst = sem("s_kx"), sem("s_krow"), [sem("s_kst0"), sem("s_kst1")], sem("s_vst")
        s_scm, s_tt, s_exp = sem("s_scm"), sem("s_tt"), sem("s_exp")
        s_pr, s_px, s_pT, s_pvq = sem("s_pr"), sem("s_px"), sem("s_pT"), sem("s_pvq")
        s_sqr = sem("s_sqr")
        s_bsq, s_brs, s_bo, s_bx, s_obT = sem("s_bsq"), sem("s_brs"), sem("s_bo"), sem("s_bx"), sem("s_obT")
        s_kc = [sem("s_kc0"), sem("s_kc1")]
        s_vc = [sem(f"s_vc{i}") for i in range(4)]
        s_kcx, s_kcT = sem("s_kcx"), sem("s_kcT")
        s_ssc, s_stt, s_sexp, s_spr = sem("s_ssc"), sem("s_stt"), sem("s_sexp"), sem("s_spr")
        s_spx, s_spT, s_hpv = sem("s_spx"), sem("s_spT"), sem("s_hpv")
        s_x2 = [sem(f"s_x2_{i}") for i in range(NTILE)]
        s_g = sem("s_g")
        s_c2 = sem("s_c2")
        s_2sq, s_2rs, s_h2, s_h2st = sem("s_2sq"), sem("s_2rs"), sem("s_h2"), [sem("s_h2st0"), sem("s_h2st1")]
        s_h2x, s_h2T, s_lgm, s_lg = sem("s_h2x"), sem("s_h2T"), sem("s_lgm"), sem("s_lg")
        s_gd, s_ge, s_ed, s_ee = sem("s_gd"), sem("s_ge"), sem("s_ed"), sem("s_ee")
        s_A, s_rank, s_oh, s_ohu, s_tok, s_slot = (sem(n) for n in ("s_A", "s_rank", "s_oh", "s_ohu", "s_tok", "s_slot"))
        s_wg, s_wu, s_wd = ([sem(f"s_{n}{i}") for i in range(2)] for n in ("wg", "wu", "wd"))
        s_xg = [sem("s_xg0"), sem("s_xg1")]
        s_xt, s_xtA, s_xtD, s_gu, s_sg, s_hh, s_at, s_hhT, s_dn, s_yA, s_yD = (
            sem(n) for n in ("s_xt", "s_xtA", "s_xtD", "s_gu", "s_sg", "s_hh", "s_at", "s_hhT", "s_dn", "s_yA", "s_yD"))
        s_yst = [sem("s_yst0"), sem("s_yst1")]
        s_zero = sem("s_zero")
        s_exdone = sem("s_exdone")
        s_yg = [sem("s_yg0"), sem("s_yg1")]
        s_f, s_fsq, s_frs, s_fo, s_out = sem("s_f"), sem("s_fsq"), sem("s_frs"), sem("s_fo"), [sem("s_out0"), sem("s_out1")]

        hooks = {}

        def hook(u, *what):
            hooks.setdefault(u, []).append(what)

        hook(stage_units[1][-1], "code")
        va_units = stage_units[2] + stage_units[3]
        for f in range(GH + 2):
            hook(va_units[min(2 * f, len(va_units) - 1)], "dec", f)
        for i in range(NTILE):
            hook(stage_units[5][i], "kend", i)
        ga_units = stage_units[6] + stage_units[7]
        for i in range(NTILE):
            hook(ga_units[3 * i + 2], "gla", i)
        vb_units = stage_units[14] + stage_units[15]
        for i in range(NTILE):
            hook(vb_units[2 * i + 1], "kout", i)
        hook(vb_units[-1], "attn")
        for i in range(NTILE):
            hook(stage_units[21][i], "h2", i)
            hook(stage_units[21][min(i + 1, NTILE - 1)], "router", i)
        first_qb, first_gb, last_unit = stage_units[10][0], stage_units[16][0], len(units) - 1
        last_pa = stage_units[9][-1]

        def emptied(eng, u):
            eng.wait_ge(s_ev[units[u]["eng"]], units[u]["count"])

        block = ctx.enter_context(nc.Block())

        @block.sync
        def _(sp):
            dram = {"w_in": w_in, "w_proj_a": w_proj_a, "w_proj_b": w_proj_b, "w_out": w_out}
            for n, (name, col) in enumerate(wtiles):
                if n >= RING:
                    sp.wait_ge(s_unit, stage_units[n - RING][-1] + 1)
                src = dram[name][0, :, col:col + WC].rearrange("(c p) n -> p c n", p=P)
                sp.dma_start(ring[:, n % RING, :].rearrange("p (c n) -> p c n", c=KC), src).then_inc(s_w[n % RING], 16)
            sp.wait_ge(s_unit, last_unit + 1)

            def load_expert(e, slot):
                e1 = bass.ds(e, 1)
                sp.dma_start(wg[:, slot], w_gate[0, e1].rearrange("a (c p) n -> p (a c) n", p=P)).then_inc(s_wg[slot], 16)
                sp.dma_start(wu[:, slot], w_up[0, e1].rearrange("a (c p) n -> p (a c) n", p=P)).then_inc(s_wu[slot], 16)
                return w_down[0, e1].rearrange("a (c p) n -> p (a c) n", p=P)

            for e in range(2):
                src = load_expert(e, e)
                sp.dma_start(wd[:, e], src).then_inc(s_wd[e], 16)
            with sp.Fori(0, NE // 2 - 1) as it:
                for k in range(2):
                    sp.wait_ge(s_gu, it * 2 + (k + 1))
                    src = load_expert(it * 2 + (k + 2), k)
                    sp.wait_ge(s_dn, it * 2 + (k + 1))
                    sp.dma_start(wd[:, k], src).then_inc(s_wd[k], 16)
            sp.wait_ge(s_slot, 1)
            n_ovf = sp.value_load(ovi[0:1, 0:1], min_val=0, max_val=NOVF)
            for i in range(NOVF):
                e = sp.value_load(ovi[0:1, 1 + i:2 + i], min_val=0, max_val=NE - 1)
                with sp.If(n_ovf > i):
                    sp.wait_ge(s_gu, NE + i)
                    sp.wait_ge(s_dn, NE + i)
                    src = load_expert(e, 0)
                    sp.dma_start(wd[:, 0], src).then_inc(s_wd[0], 16)
            for i, (t0, n) in enumerate(TILES):
                sp.wait_ge(s_fo, i + 1)
                dst = y_prompt[0, t0:t0 + n] if i < NTILE - 1 else y_sample[0]
                sp.dma_start(dst, fo[0:n, i % 2]).then_inc(s_out[i % 2], 16)
            sp.wait_ge(s_out[0], 48)
            sp.wait_ge(s_out[1], 32)
            for i in range(2):
                sp.wait_ge(s_kst[i], 16 * ((NTILE + 1 - i) // 2))
                sp.wait_ge(s_h2st[i], 16 * ((NTILE + 1 - i) // 2))
            sp.wait_ge(s_vst, 32)
            sp.wait_ge(s_Sst, 32)

        @block.gpsimd
        def _(pool):
            steps = [0]

            def step(ins):
                steps[0] += 1
                ins.then_inc(s_pool, 1)
                pool.wait_ge(s_pool, steps[0])

            step(pool.memset(ident[:], 0.0))
            step(pool.affine_select(out=ident[:], in_=ident[:], compare_op=ALU.not_equal, fill=1.0, base=0,
                                    pattern=[[-1, P]], channel_multiplier=1))
            step(pool.memset(ones[:], 1.0))
            step(pool.memset(eps[:], EPS))
            pool.wait_ge(s_mz, 1)
            for i in range(NOVF):
                pool.dma_start(y_rows[CAP * (NE + i):CAP * (NE + i + 1)].rearrange("p (a n) -> p a n", n=256),
                               rep(att[:].rearrange("p h t -> p (h t)"), 1, D // 256)).then_inc(s_zero, 16)
            step(pool.memset(trif[:], 1.0))
            for a in range(2):
                t = trif[64 * a:64 * a + 64, :]
                step(pool.affine_select(out=t, in_=t, compare_op=ALU.is_ge, fill=0.0, base=0,
                                        pattern=[[1, CHUNK]], channel_multiplier=-1))
            pool.tensor_copy(trimask[:], trif[:]).then_inc(s_const, 1)
            pool.wait_ge(s_hT, NTILE)
            step(pool.memset(keep[:], 1.0))
            step(pool.memset(keep[:, 0:TP].rearrange("p (c t) -> p c t", t=CHUNK)[:, :, 0:1], 0.0))
            pool.memset(keep[:, TP:TP + 1], 0.0).then_inc(s_const, 1)
            pool.dma_start(S_in[:], state_gla[0, 0].rearrange("h k v -> k h v")).then_inc(s_sin, 16)
            pool.wait_ge(s_S, NCH - 1)
            pool.dma_start(new_s_p[0, 0].rearrange("h k v -> k h v"), S[:, 0]).then_inc(s_Sst, 16)
            pool.wait_ge(s_S, NCH)
            pool.dma_start(new_s_s[0, 0].rearrange("h k v -> k h v"), S[:, 1]).then_inc(s_Sst, 16)
            pool.wait_ge(s_unit, last_pa + 1)
            emptied(pool, last_pa)
            pool.wait_ge(s_Sst, 32)
            step(pool.iota(dist[:], pattern=[[-1, TP]], base=TP - P, channel_multiplier=1,
                           allow_small_or_imprecise_dtypes=True))
            for j in range(4):
                step(pool.iota(dist_s[32 * j:32 * j + 32], pattern=[[-1, PAST + TS]], base=PAST,
                               channel_multiplier=1, allow_small_or_imprecise_dtypes=True))
                for g in range(2):
                    step(pool.memset(slope[32 * j:32 * j + 32, g:g + 1], 2.0 ** -(4 * g + j + 1)))
            pool.memset(att_st[:], 0.0).then_inc(s_dist, 1)

            def load_cache(h):
                pool.dma_start(kraw[:, h % 2], cache_k[0, 0, :, h, :].rearrange("(c p) d -> p c d", p=P)).then_inc(s_kc[h % 2], 16)
                pool.dma_start(vc[:, h % 4], cache_v[0, 0, :, h, :].rearrange("(c p) d -> p c d", p=P)).then_inc(s_vc[h % 4], 16)

            for h in range(2):
                load_cache(h)
            for i, (t0, n) in enumerate(TILES):
                pool.wait_ge(s_krow, 2 * (i + 1))
                dst = new_k_p[0, 0, t0:t0 + n] if i < NTILE - 1 else new_k_s[0, 0]
                pool.dma_start(dst.rearrange("t h d -> t (h d)"), kb_rows[0:n, i % 2]).then_inc(s_kst[i % 2], 16)
            emptied(pool, vb_units[-1])
            emptied(pool, vb_units[-2])
            pool.dma_start(new_v_p[0, 0].rearrange("(i p) h d -> p i (h d)", p=P), vb[:, 0:4]).then_inc(s_vst, 16)
            pool.dma_start(new_v_s[0, 0].rearrange("t h d -> t (h d)"), vb[0:TS, 4]).then_inc(s_vst, 16)
            pool.wait_ge(s_bs, 1)
            for h in range(DH):
                if h >= 2:
                    pool.wait_ge(s_tt, 8 * (h - 1))
                pool.tensor_scalar(bias[:, h % 2, 0:TP], dist[:], 2.0 ** -(h + 1), None, ALU.mult).then_inc(s_bias, 1)
            for h in range(2, DH):
                pool.wait_ge(s_kcx, 2 * (h - 1))
                pool.dma_start(kraw[:, h % 2], cache_k[0, 0, :, h, :].rearrange("(c p) d -> p c d", p=P)).then_inc(s_kc[h % 2], 16)
                if h >= 4:
                    pool.wait_ge(s_hpv, h - 3)
                pool.dma_start(vc[:, h % 4], cache_v[0, 0, :, h, :].rearrange("(c p) d -> p c d", p=P)).then_inc(s_vc[h % 4], 16)
            pool.wait_ge(s_unit, first_gb + 1)
            pool.wait_ge(s_obT, DH + 2)
            for i in range(2):
                pool.wait_ge(s_kst[i], 16 * ((NTILE + 1 - i) // 2))
            pool.wait_ge(s_vst, 32)
            for i, (t0, n) in enumerate(TILES):
                src = x_prompt[0, t0:t0 + n] if i < NTILE - 1 else x_sample[0]
                pool.dma_start(x2[0:n, i], src).then_inc(s_x2[i], 16)
            pool.dma_start(gffn[:], norm_ffn.broadcast_to([P, D])).then_inc(s_g, 16)
            pool.dma_start(gfin[:], norm_final.unsqueeze(0).broadcast_to([P, D])).then_inc(s_g, 16)
            step(pool.iota(iota_e[:], pattern=[[1, NE]], base=0, channel_multiplier=0, allow_small_or_imprecise_dtypes=True))
            step(pool.iota(iota_s[:], pattern=[[1, CAP]], base=0, channel_multiplier=0, allow_small_or_imprecise_dtypes=True))
            step(pool.iota(tok_id[:], pattern=[[P, NTILE]], base=0, channel_multiplier=1, allow_small_or_imprecise_dtypes=True))
            step(pool.memset(upper[:], 1.0))
            step(pool.affine_select(out=upper[:], in_=upper[:], compare_op=ALU.is_gt, fill=0.0, base=0,
                                    pattern=[[1, P]], channel_multiplier=-1))
            pool.memset(lg[:], 0.0).then_inc(s_c2, 1)

            def rows_in(i):
                n = TILES[i][1]
                pool.wait_ge(s_h2, i + 1)
                pool.dma_start(h2_rows[TILES[i][0]:TILES[i][0] + n], h2[0:n, i % 2]).then_inc(s_h2st[i % 2], 16)

            for i in range(NTILE):
                rows_in(i)
            pool.wait_ge(s_h2st[0], 48)
            pool.wait_ge(s_h2st[1], 32)
            pool.wait_ge(s_slot, 1)

            def gather(j, slot):
                pool.indirect_dma_start(xg[:, slot], None, h2_rows,
                                        bass.IndirectOffsetOnAxis(slot_i[:, j:j + 1], 0)).then_inc(s_xg[slot], 16)

            for e in range(NE):
                if e >= 2:
                    pool.wait_ge(s_xt, e - 1)
                gather(e, e % 2)
            n_ovf = pool.value_load(ovi[0:1, 0:1], min_val=0, max_val=NOVF)
            for i in range(NOVF):
                with pool.If(n_ovf > i):
                    pool.wait_ge(s_xt, NE + i)
                    gather(NE + i, 0)
            pool.wait_ge(s_yst[0], 16 * NE // 2)
            pool.wait_ge(s_yst[1], 16 * NE // 2)
            pool.wait_ge(s_exdone, 1)
            for i, (t0, n) in enumerate(TILES):
                if i >= 2:
                    pool.wait_ge(s_f, 2 * (i - 1))
                for k in range(2):
                    pool.indirect_dma_start(yg[0:n, i % 2, k], None, y_rows,
                                            bass.IndirectOffsetOnAxis(ysl[0:n, k, i:i + 1], 0)).then_inc(s_yg[i % 2], 16)

        @block.scalar
        def _(act):
            steps = [0]

            def step(ins):
                steps[0] += 1
                ins.then_inc(s_act, 1)
                act.wait_ge(s_act, steps[0])

            for i, (t0, n) in enumerate(TILES):
                src = x_prompt[0, t0:t0 + n] if i < NTILE - 1 else x_sample[0]
                act.dma_start(x0[0:n, i], src).then_inc(s_x[i], 16)
            with nc.allow_non_contiguous_dma("a few parameter columns"):
                act.dma_start(g_mix, norm_mix[0].rearrange("(c p) -> p c", p=P)).then_inc(s_small, 16)
                for h in range(GH):
                    act.dma_start(g_gla[:, 2 * h:2 * h + 2], gla_norm[0].rearrange("(c p) -> p c", p=P)).then_inc(s_small, 16)
                act.dma_start(g_diff, diff_norm[0].rearrange("(c p) -> p c", p=P)).then_inc(s_small, 16)
                act.dma_start(b_dec, b_decay[0].rearrange("(c p) -> p c", p=P)).then_inc(s_small, 16)
                for k, l in enumerate((lambda_q1, lambda_k1, lambda_q2, lambda_k2)):
                    act.dma_start(lamt[:, k], l.broadcast_to([P, DQ])).then_inc(s_small, 16)
                act.dma_start(w_code[:], w_in[0, :, C_CODE:C_CODE + RANK].rearrange("(c p) n -> p c n", p=P)).then_inc(s_wcode, 16)
                act.dma_start(w_dec[:], w_decay[0]).then_inc(s_wcode, 16)
                act.dma_start(wr[:, :, 0:NG], w_router_group[0].rearrange("(c p) n -> p c n", p=P)).then_inc(s_wcode, 16)
                act.dma_start(wr[:, :, NG:NG + NE], w_router_expert[0].rearrange("(c p) n -> p c n", p=P)).then_inc(s_wcode, 16)
                act.dma_start(br[:, 0:NG], b_router_group.broadcast_to([P, NG])).then_inc(s_wcode, 16)
                act.dma_start(br[:, NG:NG + NE], b_router_expert.broadcast_to([P, NE])).then_inc(s_wcode, 16)
            act.wait_ge(s_const, 1)
            for i, (t0, n) in enumerate(TILES):
                act.wait_ge(s_x[i], 16)
                step(act.activation(sq0[0:n], x0[0:n, i], ACT.Square, accum_out=stat[0:n, i:i + 1]))
                act.activation(stat[0:n, 8 + i:9 + i], stat[0:n, i:i + 1], ACT.Sqrt, bias=eps[0:n], scale=1.0 / D).then_inc(s_xsq, 1)
            act.wait_ge(s_lamp, 1)
            act.activation(lam[:, 2:4], lam[:, 0:2], ACT.Exp).then_inc(s_lame, 1)

            def do(what, i=0):
                if what == "code":
                    act.wait_ge(s_code_mm, 1)
                    act.activation(code[:].rearrange("r (b t) -> r b t", b=2), ps[0:RANK, 4:6, 0:HALF], ACT.Copy).then_inc(s_code, 1)
                elif what == "dec":
                    if i < GH:
                        act.wait_ge(s_dec_mm, i + 1)
                        act.activation(t1[:, i].rearrange("p (b t) -> p b t", b=2), ps[:, 4 + 2 * (i % 2):6 + 2 * (i % 2), 0:HALF],
                                       ACT.Abs, bias=b_dec[:, i:i + 1]).then_inc(s_abs, 1)
                        act.wait_ge(s_abs, i + 1)
                        step(act.activation(t1[:, i], t1[:, i], ACT.Exp, scale=-1.0))
                        act.activation(t1[:, i], t1[:, i], ACT.Ln, bias=ones[:, 0:1]).then_inc(s_ln, 1)
                    if 1 <= i <= GH:
                        f = i - 1
                        act.wait_ge(s_delta, f + 1)
                        act.activation(t2[:, f], t2[:, f], ACT.Exp, scale=1.0 / TAU)
                        act.activation(t1[:, f], bT[:, f], ACT.Exp, scale=1.0 / TAU)
                        act.activation(t3[:, f], bT[:, f], ACT.Exp, scale=-1.0 / TAU)
                        act.activation(ebl[:, f, 0:8], bT[:, f, 0:TP].rearrange("p (c t) -> p c t", t=CHUNK)[:, :, CHUNK - 1],
                                       ACT.Exp, scale=1.0 / TAU)
                        act.activation(ebl[:, f, 8:9], bT[:, f, NT - 1:NT], ACT.Exp, scale=1.0 / TAU).then_inc(s_exps, 1)
                elif what == "kend":
                    n = TILES[i][1]
                    act.wait_ge(s_ke_mm, i + 1)
                    act.activation(kend[0:n, i].rearrange("p h d -> p (h d)"), ps[0:n, 4 + i % 4], ACT.Copy).then_inc(s_ke, 1)
                elif what == "gla":
                    n = TILES[i][1]
                    act.wait_ge(s_o, min(2 * i + 2, NCH))
                    for h in range(GH):
                        step(act.activation(sqa[0:n], ps[0:n, 5 + h // 2, DV * (h % 2):DV * (h % 2) + DV], ACT.Square,
                                            accum_out=stat[0:n, 16 + h:17 + h]))
                    if i:
                        act.wait_ge(s_og, i)
                    act.activation(stat[0:n, 20:24], stat[0:n, 16:20], ACT.Sqrt, bias=eps[0:n], scale=1.0 / DV).then_inc(s_osq, 1)
                elif what == "kout":
                    n, b = TILES[i][1], 3 + 2 * (i % 2)
                    act.wait_ge(s_kx, i + 1)
                    if i >= 2:
                        act.wait_ge(s_kst[i % 2], 16 * (i // 2))
                    for k in range(2):
                        act.activation(kb_rows[0:n, i % 2, 512 * k:512 * k + 512], ps[0:n, b + k], ACT.Copy).then_inc(s_krow, 1)
                elif what == "attn":
                    attention()
                elif what == "h2":
                    n = TILES[i][1]
                    emptied(act, stage_units[21][i])
                    step(act.activation(sq2[0:n], x2[0:n, i], ACT.Square, accum_out=stat[0:n, 40 + i:41 + i]))
                    act.activation(stat[0:n, 45 + i:46 + i], stat[0:n, 40 + i:41 + i], ACT.Sqrt, bias=eps[0:n], scale=1.0 / D).then_inc(s_2sq, 1)
                elif what == "router":
                    n = TILES[i][1]
                    act.wait_ge(s_h2x, i + 1)
                    if i:
                        act.wait_ge(s_lgm, i)
                    act.activation(h2T[:, :, 0:n], ps[:, 3:5].rearrange("p b (c t) -> p (b c) t", t=P)[:, :, 0:n], ACT.Copy).then_inc(s_h2T, 1)

            def attention():
                n_norm = [0]

                def head_norm(n, bank):
                    k = n_norm[0]
                    if k < DH:
                        act.wait_ge(s_pvq, 4 * (k + 1))
                    else:
                        act.wait_ge(s_hpv, 4 * (k - DH + 1))
                    if k:
                        act.wait_ge(s_bo, k)
                        act.wait_ge(s_bx, k)
                    act.activation(ob[0:n], ps[0:n, bank], ACT.Square).then_inc(s_sqr, 1)
                    act.wait_ge(s_brs, k + 1)
                    act.activation(stat[0:n, 28:32], stat[0:n, 24:28], ACT.Sqrt, bias=eps[0:n], scale=1.0 / DVB).then_inc(s_bsq, 1)
                    n_norm[0] += 1

                k = 0
                for h in range(DH):
                    for q in range(4):
                        w = P * (q + 1)
                        act.wait_ge(s_tt, 2 * k + 2)
                        act.activation(sc[:, k % 2, 0, 0:w], sc[:, k % 2, 0, 0:w], ACT.Exp, bias=att_st[:, k % 2, 0:1],
                                       scale=-1.0, accum_out=att_st[:, k % 2, 2:3])
                        act.activation(sc[:, k % 2, 1, 0:w], sc[:, k % 2, 1, 0:w], ACT.Exp, bias=att_st[:, k % 2, 1:2],
                                       scale=-1.0, accum_out=att_st[:, k % 2, 3:4]).then_inc(s_exp, 1)
                        if k >= 1:
                            probs_out(k - 1)
                        if q == 2 and h:
                            head_norm(P, 2 + 5 * ((h - 1) % 2))
                        k += 1
                probs_out(k - 1)
                head_norm(P, 7)
                for g in range(2):
                    for j in range(4):
                        h = 4 * g + j
                        for b in range(2):
                            act.wait_ge(s_kcx, 2 * h + b + 1)
                            if h >= 2:
                                act.wait_ge(s_ssc, h - 1)
                            act.activation(kcT[:, h % 2, 512 * b:512 * b + 512], ps[:, 6 + b], ACT.Copy).then_inc(s_kcT, 1)
                    act.wait_ge(s_stt, 2 * g + 2)
                    for b in range(2):
                        c = act.activation(scs[:, b], scs[:, b], ACT.Exp, bias=att_st[:, g, b:b + 1], scale=-1.0,
                                           accum_out=att_st[:, g, 2 + b:3 + b])
                    c.then_inc(s_sexp, 1)
                    if g == 0:
                        for b in range(2):
                            act.wait_ge(s_kst[b], 16 * ((NTILE + 1 - b) // 2))
                    for b in range(3):
                        nb = 4 if b < 2 else 1
                        rows = P if b < 2 else TS
                        act.wait_ge(s_spx, 3 * g + b + 1)
                        if b == 0 and g:
                            act.wait_ge(s_hpv, 4 * g)
                        act.activation(pTs_v[0:rows, 4 * b:4 * b + nb].rearrange("p c q -> p (c q)"),
                                       ps[0:rows, 6 + b % 2, 0:nb * P], ACT.Copy).then_inc(s_spT, 1)
                    head_norm(TS, 0)

            def probs_out(k):
                w = P * (k % 4 + 1)
                act.wait_ge(s_px, k + 1)
                if k >= 2:
                    act.wait_ge(s_pvq, k - 1)
                act.activation(pT[:, k % 2, 0:w], ps[:, k % 2, 0:w], ACT.Copy).then_inc(s_pT, 1)

            for u, d in enumerate(units):
                if d["eng"] == "A":
                    if u == first_qb or (u == first_qb + 1):
                        act.wait_ge(s_Sst, 32)
                    act.wait_ge(s_unit, u + 1)
                    kind, a, b, bank = d["kind"], d["a"], d["b"], bank_of[u]
                    if d["token_major"]:
                        t0, n = TILES[a]
                        dst = {"va": va, "ra": ra, "vb": vb}[kind][0:n, a, WC * d["nth"]:WC * d["nth"] + WC]
                        act.activation(dst, ps[0:n, bank], ACT.Silu if kind == "ra" else ACT.Copy).then_inc(s_ev["A"], 1)
                    else:
                        f = 4 * d["nth"] + a
                        cols = slice(HALF * b, HALF * b + HALF)
                        dst = {"qa": fmA[:, f, cols], "ka": fmA[:, GH + a, cols], "ga": mixT[:, f, cols], "qb": qbT[:, f, cols],
                               "kb": kbT[:, f, cols], "gb": sgb[:, a, cols]}[kind]
                        if kind == "gb" and d["nth"] == 1:
                            act.wait_ge(s_ev["D"], units[u_of("pb", 0, a, b)]["count"])
                        if kind in ("ga", "gb"):
                            act.activation(dst, ps[:, bank, 0:HALF], ACT.Sigmoid).then_inc(s_ev["A"], 1)
                        elif kind == "qb":
                            act.activation(dst, ps[:, bank, 0:HALF], ACT.Copy, scale=-DQ ** -0.5).then_inc(s_ev["A"], 1)
                        else:
                            act.activation(dst, ps[:, bank, 0:HALF], ACT.Copy).then_inc(s_ev["A"], 1)
                for what in hooks.get(u, []):
                    do(*what)
            act.wait_ge(s_gd, 1)
            act.activation(rt[:, 0, 0:NTILE * NG], rt[:, 0, 0:NTILE * NG], ACT.Exp).then_inc(s_ge, 1)
            act.wait_ge(s_ed, 1)
            act.activation(rs[:, 8], rs[:, 8], ACT.Exp).then_inc(s_ee, 1)

            def x_out(e, slot):
                act.wait_ge(s_xt, e + 1)
                act.activation(xgT[:, slot, 0:4].rearrange("p c t -> p (c t)"), ps[:, 4], ACT.Copy).then_inc(s_xtA, 1)

            def silu(e):
                act.wait_ge(s_gu, e + 1)
                act.activation(sg[:], ps[:, 0], ACT.Silu).then_inc(s_sg, 1)

            def h_out(e):
                act.wait_ge(s_at, e + 1)
                act.activation(hhT[:].rearrange("p c t -> p (c t)"), ps[:, 2], ACT.Copy).then_inc(s_hhT, 1)

            def y_out(e, slot):
                act.wait_ge(s_dn, e + 1)
                act.activation(yo[:, slot, 0:512], ps[:, 6], ACT.Copy).then_inc(s_yA, 1)
                act.wait_ge(s_yA, e + 1)
                act.wait_ge(s_yD, e + 1)

            act.wait_ge(s_slot, 1)
            x_out(0, 0)
            silu(0)
            x_out(1, 1)

            def y_of(e):
                return y_rows[bass.ds(e * CAP, CAP)]

            def body(e, odd, last=False):
                act.wait_ge(s_hh, e)
                silu(e)
                after(act, s_dn, e - 1)
                h_out(e - 1)
                if not last:
                    act.wait_ge(s_gu, e)
                    x_out(e + 1, 1 - odd)
                after(act, s_yst[1 - odd], store_count(e - 1, 1 - odd))
                y_out(e - 1, 1 - odd)
                act.dma_start(y_of(e - 1), yo[:, 1 - odd]).then_inc(s_yst[1 - odd], 16)

            def store_count(e, slot):
                return (e - slot) * 8

            body(1, 1)
            body(2, 0)
            with act.Fori(1, NE // 2 - 1) as it:
                body(it * 2 + 1, 1)
                body(it * 2 + 2, 0)
            body(NE - 1, 1, last=True)
            act.wait_ge(s_dn, NE - 1)
            h_out(NE - 1)
            act.wait_ge(s_yst[1], store_count(NE - 1, 1))
            y_out(NE - 1, 1)
            act.dma_start(y_of(NE - 1), yo[:, 1]).then_inc(s_yst[1], 16)
            act.wait_ge(s_zero, 16 * NOVF)
            n_ovf = act.value_load(ovi[0:1, 0:1], min_val=0, max_val=NOVF)
            for i in range(NOVF):
                with act.If(n_ovf > i):
                    e = NE + i
                    x_out(e, 0)
                    silu(e)
                    h_out(e)
                    act.wait_ge(s_yst[0], 16 * (NE // 2 + i))
                    y_out(e, 0)
                    act.dma_start(y_rows[CAP * e:CAP * (e + 1)], yo[:, 0]).then_inc(s_yst[0], 16)
                    act.wait_ge(s_yst[0], 16 * (NE // 2 + i + 1))
            act.activation(stat[:, 60:61], eps[:], ACT.Copy).then_inc(s_exdone, 1)
            for i, (t0, n) in enumerate(TILES):
                act.wait_ge(s_f, 2 * (i + 1))
                step(act.activation(sqf[0:n], x2[0:n, i], ACT.Square, accum_out=stat[0:n, 50 + i:51 + i]))
                act.activation(stat[0:n, 55 + i:56 + i], stat[0:n, 50 + i:51 + i], ACT.Sqrt, bias=eps[0:n], scale=1.0 / D).then_inc(s_fsq, 1)

        @block.tensor
        def _(pe):
            def transposes(ident_n, outs, done):
                for out, src in outs:
                    last = pe.transpose(out, src, ident[0:ident_n, 0:ident_n])
                last.then_inc(done, 1)

            pe.wait_ge(s_const, 1)
            for i, (t0, n) in enumerate(TILES):
                pe.wait_ge(s_h, i + 1)
                if i >= 2:
                    pe.wait_ge(s_hT, i - 1)
                b = 4 + 2 * (i % 2)
                transposes(n, [(ps[:, b + c // 4, P * (c % 4):P * (c % 4) + n], x0[0:n, i, P * c:P * c + P]) for c in range(KC)], s_hx)
            pe.wait_ge(s_hT, NTILE)

            def do(what, i=0):
                n = TILES[i][1] if i < NTILE else 0
                t0 = TILES[i][0] if i < NTILE else 0
                if what == "code":
                    pe.wait_ge(s_wcode, 96)
                    for b in range(2):
                        for c in range(KC):
                            last = pe.matmul(ps[0:RANK, 4 + b, 0:HALF], w_code[:, c], hT[:, c, HALF * b:HALF * b + HALF],
                                             start=c == 0, stop=c == KC - 1)
                    last.then_inc(s_code_mm, 1)
                elif what == "dec" and i < GH:
                    pe.wait_ge(s_code, 1)
                    if i >= 2:
                        pe.wait_ge(s_dec_rd, i - 1)
                        pe.wait_ge(s_ln, i - 1)
                    for b in range(2):
                        last = pe.matmul(ps[:, 4 + 2 * (i % 2) + b, 0:HALF], w_dec[:, P * i:P * i + P], code[:, HALF * b:HALF * b + HALF],
                                         start=True, stop=True)
                    last.then_inc(s_dec_mm, 1)
                elif what == "kend":
                    pe.wait_ge(s_qk, GH)
                    if i >= 4:
                        pe.wait_ge(s_ke, i - 3)
                    transposes(P, [(ps[0:n, 4 + i % 4, P * h:P * h + P], t2[:, h, t0:t0 + n]) for h in range(GH)], s_ke_mm)
                elif what == "gla":
                    gla_tile(i, t0, n)
                elif what == "kout":
                    b = 3 + 2 * (i % 2)
                    for u in stage_units[13][-2:]:
                        emptied(pe, u)
                    if i >= 2:
                        pe.wait_ge(s_krow, 2 * (i - 1))
                    transposes(P, [(ps[0:n, b + h // 4, P * (h % 4):P * (h % 4) + P], kbT[:, h, t0:t0 + n]) for h in range(DH)], s_kx)
                elif what == "attn":
                    attention()
                elif what == "router":
                    pe.wait_ge(s_h2, i + 1)
                    if i:
                        pe.wait_ge(s_h2T, i)
                    transposes(n, [(ps[:, 3 + c // 4, P * (c % 4):P * (c % 4) + n], h2[0:n, i % 2, P * c:P * c + P]) for c in range(KC)], s_h2x)
                    pe.wait_ge(s_h2T, i + 1)
                    if i:
                        pe.wait_ge(s_lg, i)
                    for c in range(KC):
                        last = pe.matmul(ps[0:n, 5, 0:NG + NE], h2T[:, c, 0:n], wr[:, c], start=c == 0, stop=c == KC - 1)
                    last.then_inc(s_lgm, 1)

            def gla_tile(i, t0, n):
                chunks = [2 * i, 2 * i + 1] if i < NTILE - 1 else [NCH - 1]
                m = CHUNK if i < NTILE - 1 else TS
                pe.wait_ge(s_ke, NTILE)
                for u in stage_units[3][-2:] + stage_units[2][-2:]:
                    emptied(pe, u)
                if i:
                    pe.wait_ge(s_oaT, i)
                for c in chunks:
                    p0, tc = CHUNK * (c % 2) if i < NTILE - 1 else 0, CHUNK * c
                    rows = slice(p0, p0 + m)
                    if c >= 2:
                        pe.wait_ge(s_att, c - 1)
                    for h in range(GH):
                        last = pe.matmul(ps[rows, 4, CHUNK * h:CHUNK * h + m], fmA[:, GH + h, tc:tc + m], fmA[:, h, tc:tc + m],
                                         start=True, stop=True)
                    last.then_inc(s_att_mm, 1)
                    if c:
                        pe.wait_ge(s_S, c)
                    for h in range(GH):
                        last = pe.matmul(ps[:, 3 + 4 * (h // 2), DV * (h % 2):DV * (h % 2) + DV], kend[rows, i, h], va[rows, i, DV * h:DV * h + DV],
                                         start=True, stop=True)
                    last.then_inc(s_dS, 1)
                    if c == NCH - 1:
                        pe.wait_ge(s_sin, 16)
                    pe.wait_ge(s_att, c + 1)
                    for h in range(GH):
                        out = ps[rows, 5 + h // 2, DV * (h % 2):DV * (h % 2) + DV]
                        if c:
                            state = S_in[:, h] if c == NCH - 1 else S[:, c % 2, h]
                            pe.matmul(out, fmA[:, h, tc:tc + m], state, start=True, stop=False)
                        last = pe.matmul(out, att[rows, h, 0:m], va[rows, i, DV * h:DV * h + DV], start=c == 0, stop=True)
                    last.then_inc(s_o, 1)
                pe.wait_ge(s_og, i + 1)
                transposes(n, [(ps[:, 5 + c // 4, P * (c % 4):P * (c % 4) + n], ra[0:n, i, P * c:P * c + P]) for c in range(8)], s_ox)

            def attention():
                for u in stage_units[11][-2:] + stage_units[15][-2:] + stage_units[14][-2:]:
                    emptied(pe, u)
                pe.wait_ge(s_krow, 2 * NTILE)

                def scores(k):
                    h, q = k // 4, k % 4
                    w, b = P * (q + 1), 3 + 2 * (k % 2)
                    if k >= 2:
                        pe.wait_ge(s_tt, 2 * (k - 1))
                    for a in range(2):
                        r = slice(DQ * a, DQ * a + DQ)
                        last = pe.matmul(ps[:, b + a, 0:w], qbT[r, h, P * q:P * q + P], kbT[r, h, 0:w], start=True, stop=True)
                    last.then_inc(s_scm, 1)

                def probs_t(k):
                    pe.wait_ge(s_pr, k + 1)
                    if k >= 2:
                        pe.wait_ge(s_pT, k - 1)
                    transposes(P, [(ps[:, k % 2, P * c:P * c + P], sc[:, k % 2, 0, P * c:P * c + P]) for c in range(k % 4 + 1)], s_px)

                def values(k):
                    h, q = k // 4, k % 4
                    bank = 2 + 5 * (h % 2)
                    pe.wait_ge(s_pT, k + 1)
                    if q == 0 and h >= 2:
                        pe.wait_ge(s_obT, h - 1)
                    for c in range(q + 1):
                        last = pe.matmul(ps[:, bank, DVB * q:DVB * q + DVB], pT[:, k % 2, P * c:P * c + P], vb[:, c, DVB * h:DVB * h + DVB],
                                         start=c == 0, stop=c == q)
                    last.then_inc(s_pvq, 1)

                def out_t(h):
                    pe.wait_ge(s_bo, h + 1)
                    bank = 2 + 5 * (h % 2)
                    transposes(P, [(ps[:, bank, P * q:P * q + P], ob[:, P * q:P * q + P]) for q in range(4)], s_bx)

                NK = 4 * DH
                scores(0)
                scores(1)
                for k in range(NK):
                    probs_t(k)
                    if k + 2 < NK:
                        scores(k + 2)
                    values(k)
                    if k % 4 == 2 and k >= 6:
                        out_t(k // 4 - 1)
                out_t(DH - 1)
                pe.wait_ge(s_obT, DH)
                pe.wait_ge(s_pT, NK)
                for g in range(2):
                    for j in range(4):
                        h = 4 * g + j
                        pe.wait_ge(s_kc[h % 2], 16 * (h // 2 + 1))
                        for b in range(2):
                            if h:
                                pe.wait_ge(s_kcT, 2 * h - 1 + b)
                            if j == 0 and g:
                                pe.wait_ge(s_spT, 3 * g)
                            transposes(P, [(ps[:, 6 + b, P * c:P * c + P], kraw[:, h % 2, 4 * b + c]) for c in range(4)], s_kcx)
                        pe.wait_ge(s_kcT, 2 * h + 2)
                        if j == 0 and g:
                            pe.wait_ge(s_obT, DH + g)
                        rows = slice(32 * j, 32 * j + 32)
                        for a in range(2):
                            r = slice(DQ * a, DQ * a + DQ)
                            for b in range(2):
                                pe.matmul(ps[rows, 3 * a + b], qbT[r, h, TP:NT], kcT[r, h % 2, 512 * b:512 * b + 512], start=True, stop=True)
                            last = pe.matmul(ps[rows, 3 * a + 2, 0:TS], qbT[r, h, TP:NT], kbT[r, h, TP:NT], start=True, stop=True)
                        last.then_inc(s_ssc, 1)
                    pe.wait_ge(s_spr, g + 1)
                    for b in range(3):
                        if b == 2:
                            pe.wait_ge(s_spT, 3 * g + 1)
                        if b == 0:
                            pe.wait_ge(s_kcT, 8 * (g + 1))
                        if b < 2:
                            transposes(P, [(ps[:, 6 + b, P * c:P * c + P], scs[:, 0, 512 * b + P * c:512 * b + P * c + P]) for c in range(4)], s_spx)
                        else:
                            transposes(P, [(ps[0:TS, 6, 0:P], scs[:, 0, PAST:PAST + TS])], s_spx)
                    pe.wait_ge(s_spT, 3 * g + 3)
                    for j in range(4):
                        h = 4 * g + j
                        pe.wait_ge(s_vc[h % 4], 16 * (h // 4 + 1))
                        for c in range(PAST // P + 1):
                            kk = P if c < PAST // P else TS
                            rhs = vc[:, h % 4, c] if c < PAST // P else vb[0:TS, 4, DVB * h:DVB * h + DVB]
                            last = pe.matmul(ps[0:TS, 0, DVB * j:DVB * j + DVB], pTs_v[0:kk, c, 32 * j:32 * j + 32], rhs,
                                             start=c == 0, stop=c == PAST // P)
                        last.then_inc(s_hpv, 1)
                    pe.wait_ge(s_bo, DH + g + 1)
                    transposes(TS, [(ps[:, 0, TS * j:TS * j + TS], ob[0:TS, P * j:P * j + P]) for j in range(4)], s_bx)

            for u, d in enumerate(units):
                n, kind, a, b, bank = d["tile"], d["kind"], d["a"], d["b"], bank_of[u]
                if d["first"]:
                    pe.wait_ge(s_w[n % RING], 16 * (n // RING + 1))
                    if kind == "pa":
                        pe.wait_ge(s_oaT, NTILE)
                    if kind == "gb":
                        pe.wait_ge(s_obT, DH + 2)
                    if kind == "wo" and d["nth"] == 0:
                        emptied(pe, stage_units[19][-1])
                if u >= 3:
                    emptied(pe, u - 3)
                w = ring[:, n % RING, :].rearrange("p (c n) -> p c n", c=KC)
                act_in = {"pa": fmA, "pb": obT, "wo": mixT}.get(kind, hT)
                for c in range(KC):
                    if d["token_major"]:
                        t0, m = TILES[a]
                        last = pe.matmul(ps[0:m, bank], act_in[:, c, t0:t0 + m], w[:, c], start=c == 0, stop=c == KC - 1)
                    else:
                        last = pe.matmul(ps[:, bank, 0:HALF], w[:, c, P * a:P * a + P], act_in[:, c, HALF * b:HALF * b + HALF],
                                         start=c == 0, stop=c == KC - 1)
                last.then_inc(s_unit, 1)
                for what in hooks.get(u, []):
                    do(*what)
            pe.wait_ge(s_A, 1)
            A = rt[:, 9].rearrange("p (i e) -> p i e", e=NE)
            for i, (t0, n) in enumerate(TILES):
                for j in range(i + 1):
                    k = TILES[j][1]
                    pe.matmul(ps[:, 0, NE * i:NE * i + NE], (upper if j == i else ones)[0:k, :], A[0:k, j], start=j == 0, stop=j == i)
            for j in range(NTILE):
                k = TILES[j][1]
                last = pe.matmul(ps[:, 0, NE * NTILE:NE * NTILE + NE], ones[0:k, :], A[0:k, j], start=j == 0, stop=j == NTILE - 1)
            last.then_inc(s_rank, 1)
            for i, (t0, n) in enumerate(TILES):
                pe.wait_ge(s_oh, i + 1)
                for j in range(NBLK):
                    last = pe.matmul(ps[:, 1, j:j + 1], onehot[0:n, i % 2, j], tok_id[0:n, i:i + 1], start=i == 0 and j == 0,
                                     stop=i == NTILE - 1, skip_group_check=True)
                last.then_inc(s_tok, 1)

            def XT(e, slot, count):
                pe.wait_ge(s_xg[slot], count)
                transposes(P, [(ps[:, 4 + c // 4, P * (c % 4):P * (c % 4) + P], xg[:, slot, P * c:P * c + P]) for c in range(KC)], s_xt)

            def GU(e, slot, count):
                pe.wait_ge(s_xtA, e + 1)
                pe.wait_ge(s_xtD, e + 1)
                for w, s, bank in ((wg, s_wg, 0), (wu, s_wu, 1)):
                    pe.wait_ge(s[slot], count)
                    for c in range(KC):
                        last = pe.matmul(ps[:, bank], xgT[:, slot, c], w[:, slot, c], start=c == 0, stop=c == KC - 1)
                last.then_inc(s_gu, 1)

            def AT(e, slot):
                pe.wait_ge(s_hh, e + 1)
                transposes(P, [(ps[:, 2, P * c:P * c + P], hh[:, slot, P * c:P * c + P]) for c in range(FE // P)], s_at)

            def Dn(e, slot, count):
                pe.wait_ge(s_hhT, e + 1)
                pe.wait_ge(s_wd[slot], count)
                for b in range(2):
                    for c in range(FE // P):
                        last = pe.matmul(ps[:, 6 + b], hhT[:, c], wd[:, slot, c, 512 * b:512 * b + 512], start=c == 0, stop=c == FE // P - 1)
                last.then_inc(s_dn, 1)

            def count(e, slot):
                return (e - slot) * 8 + 16

            pe.wait_ge(s_slot, 1)
            XT(0, 0, 16)
            GU(0, 0, 16)
            XT(1, 1, 16)

            def body(e, odd, last=False):
                pe.wait_ge(s_hh, e)
                GU(e, odd, count(e, odd))
                AT(e - 1, 1 - odd)
                if not last:
                    XT(e + 1, 1 - odd, count(e + 1, 1 - odd))
                after(pe, s_yA, e - 1)
                after(pe, s_yD, e - 1)
                Dn(e - 1, 1 - odd, count(e - 1, 1 - odd))

            body(1, 1)
            body(2, 0)
            with pe.Fori(1, NE // 2 - 1) as it:
                body(it * 2 + 1, 1)
                body(it * 2 + 2, 0)
            body(NE - 1, 1, last=True)
            AT(NE - 1, 1)
            pe.wait_ge(s_yA, NE - 1)
            pe.wait_ge(s_yD, NE - 1)
            Dn(NE - 1, 1, count(NE - 1, 1))
            n_ovf = pe.value_load(ovi[0:1, 0:1], min_val=0, max_val=NOVF)
            for i in range(NOVF):
                with pe.If(n_ovf > i):
                    e, c = NE + i, 16 * (NE // 2 + i + 1)
                    pe.wait_ge(s_yA, e)
                    pe.wait_ge(s_yD, e)
                    XT(e, 0, c)
                    GU(e, 0, c)
                    AT(e, 0)
                    Dn(e, 0, c)

        @block.vector
        def _(dve):
            steps = [0]

            def step(ins):
                steps[0] += 1
                ins.then_inc(s_dve, 1)
                dve.wait_ge(s_dve, steps[0])

            dve.memset(att[:], 0.0).then_inc(s_mz, 1)
            dve.wait_ge(s_small, 16 * 11)
            step(dve.tensor_tensor_reduce(lamt[:, 0], lamt[:, 0], lamt[:, 1], 1.0, 0.0, ALU.mult, ALU.add, lam[:, 0:1]))
            dve.tensor_tensor_reduce(lamt[:, 2], lamt[:, 2], lamt[:, 3], 1.0, 0.0, ALU.mult, ALU.add, lam[:, 1:2]).then_inc(s_lamp, 1)
            step(dve.tensor_scalar(g_diff_s, g_diff, 1.0 - LAM_INIT, None, ALU.mult))
            for i, (t0, n) in enumerate(TILES):
                dve.wait_ge(s_xsq, i + 1)
                step(dve.reciprocal(stat[0:n, 8 + i:9 + i], stat[0:n, 8 + i:9 + i]))
                dve.tensor_scalar(x0[0:n, i], x0[0:n, i], stat[0:n, 8 + i:9 + i], None, ALU.mult).then_inc(s_h, 1)
                dve.wait_ge(s_hx, i + 1)
                b = 4 + 2 * (i % 2)
                dve.tensor_tensor(hT[:, :, t0:t0 + n], ps[:, b:b + 2].rearrange("p b (c t) -> p (b c) t", t=P)[:, :, 0:n],
                                  rep(g_mix, 2, n), ALU.mult).then_inc(s_hT, 1)
            dve.wait_ge(s_lame, 1)
            step(dve.tensor_tensor(lam[:, 4:5], lam[:, 3:4], lam[:, 2:3], ALU.subtract))
            step(dve.tensor_scalar(lam[:, 4:5], lam[:, 4:5], LAM_INIT, None, ALU.subtract))
            dve.wait_ge(s_hT, NTILE)
            dve.wait_ge(s_const, 2)

            def do(what, i=0):
                n = TILES[i][1] if i < NTILE else 0
                t0 = TILES[i][0] if i < NTILE else 0
                if what == "dec":
                    if i < GH:
                        dve.wait_ge(s_abs, i + 1)
                        src = ps[:, 4 + 2 * (i % 2):6 + 2 * (i % 2), 0:HALF]
                        dve.tensor_scalar(bT[:, i].rearrange("p (b t) -> p b t", b=2), src, b_dec[:, i:i + 1], 0.0, ALU.add, ALU.min).then_inc(s_dec_rd, 1)
                    if 1 <= i <= GH:
                        f = i - 1
                        dve.wait_ge(s_ln, f + 1)
                        dve.wait_ge(s_dec_rd, f + 1)
                        step(dve.tensor_tensor(t1[:, f], bT[:, f], t1[:, f], ALU.subtract))
                        step(dve.tensor_tensor_scan(bT[:, f], keep[:], t1[:, f], 0.0, ALU.mult, ALU.add))
                        bv = bT[:, f, 0:TP].rearrange("p (c t) -> p c t", t=CHUNK)
                        step(dve.tensor_tensor(t2[:, f, 0:TP].rearrange("p (c t) -> p c t", t=CHUNK),
                                               rep(bv[:, :, CHUNK - 1], 2, CHUNK), bv, ALU.subtract))
                        dve.tensor_scalar(t2[:, f, TP:NT], bT[:, f, TP:NT], bT[:, f, NT - 1:NT], -1.0, ALU.subtract, ALU.mult).then_inc(s_delta, 1)
                    if i >= 2:
                        f = i - 2
                        if f == 0:
                            for u in stage_units[1][-2:]:
                                emptied(dve, u)
                        dve.wait_ge(s_exps, f + 1)
                        step(dve.tensor_tensor(t2[:, f], t2[:, f], fmA[:, GH + f], ALU.mult))
                        step(dve.tensor_tensor(fmA[:, GH + f], fmA[:, GH + f], t3[:, f], ALU.mult))
                        dve.scalar_tensor_tensor(fmA[:, f], fmA[:, f], DK ** -0.5, t1[:, f], ALU.mult, ALU.mult).then_inc(s_qk, 1)
                elif what == "gla":
                    chunks = [2 * i, 2 * i + 1] if i < NTILE - 1 else [NCH - 1]
                    m = CHUNK if i < NTILE - 1 else TS
                    for c in chunks:
                        p0 = CHUNK * (c % 2) if i < NTILE - 1 else 0
                        rows = slice(p0, p0 + m)
                        dve.wait_ge(s_att_mm, c + 1)
                        dve.wait_ge(s_mz, 1)
                        dve.wait_ge(s_zero, 16 * NOVF)
                        if c >= 2:
                            dve.wait_ge(s_o, c - 1)
                        dve.copy_predicated(att[rows, :, 0:m], rep(trimask[rows, 0:m], 1, GH),
                                            ps[rows, 4, 0:GH * CHUNK].rearrange("p (h t) -> p h t", h=GH)[:, :, 0:m]).then_inc(s_att, 1)
                        dve.wait_ge(s_dS, c + 1)
                        if c:
                            dve.wait_ge(s_o, c)
                            dve.wait_ge(s_S, c)
                        if c == NCH - 1:
                            dve.wait_ge(s_sin, 16)
                        for h in range(GH):
                            dS = ps[:, 3 + 4 * (h // 2), DV * (h % 2):DV * (h % 2) + DV]
                            if c == 0:
                                last = dve.tensor_copy(S[:, 1, h], dS)
                            else:
                                last = dve.scalar_tensor_tensor(S[:, (c + 1) % 2, h], S_in[:, h] if c == NCH - 1 else S[:, c % 2, h],
                                                                ebl[:, h, c:c + 1], dS, ALU.mult, ALU.add)
                        last.then_inc(s_S, 1)
                    dve.wait_ge(s_osq, i + 1)
                    step(dve.reciprocal(stat[0:n, 32:36], stat[0:n, 20:24]))
                    if i == 0:
                        for k in (4, 5):
                            emptied(dve, stage_units[k][-1])
                    for h in range(GH):
                        last = dve.scalar_tensor_tensor(ra[0:n, i, DV * h:DV * h + DV], ps[0:n, 5 + h // 2, DV * (h % 2):DV * (h % 2) + DV],
                                                        stat[0:n, 32 + h:33 + h], ra[0:n, i, DV * h:DV * h + DV], ALU.mult, ALU.mult)
                    last.then_inc(s_og, 1)
                    dve.wait_ge(s_ox, i + 1)
                    dve.tensor_tensor(fmA[:, :, t0:t0 + n], ps[:, 5:7].rearrange("p b (c t) -> p (b c) t", t=P)[:, :, 0:n],
                                      rep(g_gla, 2, n), ALU.mult).then_inc(s_oaT, 1)
                elif what == "attn":
                    attention()
                elif what == "h2":
                    dve.wait_ge(s_2sq, i + 1)
                    step(dve.reciprocal(stat[0:n, 45 + i:46 + i], stat[0:n, 45 + i:46 + i]))
                    if i == 0:
                        dve.wait_ge(s_g, 32)
                    if i >= 2:
                        dve.wait_ge(s_h2st[i % 2], 16 * (i // 2))
                        dve.wait_ge(s_h2x, i - 1)
                    dve.scalar_tensor_tensor(h2[0:n, i % 2], x2[0:n, i], stat[0:n, 45 + i:46 + i], gffn[0:n], ALU.mult, ALU.mult).then_inc(s_h2, 1)
                elif what == "router":
                    dve.wait_ge(s_lgm, i + 1)
                    if i == 0:
                        dve.wait_ge(s_c2, 1)
                    dve.tensor_tensor(lg[0:n, i], ps[0:n, 5, 0:NG + NE], br[0:n], ALU.add).then_inc(s_lg, 1)

            def attention():
                dve.wait_ge(s_dist, 1)
                step(dve.scalar_tensor_tensor(dist[:], dist[:], -1.0, dist[:], ALU.mult, ALU.max))
                step(dve.memset(dist[0:CHUNK, TP - CHUNK:TP], BIG))
                dve.scalar_tensor_tensor(dist_s[:], dist_s[:], -1.0, dist_s[:], ALU.mult, ALU.max).then_inc(s_bs, 1)

                def head_norm(n, k, bank):
                    dve.wait_ge(s_sqr, k + 1)
                    dve.tensor_reduce(stat[0:n, 24:28], ob[0:n].rearrange("p (q d) -> p q d", q=4), AX_X, ALU.add).then_inc(s_brs, 1)
                    dve.wait_ge(s_bsq, k + 1)
                    step(dve.reciprocal(stat[0:n, 36:40], stat[0:n, 28:32]))
                    if k:
                        dve.wait_ge(s_bx, k)
                    dve.tensor_tensor(ob[0:n].rearrange("p (q d) -> p q d", q=4), ps[0:n, bank].rearrange("p (q d) -> p q d", q=4),
                                      rep(stat[0:n, 36:40], 2, DVB), ALU.mult).then_inc(s_bo, 1)

                def head_out(k, bank, dst, src):
                    dve.wait_ge(s_bx, k + 1)
                    dve.tensor_scalar(dst, src, g_diff_s, None, ALU.mult).then_inc(s_obT, 1)

                def combine(k):
                    w = P * (k % 4 + 1)
                    st = att_st[:, k % 2]
                    dve.wait_ge(s_exp, k + 1)
                    step(dve.reciprocal(st[:, 4:6], st[:, 2:4]))
                    step(dve.tensor_tensor(st[:, 5:6], st[:, 5:6], lam[:, 4:5], ALU.mult))
                    step(dve.tensor_scalar(sc[:, k % 2, 1, 0:w], sc[:, k % 2, 1, 0:w], st[:, 5:6], None, ALU.mult))
                    dve.scalar_tensor_tensor(sc[:, k % 2, 0, 0:w], sc[:, k % 2, 0, 0:w], st[:, 4:5], sc[:, k % 2, 1, 0:w],
                                             ALU.mult, ALU.add).then_inc(s_pr, 1)

                k = 0
                for h in range(DH):
                    dve.wait_ge(s_bias, h + 1)
                    for q in range(4):
                        w, b = P * (q + 1), 3 + 2 * (k % 2)
                        dve.wait_ge(s_scm, k + 1)
                        if k >= 2:
                            dve.wait_ge(s_px, k - 1)
                        for a in range(2):
                            dve.tensor_tensor_reduce(sc[:, k % 2, a, 0:w], ps[:, b + a, 0:w], bias[:, h % 2, TP - w:TP], 1.0, 3.0e38,
                                                     ALU.add, ALU.min, att_st[:, k % 2, a:a + 1]).then_inc(s_tt, 1)
                        if k:
                            combine(k - 1)
                        if q == 2 and h:
                            head_norm(P, h - 1, 2 + 5 * ((h - 1) % 2))
                        if q == 3 and h:
                            head_out(h - 1, 0, qbT[:, h - 1, 0:TP], ps[:, 2 + 5 * ((h - 1) % 2)])
                        k += 1
                combine(k - 1)
                head_norm(P, DH - 1, 7)
                head_out(DH - 1, 0, qbT[:, DH - 1, 0:TP], ps[:, 7])
                dve.wait_ge(s_bs, 1)
                for g in range(2):
                    step(dve.tensor_scalar(bias_s, dist_s[:], slope[:, g:g + 1], None, ALU.mult))
                    dve.wait_ge(s_ssc, 4 * g + 4)
                    if g:
                        dve.wait_ge(s_spx, 3 * g)
                    for a in range(2):
                        dve.tensor_tensor_reduce(scs[:, a], ps[:, 3 * a:3 * a + 3].rearrange("p b n -> p (b n)")[:, 0:PAST + TS],
                                                 bias_s, 1.0, 3.0e38, ALU.add, ALU.min, att_st[:, g, a:a + 1]).then_inc(s_stt, 1)
                    st = att_st[:, g]
                    dve.wait_ge(s_sexp, g + 1)
                    step(dve.reciprocal(st[:, 4:6], st[:, 2:4]))
                    step(dve.tensor_tensor(st[:, 5:6], st[:, 5:6], lam[:, 4:5], ALU.mult))
                    step(dve.tensor_scalar(scs[:, 1], scs[:, 1], st[:, 5:6], None, ALU.mult))
                    dve.scalar_tensor_tensor(scs[:, 0], scs[:, 0], st[:, 4:5], scs[:, 1], ALU.mult, ALU.add).then_inc(s_spr, 1)
                    head_norm(TS, DH + g, 0)
                    head_out(DH + g, 0, qbT[:, 4 * g:4 * g + 4, TP:NT], ps[:, 0, 0:4 * TS].rearrange("p (j t) -> p j t", j=4))

            for u, d in enumerate(units):
                if d["eng"] == "D":
                    if u == first_qb or (u == first_qb + 1):
                        dve.wait_ge(s_Sst, 32)
                    dve.wait_ge(s_unit, u + 1)
                    kind, a, b, bank = d["kind"], d["a"], d["b"], bank_of[u]
                    if kind == "wo":
                        t0, n = TILES[a]
                        if d["nth"] == 0:
                            dve.wait_ge(s_x2[a], 16)
                        col = WC * d["nth"]
                        last = dve.tensor_tensor(x2[0:n, a, col:col + WC], ps[0:n, bank], x2[0:n, a, col:col + WC], ALU.add)
                        last.then_inc(s_ev["D"], 1)
                    elif d["token_major"]:
                        t0, n = TILES[a]
                        dst = {"va": va, "ra": ra, "vb": vb}[kind][0:n, a, WC * d["nth"]:WC * d["nth"] + WC]
                        dve.tensor_copy(dst, ps[0:n, bank]).then_inc(s_ev["D"], 1)
                    else:
                        f = 4 * d["nth"] + a
                        cols = slice(HALF * b, HALF * b + HALF)
                        src = ps[:, bank, 0:HALF]
                        if kind == "pa":
                            emptied(dve, u_of("ga", d["nth"], a, b))
                            dve.tensor_tensor(mixT[:, f, cols], src, mixT[:, f, cols], ALU.mult).then_inc(s_ev["D"], 1)
                        elif kind == "pb":
                            emptied(dve, u_of("gb", d["nth"], a, b))
                            step(dve.tensor_tensor(tmpm[:, b], src, sgb[:, a, cols], ALU.mult))
                            dve.tensor_tensor(mixT[:, f, cols], mixT[:, f, cols], tmpm[:, b], ALU.add).then_inc(s_ev["D"], 1)
                        elif kind == "qb":
                            dve.tensor_scalar(qbT[:, f, cols], src, -DQ ** -0.5, None, ALU.mult).then_inc(s_ev["D"], 1)
                        else:
                            dst = {"qa": fmA[:, f, cols], "ka": fmA[:, GH + a, cols], "kb": kbT[:, f, cols]}[kind]
                            dve.tensor_copy(dst, src).then_inc(s_ev["D"], 1)
                for what in hooks.get(u, []):
                    do(*what)

            def t3d(k, n):
                return rt[:, k, 0:NTILE * n].rearrange("p (i e) -> p i e", e=n)

            dve.wait_ge(s_lg, NTILE)
            gl, el = lg[:, :, 0:NG], lg[:, :, NG:NG + NE]
            step(dve.tensor_reduce(rs[:, 0], gl, AX_X, ALU.max))
            dve.tensor_tensor(t3d(0, NG), gl, rep(rs[:, 0], 2, NG), ALU.subtract).then_inc(s_gd, 1)

            def first_of(values, best, n, equal, cand, low, out):
                step(dve.tensor_tensor(equal, values, rep(best, 2, n), ALU.is_equal))
                step(dve.tensor_scalar(cand, equal, -64.0, None, ALU.mult))
                step(dve.tensor_tensor(cand, cand, rep(iota_e[:, 0:n], 1, NTILE), ALU.add))
                step(dve.tensor_reduce(low, cand, AX_X, ALU.min))
                step(dve.tensor_tensor(out, cand, rep(low, 2, n), ALU.is_equal))

            first_of(gl, rs[:, 0], NG, t3d(1, NG), t3d(2, NG), rs[:, 1], t3d(3, NG))
            step(dve.tensor_scalar(t3d(3, NG), t3d(3, NG), -1.0, BIG, ALU.add, ALU.mult))
            for i in range(NTILE):
                step(dve.tensor_tensor(t3d(4, NE)[:, i].rearrange("p (g e) -> p g e", g=NG), el[:, i].rearrange("p (g e) -> p g e", g=NG),
                                       rep(t3d(3, NG)[:, i], 2, EG), ALU.add))
            step(dve.tensor_reduce(rs[:, 2], t3d(4, NE), AX_X, ALU.max))
            first_of(t3d(4, NE), rs[:, 2], NE, t3d(5, NE), t3d(6, NE), rs[:, 3], t3d(7, NE))
            step(dve.scalar_tensor_tensor(t3d(4, NE), t3d(7, NE), -3.0 * BIG, t3d(4, NE), ALU.mult, ALU.add))
            step(dve.tensor_reduce(rs[:, 4], t3d(4, NE), AX_X, ALU.max))
            first_of(t3d(4, NE), rs[:, 4], NE, t3d(5, NE), t3d(6, NE), rs[:, 5], t3d(8, NE))
            dve.tensor_tensor(t3d(9, NE), t3d(7, NE), t3d(8, NE), ALU.add).then_inc(s_A, 1)
            dve.tensor_tensor(rs[:, 8], rs[:, 4], rs[:, 2], ALU.subtract).then_inc(s_ed, 1)
            dve.wait_ge(s_ge, 1)
            step(dve.tensor_reduce(rs[:, 6], t3d(0, NG), AX_X, ALU.add))
            step(dve.reciprocal(rs[:, 7], rs[:, 6]))
            dve.wait_ge(s_ee, 1)
            step(dve.tensor_scalar(rs[:, 9], rs[:, 8], 1.0, None, ALU.add))
            step(dve.reciprocal(rs[:, 10], rs[:, 9]))
            step(dve.tensor_tensor(rs[:, 11], rs[:, 10], rs[:, 7], ALU.mult))
            step(dve.tensor_tensor(rs[:, 12], rs[:, 11], rs[:, 8], ALU.mult))
            dve.wait_ge(s_rank, 1)
            dve.wait_ge(s_A, 1)
            rank = ps[:, 0, 0:NE * NTILE].rearrange("p (i e) -> p i e", e=NE)
            step(dve.tensor_copy(ov[:, 0], ps[:, 0, NE * NTILE:NE * NTILE + NE]))
            step(dve.scalar_tensor_tensor(t3d(10, NE), rank, 1.0, t3d(9, NE), ALU.add, ALU.mult))
            step(dve.tensor_scalar(rsel[:, :, 0:NE], t3d(10, NE), -1.0, None, ALU.add))
            step(dve.tensor_scalar(ov[:, 2], ov[:, 0], float(CAP), None, ALU.is_gt))
            for k in range(2, MORE + 1):
                step(dve.scalar_tensor_tensor(ov[:, 2], ov[:, 0], float(k * CAP), ov[:, 2], ALU.is_gt, ALU.add))
            step(dve.tensor_tensor_scan(ov[:, 3], ones[:, 0:NE], ov[:, 2], 0.0, ALU.mult, ALU.add))
            step(dve.tensor_tensor(ov[:, 4], ov[:, 3], ov[:, 2], ALU.subtract))
            step(dve.tensor_scalar(ov[:, 1], iota_e[:], float(CAP), None, ALU.mult))
            step(dve.tensor_scalar(ov[:, 6], ov[:, 4], NE - 1.0, float(CAP), ALU.add, ALU.mult))
            step(dve.tensor_tensor(ov[:, 6], ov[:, 6], ov[:, 1], ALU.subtract))
            step(dve.tensor_scalar(t3d(6, NE), rsel[:, :, 0:NE], float(CAP), None, ALU.is_ge))
            step(dve.tensor_tensor(t3d(6, NE), t3d(6, NE), rep(ov[:, 6], 1, NTILE), ALU.mult))
            step(dve.tensor_tensor(t3d(5, NE), rsel[:, :, 0:NE], rep(ov[:, 1], 1, NTILE), ALU.add))
            step(dve.tensor_tensor(t3d(5, NE), t3d(5, NE), t3d(6, NE), ALU.add))
            for k in range(2):
                step(dve.tensor_tensor(t3d(6, NE), t3d(5, NE), t3d(7 + k, NE), ALU.mult))
                step(dve.tensor_reduce(rs[:, 13], t3d(6, NE), AX_X, ALU.add))
                step(dve.tensor_copy(ysl[:, k], rs[:, 13]))
            ith = rep(iota_e[:, 0:NOVF], 2, NE)
            step(dve.tensor_tensor(ovm[:, :, 0], rep(ov[:, 4], 1, NOVF), ith, ALU.is_le))
            step(dve.tensor_tensor(ovm[:, :, 1], rep(ov[:, 3], 1, NOVF), ith, ALU.is_gt))
            step(dve.tensor_tensor(ovm[:, :, 0], ovm[:, :, 0], ovm[:, :, 1], ALU.mult))
            step(dve.tensor_tensor(ovm[:, :, 1], ovm[:, :, 0], rep(iota_e[:], 1, NOVF), ALU.mult))
            step(dve.tensor_reduce(ovb[:, :, 0], ovm[:, :, 1], AX_X, ALU.add))
            step(dve.tensor_tensor(ovm[:, :, 2], ith, rep(ov[:, 4], 1, NOVF), ALU.subtract))
            step(dve.tensor_tensor(ovm[:, :, 2], ovm[:, :, 2], ovm[:, :, 0], ALU.mult))
            step(dve.tensor_reduce(ovb[:, :, 1], ovm[:, :, 2], AX_X, ALU.add))
            step(dve.tensor_scalar(ovb[:, :, 1], ovb[:, :, 1], 1.0, float(CAP), ALU.add, ALU.mult))
            step(dve.tensor_copy(ovi[:, 1:1 + NOVF], ovb[:, :, 0]))
            step(dve.tensor_copy(ovi[:, 0:1], ov[:, 3, NE - 1:NE]))
            for i in range(NTILE):
                big = rt[:, 0:2].rearrange("p a b -> p (a b)")[:, 0:NOVF * NE].rearrange("p (a b) -> p a b", b=NE)
                step(dve.tensor_tensor(big, ovm[:, :, 0], rep(t3d(10, NE)[:, i], 1, NOVF), ALU.mult))
                step(dve.tensor_reduce(rsel[:, i, NE:NBLK], big, AX_X, ALU.add))
                step(dve.tensor_tensor(rsel[:, i, NE:NBLK], rsel[:, i, NE:NBLK], ovb[:, :, 1], ALU.subtract))
                step(dve.tensor_scalar(rsel[:, i, NE:NBLK], rsel[:, i, NE:NBLK], -1.0, None, ALU.add))
                if i >= 2:
                    dve.wait_ge(s_tok, i - 1)
                dve.tensor_tensor(onehot[:, i % 2], rep(iota_s[:], 1, NBLK), rep(rsel[:, i], 2, CAP), ALU.is_equal).then_inc(s_oh, 1)
            dve.wait_ge(s_tok, NTILE)
            dve.tensor_copy(slot_i[:], ps[:, 1, 0:NBLK]).then_inc(s_slot, 1)
            dve.wait_ge(s_slot, 1)

            def x_out(e, slot):
                dve.wait_ge(s_xt, e + 1)
                dve.tensor_copy(xgT[:, slot, 4:8].rearrange("p c t -> p (c t)"), ps[:, 5]).then_inc(s_xtD, 1)

            def gated(e, slot):
                dve.wait_ge(s_sg, e + 1)
                dve.tensor_tensor(hh[:, slot], ps[:, 1], sg[:], ALU.mult).then_inc(s_hh, 1)

            def y_out(e, slot):
                dve.wait_ge(s_dn, e + 1)
                dve.tensor_copy(yo[:, slot, 512:1024], ps[:, 7]).then_inc(s_yD, 1)

            def store_count(e, slot):
                return (e - slot) * 8

            def body(e, odd, last=False):
                after(dve, s_at, e - 1)
                gated(e, odd)
                if not last:
                    x_out(e + 1, 1 - odd)
                after(dve, s_yst[1 - odd], store_count(e - 1, 1 - odd))
                y_out(e - 1, 1 - odd)

            x_out(0, 0)
            gated(0, 0)
            x_out(1, 1)
            body(1, 1)
            body(2, 0)
            with dve.Fori(1, NE // 2 - 1) as it:
                body(it * 2 + 1, 1)
                body(it * 2 + 2, 0)
            body(NE - 1, 1, last=True)
            dve.wait_ge(s_yst[1], store_count(NE - 1, 1))
            y_out(NE - 1, 1)
            n_ovf = dve.value_load(ovi[0:1, 0:1], min_val=0, max_val=NOVF)
            for i in range(NOVF):
                with dve.If(n_ovf > i):
                    e = NE + i
                    x_out(e, 0)
                    gated(e, 0)
                    dve.wait_ge(s_yst[0], 16 * (NE // 2 + i))
                    y_out(e, 0)
            for i, (t0, n) in enumerate(TILES):
                dve.wait_ge(s_yg[i % 2], 32 * (i // 2 + 1))
                for k in range(2):
                    dve.scalar_tensor_tensor(x2[0:n, i], yg[0:n, i % 2, k], rs[0:n, 11 + k, i:i + 1], x2[0:n, i], ALU.mult, ALU.add).then_inc(s_f, 1)
                    dve.wait_ge(s_f, 2 * i + k + 1)
                dve.wait_ge(s_fsq, i + 1)
                step(dve.reciprocal(stat[0:n, 55 + i:56 + i], stat[0:n, 55 + i:56 + i]))
                if i >= 2:
                    dve.wait_ge(s_out[i % 2], 16 * (i // 2))
                dve.scalar_tensor_tensor(fo[0:n, i % 2], x2[0:n, i], stat[0:n, 55 + i:56 + i], gfin[0:n], ALU.mult, ALU.mult).then_inc(s_fo, 1)


_INS = ["x_prompt", "x_sample", "cache_k", "cache_v", "state_gla", "norm_mix", "w_in", "w_decay", "b_decay", "gla_norm",
        "w_proj_a", "lambda_q1", "lambda_k1", "lambda_q2", "lambda_k2", "diff_norm", "w_proj_b", "w_out", "norm_ffn",
        "w_router_group", "b_router_group", "w_router_expert", "b_router_expert", "w_gate", "w_up", "w_down", "norm_final"]
_OUTS = [(1, TP, D), (1, TS, D), (1, 1, TP, DH, 2 * DQ), (1, 1, TP, DH, DVB), (1, 1, GH, DK, DV),
         (1, 1, TS, DH, 2 * DQ), (1, 1, TS, DH, DVB), (1, 1, GH, DK, DV)]


def kernel(**inputs):
    import numpy as _np
    import concourse.bacc as _bacc
    from concourse import mybir as _mybir
    from concourse.bass_utils import run_bass_kernel_spmd as _run

    nc = _bacc.Bacc("TRN2", target_bir_lowering=False, num_devices=1)
    arrays, args = {}, []
    for name in _INS:
        a = _np.ascontiguousarray(inputs[name])
        arrays[f"in_{name}_dram"] = a
        args.append(nc.dram_tensor(f"in_{name}_dram", a.shape, _mybir.dt.from_np(a.dtype), kind="ExternalInput").ap())
    for i, shape in enumerate(_OUTS):
        args.append(nc.dram_tensor(f"out_{i}_dram", shape, F32, kind="ExternalOutput").ap())
    build(nc, *args)
    r = _run(nc, [arrays], core_ids=[0])
    return tuple(r.results[0][f"out_{i}_dram"] for i in range(len(_OUTS)))
```

```python
from contextlib import ExitStack

import concourse.bass as bass
from concourse import mybir

ALU = mybir.AluOpType
ACT = mybir.ActivationFunctionType
F32 = mybir.dt.float32
F16 = mybir.dt.float16
I32 = mybir.dt.int32
AX_X = mybir.AxisListType.X

P = 128
D = 1024
KC = D // P
TP = 512
TS = 32
NT = TP + TS
TILES = [(i * P, P) for i in range(TP // P)] + [(TP, TS)]
NTILE = len(TILES)
HALF = NT // 2
PAST = 1024
VBUF = 3
EPS = 1e-6
CHUNK = 64
GH, DK, DV = 4, 128, 256
RANK = 16
TAU = 16.0
NCH = TP // CHUNK + 1
DH, DVB = 8, 128
DQ = 64
LAM_INIT = 0.2
NG, EG = 4, 4
NE = NG * EG
FE = 512
CAP = 128
MORE = (NT - 1) // CAP
NOVF = 2 * NT // CAP
NBLK = NE + NOVF
BIG = 1e30
WC = 256
RING = 2
SPLIT = ("qa", "ka", "va", "ra", "ga", "qb", "kb", "vb", "gb")
F32R = mybir.dt.float32r

C_QA, C_KA, C_VA, C_RA, C_CODE = 0, 512, 1024, 2048, 3072
C_QB, C_KB, C_VB, C_GA, C_GB = 3088, 4112, 5136, 6160, 7184


def layout_of_units():
    stages = [("qa", "w_in", C_QA, GH * DK), ("ka", "w_in", C_KA, GH * DK), ("va", "w_in", C_VA, GH * DV),
              ("ra", "w_in", C_RA, GH * DV), ("ga", "w_in", C_GA, D), ("pa", "w_proj_a", 0, D),
              ("qb", "w_in", C_QB, D), ("kb", "w_in", C_KB, D), ("vb", "w_in", C_VB, D), ("gb", "w_in", C_GB, D),
              ("pb", "w_proj_b", 0, D), ("wo", "w_out", 0, D)]
    tiles, kinds, nth = [], [], []
    for kind, name, col, width in stages:
        for n in range(width // WC):
            tiles.append((name, col + n * WC))
            kinds.append(kind)
            nth.append(n)
    units, emptied = [], {"A": 0, "D": 0}
    for n, kind in enumerate(kinds):
        token_major = kind in ("va", "ra", "vb", "wo")
        parts = [(i, 0) for i in range(0, NTILE, 2)] if token_major else [(f, h) for f in range(WC // P) for h in range(2)]
        for m, (a, b) in enumerate(parts):
            if kind in ("ra", "ga", "gb"):
                eng = "A"
            elif kind in ("pa", "pb", "wo"):
                eng = "D"
            else:
                eng = "AD"[len(units) % 2]
            emptied[eng] += 1
            units.append(dict(tile=n, kind=kind, nth=nth[n], a=a, b=b, first=m == 0, last=m == len(parts) - 1,
                              eng=eng, count=emptied[eng], token_major=token_major))
    return tiles, kinds, units


def build(nc, x_prompt, x_sample, cache_k, cache_v, state_gla, norm_mix, w_in, w_decay, b_decay, gla_norm, w_proj_a,
          lambda_q1, lambda_k1, lambda_q2, lambda_k2, diff_norm, w_proj_b, w_out, norm_ffn, w_router_group,
          b_router_group, w_router_expert, b_router_expert, w_gate, w_up, w_down, norm_final,
          y_prompt, y_sample, new_k_p, new_v_p, new_s_p, new_k_s, new_v_s, new_s_s):
    wtiles, wkinds, units = layout_of_units()
    bank_of = [u % 3 for u in range(len(units))]
    stage_units = {}
    for u, d in enumerate(units):
        stage_units.setdefault(d["tile"], []).append(u)
    units_of = {}
    for u, d in enumerate(units):
        units_of.setdefault(d["kind"], []).append(u)
    split_at = {n: k for k, n in enumerate(n for n, kind in enumerate(wkinds) if kind in SPLIT)}
    split_tiles = list(split_at)

    h2_rows = nc.dram_tensor("h2_rows", (NT, D), F32)
    y_rows = nc.dram_tensor("y_rows", (NBLK * CAP, D), F32)
    h2_rows, y_rows = h2_rows.ap(), y_rows.ap()

    ctx = ExitStack()
    with ctx:
        def sem(name):
            return ctx.enter_context(nc.semaphore(name))

        def sb(name, shape, dt=F32, stack=ctx):
            return stack.enter_context(nc.sbuf_tensor(name, shape, dt))

        ps = ctx.enter_context(nc.psum_tensor("ps", [P, 8, 512], F32))

        ident = sb("ident", [P, P])
        trimask = sb("trimask", [P, CHUNK], I32)
        trif = sb("trif", [P, CHUNK])
        eps = sb("eps", [P, 1])
        ones = sb("ones", [P, P])
        small = sb("small", [P, 64])
        g_mix, g_gla, g_diff, b_dec = small[:, 0:8], small[:, 8:16], small[:, 16:17], small[:, 17:21]
        g_diff_s = small[:, 21:22]
        lamt = sb("lamt", [P, 4, DQ])
        lam = sb("lam", [P, 8])
        stat = sb("stat", [P, 64])
        wr = sb("wr", [P, KC, NG + NE])
        br = sb("br", [P, NG + NE])
        w_code = sb("w_code", [P, KC, RANK])
        w_dec = sb("w_dec", [RANK, GH * DK])

        dense = ExitStack()
        ring = sb("ring", [P, RING, KC * WC], stack=dense)
        w_hi = sb("w_hi", [P, 2, KC * WC], F32R, stack=dense)
        w_lo = sb("w_lo", [P, 2, KC * WC], F32R, stack=dense)

        decay = ExitStack()
        bT = sb("bT", [P, GH, NT], stack=decay)
        t2 = sb("t2", [P, GH, NT], stack=decay)
        t1 = sb("t1", [P, GH, NT], stack=decay)
        t3 = sb("t3", [P, GH, NT], stack=decay)
        decay.close()
        mixT = sb("mixT", [P, KC, NT], stack=dense)

        low = ExitStack()
        S = sb("S", [P, 2, GH, DV], stack=low)
        S_in = sb("S_in", [P, GH, DV], stack=low)
        kend = sb("kend", [P, NTILE, GH, DK], stack=low)
        att = sb("att", [P, GH, CHUNK], stack=low)
        ebl = sb("ebl", [P, GH, NCH], stack=low)
        keep = sb("keep", [P, NT], stack=low)
        code = sb("code", [RANK, NT], stack=low)
        sqa = sb("sqa", [P, DV], stack=low)
        low.close()
        qbT = sb("qbT", [P, DH, NT], stack=dense)
        obT = qbT
        sgb = sb("sgb", [P, KC, NT], stack=dense)

        ht = ExitStack()
        h_hi = sb("h_hi", [P, KC, NT], F32R, stack=ht)
        h_lo = sb("h_lo", [P, KC, NT], F32R, stack=ht)

        gla = ExitStack()
        xa = ExitStack()
        x0 = sb("x0", [P, NTILE, D], stack=xa)
        sq0 = sb("sq0", [P, D], stack=xa)
        xa.close()
        va = sb("va", [P, NTILE, GH * DV], stack=gla)
        ra = sb("ra", [P, NTILE, GH * DV], stack=gla)
        fmA = sb("fmA", [P, 8, NT], stack=gla)
        wc_hi = sb("wc_hi", [P, KC, P], F32R, stack=gla)
        wc_lo = sb("wc_lo", [P, KC, P], F32R, stack=gla)
        gla.close()

        dif = ExitStack()
        kbT = sb("kbT", [P, DH, NT], stack=dif)
        vb = sb("vb", [P, NTILE, DH * DVB], stack=dif)
        kb_rows = sb("kb_rows", [P, 2, D], stack=dif)
        dist = sb("dist", [P, TP], stack=dif)
        bias = sb("bias", [P, 2, TP + TS // 2], stack=dif)
        slope = sb("slope", [P, 2], stack=dif)
        sc = sb("sc", [P, 2, 2, TP + 16], stack=dif)
        pT = sb("pT", [P, 2, TP], stack=dif)
        att_st = sb("att_st", [P, 2, 8], stack=dif)
        ob = sb("ob", [P, TP], stack=dif)
        dif.close()
        ht.close()

        smp = ExitStack()
        kraw = sb("kraw", [P, 2, PAST // P, P], stack=smp)
        kcT = sb("kcT", [P, 2, PAST], stack=smp)
        vc = sb("vc", [P, VBUF, PAST // P, P], stack=smp)
        dist_s = sb("dist_s", [P, PAST + TS], stack=smp)
        smp.close()

        merge = ExitStack()
        tmpm = sb("tmpm", [P, 2, HALF], stack=merge)
        h2 = sb("h2", [P, 2, D], stack=merge)
        h2T = sb("h2T", [P, KC, P], stack=merge)
        sq2 = sb("sq2", [P, D], stack=merge)
        merge.close()
        dense.close()

        ex = ExitStack()
        wg = sb("wg", [P, 2, KC, FE], stack=ex)
        wu = sb("wu", [P, 2, KC, FE], stack=ex)
        wd = sb("wd", [P, 2, FE // P, D], stack=ex)
        xg = sb("xg", [P, 2, D], stack=ex)
        xgT = sb("xgT", [P, 2, KC, P], stack=ex)
        sg = sb("sg", [P, FE], stack=ex)
        hh = sb("hh", [P, 2, FE], stack=ex)
        hhT = sb("hhT", [P, FE // P, P], stack=ex)
        yo = sb("yo", [P, 2, D], stack=ex)
        x2 = sb("x2", [P, NTILE, D], stack=ex)
        gffn = sb("gffn", [P, D], stack=ex)
        gfin = sb("gfin", [P, D], stack=ex)
        lg = sb("lg", [P, NTILE, NG + NE], stack=ex)
        rt = sb("rt", [P, 12, NTILE * NE], stack=ex)
        rs = sb("rs", [P, 16, NTILE], stack=ex)
        iota_e = sb("iota_e", [P, NE], stack=ex)
        ov = sb("ov", [P, 8, NE], stack=ex)
        iota_s = sb("iota_s", [P, CAP], stack=ex)
        tok_id = sb("tok_id", [P, NTILE], F16, stack=ex)
        upper = sb("upper", [P, P], stack=ex)
        rsel = sb("rsel", [P, NTILE, NBLK], stack=ex)
        slot_i = sb("slot_i", [P, NBLK], I32, stack=ex)
        ysl = sb("ysl", [P, 2, NTILE], I32, stack=ex)
        ovb = sb("ovb", [P, NOVF, 2], stack=ex)
        ovi = sb("ovi", [P, 2 * NOVF + 2], I32, stack=ex)
        ovm = sb("ovm", [P, NOVF, 3, NE], stack=ex)
        onehot = sb("onehot", [P, 2, NBLK, CAP], F16, stack=ex)

        ex.close()
        fin = ExitStack()
        yg = sb("yg", [P, 2, 2, D], stack=fin)
        fo = sb("fo", [P, 2, D], stack=fin)
        sqf = sb("sqf", [P, D], stack=fin)
        fin.close()
        def rep(ap, axis, n):
            a = ap.unsqueeze(axis)
            shape = list(a.shape)
            shape[axis] = n
            return a.broadcast_to(shape)

        def after(eng, s, value):
            if not (isinstance(value, int) and value <= 0):
                eng.wait_ge(s, value)

        bias_s = bias[:].rearrange("p a n -> p (a n)")
        scs = sc[:].rearrange("p k a n -> p k (a n)")
        pTs_v = kb_rows[:].rearrange("p a n -> p (a n)")[:, 0:(PAST // P + 1) * P].rearrange("p (c q) -> p c q", q=P)

        def u_of(kind, nth, a, b):
            return next(u for u, d in enumerate(units) if (d["kind"], d["nth"], d["a"], d["b"]) == (kind, nth, a, b))

        s_x = [sem(f"s_x{i}") for i in range(NTILE)]
        s_small = sem("s_small")
        s_wcode = sem("s_wcode")
        s_const = sem("s_const")
        s_pool = sem("s_pool")
        s_dve = sem("s_dve")
        s_act = sem("s_act")
        s_lamp, s_lame = sem("s_lamp"), sem("s_lame")
        s_xsq, s_xrs = sem("s_xsq"), sem("s_xrs")
        s_h = sem("s_h")
        s_hx = sem("s_hx")
        s_hT = sem("s_hT")
        s_w = [sem(f"s_w{i}") for i in range(RING)]
        s_hi, s_lo = sem("s_hi"), sem("s_lo")
        s_wc_hi, s_wc = sem("s_wc_hi"), sem("s_wc")
        s_unit = sem("s_unit")
        s_ev = {"A": sem("s_evA"), "D": sem("s_evD")}
        s_code_mm, s_code = sem("s_code_mm"), sem("s_code")
        s_dec_mm, s_dec_rd = sem("s_dec_mm"), sem("s_dec_rd")
        s_abs, s_ln, s_delta, s_exps = sem("s_abs"), sem("s_ln"), sem("s_delta"), sem("s_exps")
        s_qk = sem("s_qk")
        s_ke_mm, s_ke = sem("s_ke_mm"), sem("s_ke")
        s_sin = sem("s_sin")
        s_att_mm, s_att = sem("s_att_mm"), sem("s_att")
        s_dS, s_S, s_o = sem("s_dS"), sem("s_S"), sem("s_o")
        s_osq, s_og = sem("s_osq"), sem("s_og")
        s_ox, s_oaT = sem("s_ox"), sem("s_oaT")
        s_Sst = sem("s_Sst")
        s_mz = sem("s_mz")
        s_dist = sem("s_dist")
        s_bs = sem("s_bs")
        s_bias = sem("s_bias")
        s_kx, s_krow, s_kst, s_vst = sem("s_kx"), sem("s_krow"), [sem("s_kst0"), sem("s_kst1")], sem("s_vst")
        s_scm, s_tt, s_exp = sem("s_scm"), sem("s_tt"), sem("s_exp")
        s_pr, s_px, s_pT, s_pvq = sem("s_pr"), sem("s_px"), sem("s_pT"), sem("s_pvq")
        s_sqr = sem("s_sqr")
        s_bsq, s_brs, s_bo, s_bx, s_obT = sem("s_bsq"), sem("s_brs"), sem("s_bo"), sem("s_bx"), sem("s_obT")
        s_kc = [sem("s_kc0"), sem("s_kc1")]
        s_vc = [sem(f"s_vc{i}") for i in range(VBUF)]
        s_kcx, s_kcT = sem("s_kcx"), sem("s_kcT")
        s_ssc, s_stt, s_sexp, s_spr = sem("s_ssc"), sem("s_stt"), sem("s_sexp"), sem("s_spr")
        s_spx, s_spT, s_hpv = sem("s_spx"), sem("s_spT"), sem("s_hpv")
        s_x2 = [sem(f"s_x2_{i}") for i in range(NTILE)]
        s_g = sem("s_g")
        s_c2 = sem("s_c2")
        s_2sq, s_2rs, s_h2, s_h2st = sem("s_2sq"), sem("s_2rs"), sem("s_h2"), [sem("s_h2st0"), sem("s_h2st1")]
        s_h2x, s_h2T, s_lgm, s_lg = sem("s_h2x"), sem("s_h2T"), sem("s_lgm"), sem("s_lg")
        s_gd, s_ge, s_ed, s_ee = sem("s_gd"), sem("s_ge"), sem("s_ed"), sem("s_ee")
        s_A, s_rank, s_oh, s_ohu, s_tok, s_slot = (sem(n) for n in ("s_A", "s_rank", "s_oh", "s_ohu", "s_tok", "s_slot"))
        s_wg, s_wu, s_wd = ([sem(f"s_{n}{i}") for i in range(2)] for n in ("wg", "wu", "wd"))
        s_xg = [sem("s_xg0"), sem("s_xg1")]
        s_xt, s_xtA, s_xtD, s_gu, s_sg, s_hh, s_at, s_hhT, s_dn, s_yA, s_yD = (
            sem(n) for n in ("s_xt", "s_xtA", "s_xtD", "s_gu", "s_sg", "s_hh", "s_at", "s_hhT", "s_dn", "s_yA", "s_yD"))
        s_yst = [sem("s_yst0"), sem("s_yst1")]
        s_zero = sem("s_zero")
        s_exdone = sem("s_exdone")
        s_yg = [sem("s_yg0"), sem("s_yg1")]
        s_f, s_fsq, s_frs, s_fo, s_out = sem("s_f"), sem("s_fsq"), sem("s_frs"), sem("s_fo"), [sem("s_out0"), sem("s_out1")]

        hooks = {}

        def hook(u, *what):
            hooks.setdefault(u, []).append(what)

        hook(units_of["ka"][-1], "code")
        for f in range(GH + 2):
            hook(units_of["va"][2 * f], "dec", f)
        for i in range(NTILE):
            hook(units_of["ra"][6 + i], "kend", i)
            hook(units_of["ga"][3 * i + 2], "gla", i)
            hook(units_of["vb"][2 * i + 1], "kout", i)
        hook(units_of["gb"][-1], "attn")
        last_wo = [units_of["wo"][-len(TILES[::2]) + i // 2] for i in range(NTILE)]
        for i in range(NTILE):
            hook(last_wo[i], "h2", i)
            hook(last_wo[min(i + 1, NTILE - 1)], "router", i)
        first_qb, last_unit = units_of["qb"][0], len(units) - 1
        last_pa = units_of["pa"][-1]

        def tile_ring(n):
            return ring[:, n % RING]

        def rows_of(dst, d, bank):
            a, cols = d["a"], slice(WC * d["nth"], WC * d["nth"] + WC)
            if a < NTILE - 1:
                return dst[:, a:a + 2, cols], ps[:, bank].rearrange("p (i n) -> p i n", n=WC)
            p0 = P - TS if d["tile"] in split_at else 0
            return dst[0:TS, a, cols], ps[p0:p0 + TS, bank, 0:WC]

        def emptied(eng, u):
            eng.wait_ge(s_ev[units[u]["eng"]], units[u]["count"])

        block = ctx.enter_context(nc.Block())

        @block.sync
        def _(sp):
            dram = {"w_in": w_in, "w_proj_a": w_proj_a, "w_proj_b": w_proj_b, "w_out": w_out}
            for n, (name, col) in enumerate(wtiles):
                if n - RING in split_at:
                    sp.wait_ge(s_lo, split_at[n - RING] + 1)
                elif n >= RING:
                    sp.wait_ge(s_unit, stage_units[n - RING][-1] + 1)
                src = dram[name][0, :, col:col + WC].rearrange("(c p) n -> p c n", p=P)
                sp.dma_start(ring[:, n % RING, :].rearrange("p (c n) -> p c n", c=KC), src).then_inc(s_w[n % RING], 16)
            sp.wait_ge(s_unit, last_unit + 1)

            def load_expert(e, slot):
                e1 = bass.ds(e, 1)
                sp.dma_start(wg[:, slot], w_gate[0, e1].rearrange("a (c p) n -> p (a c) n", p=P)).then_inc(s_wg[slot], 16)
                sp.dma_start(wu[:, slot], w_up[0, e1].rearrange("a (c p) n -> p (a c) n", p=P)).then_inc(s_wu[slot], 16)
                return w_down[0, e1].rearrange("a (c p) n -> p (a c) n", p=P)

            for e in range(2):
                src = load_expert(e, e)
                sp.dma_start(wd[:, e], src).then_inc(s_wd[e], 16)
            with sp.Fori(0, NE // 2 - 1) as it:
                for k in range(2):
                    sp.wait_ge(s_gu, it * 2 + (k + 1))
                    src = load_expert(it * 2 + (k + 2), k)
                    sp.wait_ge(s_dn, it * 2 + (k + 1))
                    sp.dma_start(wd[:, k], src).then_inc(s_wd[k], 16)
            sp.wait_ge(s_slot, 1)
            n_ovf = sp.value_load(ovi[0:1, 0:1], min_val=0, max_val=NOVF)
            for i in range(NOVF):
                e = sp.value_load(ovi[0:1, 1 + i:2 + i], min_val=0, max_val=NE - 1)
                with sp.If(n_ovf > i):
                    sp.wait_ge(s_gu, NE + i)
                    sp.wait_ge(s_dn, NE + i)
                    src = load_expert(e, 0)
                    sp.dma_start(wd[:, 0], src).then_inc(s_wd[0], 16)
            for i, (t0, n) in enumerate(TILES):
                sp.wait_ge(s_fo, i + 1)
                dst = y_prompt[0, t0:t0 + n] if i < NTILE - 1 else y_sample[0]
                sp.dma_start(dst, fo[0:n, i % 2]).then_inc(s_out[i % 2], 16)
            sp.wait_ge(s_out[0], 48)
            sp.wait_ge(s_out[1], 32)
            for i in range(2):
                sp.wait_ge(s_kst[i], 16 * ((NTILE + 1 - i) // 2))
                sp.wait_ge(s_h2st[i], 16 * ((NTILE + 1 - i) // 2))
            sp.wait_ge(s_vst, 32)
            sp.wait_ge(s_Sst, 32)

        @block.gpsimd
        def _(pool):
            steps = [0]

            def step(ins):
                steps[0] += 1
                ins.then_inc(s_pool, 1)
                pool.wait_ge(s_pool, steps[0])

            step(pool.memset(ident[:], 0.0))
            step(pool.affine_select(out=ident[:], in_=ident[:], compare_op=ALU.not_equal, fill=1.0, base=0,
                                    pattern=[[-1, P]], channel_multiplier=1))
            step(pool.memset(ones[:], 1.0))
            step(pool.memset(wc_hi[:].bitcast(F32), 0.0))
            step(pool.memset(wc_lo[:].bitcast(F32), 0.0))
            step(pool.memset(eps[:], EPS))
            pool.wait_ge(s_mz, 1)
            for i in range(NOVF):
                pool.dma_start(y_rows[CAP * (NE + i):CAP * (NE + i + 1)].rearrange("p (a n) -> p a n", n=256),
                               rep(att[:].rearrange("p h t -> p (h t)"), 1, D // 256)).then_inc(s_zero, 16)
            step(pool.memset(trif[:], 1.0))
            for a in range(2):
                t = trif[64 * a:64 * a + 64, :]
                step(pool.affine_select(out=t, in_=t, compare_op=ALU.is_ge, fill=0.0, base=0,
                                        pattern=[[1, CHUNK]], channel_multiplier=-1))
            pool.tensor_copy(trimask[:], trif[:]).then_inc(s_const, 1)
            step(pool.memset(keep[:], 1.0))
            step(pool.memset(keep[:, 0:TP].rearrange("p (c t) -> p c t", t=CHUNK)[:, :, 0:1], 0.0))
            pool.memset(keep[:, TP:TP + 1], 0.0).then_inc(s_const, 1)
            pool.wait_ge(s_ke_mm, NTILE)
            pool.dma_start(S_in[:], state_gla[0, 0].rearrange("h k v -> k h v")).then_inc(s_sin, 16)
            pool.wait_ge(s_S, NCH - 1)
            pool.dma_start(new_s_p[0, 0].rearrange("h k v -> k h v"), S[:, 0]).then_inc(s_Sst, 16)
            pool.wait_ge(s_S, NCH)
            pool.dma_start(new_s_s[0, 0].rearrange("h k v -> k h v"), S[:, 1]).then_inc(s_Sst, 16)
            pool.wait_ge(s_unit, last_pa + 1)
            emptied(pool, last_pa)
            pool.wait_ge(s_Sst, 32)
            step(pool.iota(dist[:], pattern=[[-1, TP]], base=TP - P, channel_multiplier=1,
                           allow_small_or_imprecise_dtypes=True))
            for j in range(4):
                for g in range(2):
                    step(pool.memset(slope[32 * j:32 * j + 32, g:g + 1], 2.0 ** -(4 * g + j + 1)))
            step(pool.memset(att_st[:], 0.0))
            for i, (t0, n) in enumerate(TILES):
                pool.wait_ge(s_krow, 2 * (i + 1))
                dst = new_k_p[0, 0, t0:t0 + n] if i < NTILE - 1 else new_k_s[0, 0]
                pool.dma_start(dst.rearrange("t h d -> t (h d)"), kb_rows[0:n, i % 2]).then_inc(s_kst[i % 2], 16)
            emptied(pool, units_of["vb"][-1])
            emptied(pool, units_of["vb"][-2])
            pool.dma_start(new_v_p[0, 0].rearrange("(i p) h d -> p i (h d)", p=P), vb[:, 0:4]).then_inc(s_vst, 16)
            pool.dma_start(new_v_s[0, 0].rearrange("t h d -> t (h d)"), vb[0:TS, 4]).then_inc(s_vst, 16)
            pool.wait_ge(s_unit, units_of["gb"][-1] + 1)
            for j in range(4):
                last = pool.iota(dist_s[32 * j:32 * j + 32], pattern=[[-1, PAST + TS]], base=PAST,
                                 channel_multiplier=1, allow_small_or_imprecise_dtypes=True)
            last.then_inc(s_dist, 1)

            def load_cache(h):
                pool.dma_start(kraw[:, h % 2], cache_k[0, 0, :, h, :].rearrange("(c p) d -> p c d", p=P)).then_inc(s_kc[h % 2], 16)
                if h >= VBUF:
                    pool.wait_ge(s_hpv, h - VBUF + 1)
                pool.dma_start(vc[:, h % VBUF], cache_v[0, 0, :, h, :].rearrange("(c p) d -> p c d", p=P)).then_inc(s_vc[h % VBUF], 16)

            for h in range(2):
                load_cache(h)
            pool.wait_ge(s_bs, 1)
            for h in range(DH):
                if h >= 2:
                    pool.wait_ge(s_tt, 8 * (h - 1))
                pool.tensor_scalar(bias[:, h % 2, 0:TP], dist[:], 2.0 ** -(h + 1), None, ALU.mult).then_inc(s_bias, 1)
            for h in range(2, DH):
                pool.wait_ge(s_kcx, 2 * (h - 1))
                load_cache(h)
            pool.wait_ge(s_obT, DH + 2)
            for i in range(2):
                pool.wait_ge(s_kst[i], 16 * ((NTILE + 1 - i) // 2))
            pool.wait_ge(s_vst, 32)
            for i, (t0, n) in enumerate(TILES):
                src = x_prompt[0, t0:t0 + n] if i < NTILE - 1 else x_sample[0]
                pool.dma_start(x2[0:n, i], src).then_inc(s_x2[i], 16)
            pool.dma_start(gffn[:], norm_ffn.broadcast_to([P, D])).then_inc(s_g, 16)
            pool.dma_start(gfin[:], norm_final.unsqueeze(0).broadcast_to([P, D])).then_inc(s_g, 16)
            step(pool.iota(iota_e[:], pattern=[[1, NE]], base=0, channel_multiplier=0, allow_small_or_imprecise_dtypes=True))
            step(pool.iota(iota_s[:], pattern=[[1, CAP]], base=0, channel_multiplier=0, allow_small_or_imprecise_dtypes=True))
            step(pool.iota(tok_id[:], pattern=[[P, NTILE]], base=0, channel_multiplier=1, allow_small_or_imprecise_dtypes=True))
            step(pool.memset(upper[:], 1.0))
            step(pool.affine_select(out=upper[:], in_=upper[:], compare_op=ALU.is_gt, fill=0.0, base=0,
                                    pattern=[[1, P]], channel_multiplier=-1))
            pool.memset(lg[:], 0.0).then_inc(s_c2, 1)

            def rows_in(i):
                n = TILES[i][1]
                pool.wait_ge(s_h2, i + 1)
                pool.dma_start(h2_rows[TILES[i][0]:TILES[i][0] + n], h2[0:n, i % 2]).then_inc(s_h2st[i % 2], 16)

            for i in range(NTILE):
                rows_in(i)
            pool.wait_ge(s_h2st[0], 48)
            pool.wait_ge(s_h2st[1], 32)
            pool.wait_ge(s_slot, 1)

            def gather(j, slot):
                pool.indirect_dma_start(xg[:, slot], None, h2_rows,
                                        bass.IndirectOffsetOnAxis(slot_i[:, j:j + 1], 0)).then_inc(s_xg[slot], 16)

            for e in range(NE):
                if e >= 2:
                    pool.wait_ge(s_xt, e - 1)
                gather(e, e % 2)
            n_ovf = pool.value_load(ovi[0:1, 0:1], min_val=0, max_val=NOVF)
            for i in range(NOVF):
                with pool.If(n_ovf > i):
                    pool.wait_ge(s_xt, NE + i)
                    gather(NE + i, 0)
            pool.wait_ge(s_yst[0], 16 * NE // 2)
            pool.wait_ge(s_yst[1], 16 * NE // 2)
            pool.wait_ge(s_exdone, 1)
            for i, (t0, n) in enumerate(TILES):
                if i >= 2:
                    pool.wait_ge(s_f, 2 * (i - 1))
                for k in range(2):
                    pool.indirect_dma_start(yg[0:n, i % 2, k], None, y_rows,
                                            bass.IndirectOffsetOnAxis(ysl[0:n, k, i:i + 1], 0)).then_inc(s_yg[i % 2], 16)

        @block.scalar
        def _(act):
            steps = [0]

            def step(ins):
                steps[0] += 1
                ins.then_inc(s_act, 1)
                act.wait_ge(s_act, steps[0])

            for i, (t0, n) in enumerate(TILES):
                src = x_prompt[0, t0:t0 + n] if i < NTILE - 1 else x_sample[0]
                act.dma_start(x0[0:n, i], src).then_inc(s_x[i], 16)
            with nc.allow_non_contiguous_dma("a few parameter columns"):
                act.dma_start(g_mix, norm_mix[0].rearrange("(c p) -> p c", p=P)).then_inc(s_small, 16)
                for h in range(GH):
                    act.dma_start(g_gla[:, 2 * h:2 * h + 2], gla_norm[0].rearrange("(c p) -> p c", p=P)).then_inc(s_small, 16)
                act.dma_start(g_diff, diff_norm[0].rearrange("(c p) -> p c", p=P)).then_inc(s_small, 16)
                act.dma_start(b_dec, b_decay[0].rearrange("(c p) -> p c", p=P)).then_inc(s_small, 16)
                for k, l in enumerate((lambda_q1, lambda_k1, lambda_q2, lambda_k2)):
                    act.dma_start(lamt[:, k], l.broadcast_to([P, DQ])).then_inc(s_small, 16)
                act.dma_start(w_code[:], w_in[0, :, C_CODE:C_CODE + RANK].rearrange("(c p) n -> p c n", p=P)).then_inc(s_wcode, 16)
                act.dma_start(w_dec[:], w_decay[0]).then_inc(s_wcode, 16)
                act.dma_start(wr[:, :, 0:NG], w_router_group[0].rearrange("(c p) n -> p c n", p=P)).then_inc(s_wcode, 16)
                act.dma_start(wr[:, :, NG:NG + NE], w_router_expert[0].rearrange("(c p) n -> p c n", p=P)).then_inc(s_wcode, 16)
                act.dma_start(br[:, 0:NG], b_router_group.broadcast_to([P, NG])).then_inc(s_wcode, 16)
                act.dma_start(br[:, NG:NG + NE], b_router_expert.broadcast_to([P, NE])).then_inc(s_wcode, 16)
            act.wait_ge(s_const, 1)
            for i, (t0, n) in enumerate(TILES):
                act.wait_ge(s_x[i], 16)
                step(act.activation(sq0[0:n], x0[0:n, i], ACT.Square, accum_out=stat[0:n, i:i + 1]))
                act.activation(stat[0:n, 8 + i:9 + i], stat[0:n, i:i + 1], ACT.Sqrt, bias=eps[0:n], scale=1.0 / D).then_inc(s_xsq, 1)
            act.wait_ge(s_wcode, 96)
            act.activation(wc_hi[:, :, 0:RANK], w_code[:], ACT.Copy).then_inc(s_wc_hi, 1)
            act.wait_ge(s_lamp, 1)
            act.activation(lam[:, 2:4], lam[:, 0:2], ACT.Exp).then_inc(s_lame, 1)

            def take_apart(n):
                k = split_at[n]
                act.wait_ge(s_w[n % RING], 16 * (n // RING + 1))
                if k >= 2:
                    act.wait_ge(s_unit, stage_units[split_tiles[k - 2]][-1] + 1)
                act.activation(w_hi[:, k % 2], tile_ring(n), ACT.Copy).then_inc(s_hi, 1)

            def do(what, i=0):
                if what == "code":
                    act.wait_ge(s_code_mm, 1)
                    act.activation(code[:].rearrange("r (b t) -> r b t", b=2), ps[0:RANK, 4:6, 0:HALF], ACT.Copy).then_inc(s_code, 1)
                elif what == "dec":
                    if i < GH:
                        act.wait_ge(s_dec_mm, i + 1)
                        act.activation(t1[:, i].rearrange("p (b t) -> p b t", b=2), ps[:, 4 + 2 * (i % 2):6 + 2 * (i % 2), 0:HALF],
                                       ACT.Abs, bias=b_dec[:, i:i + 1]).then_inc(s_abs, 1)
                        act.wait_ge(s_abs, i + 1)
                        step(act.activation(t1[:, i], t1[:, i], ACT.Exp, scale=-1.0))
                        act.activation(t1[:, i], t1[:, i], ACT.Ln, bias=ones[:, 0:1]).then_inc(s_ln, 1)
                    if 1 <= i <= GH:
                        f = i - 1
                        act.wait_ge(s_delta, f + 1)
                        act.activation(t2[:, f], t2[:, f], ACT.Exp, scale=1.0 / TAU)
                        act.activation(t1[:, f], bT[:, f], ACT.Exp, scale=1.0 / TAU)
                        act.activation(t3[:, f], bT[:, f], ACT.Exp, scale=-1.0 / TAU)
                        act.activation(ebl[:, f, 0:8], bT[:, f, 0:TP].rearrange("p (c t) -> p c t", t=CHUNK)[:, :, CHUNK - 1],
                                       ACT.Exp, scale=1.0 / TAU)
                        act.activation(ebl[:, f, 8:9], bT[:, f, NT - 1:NT], ACT.Exp, scale=1.0 / TAU).then_inc(s_exps, 1)
                elif what == "kend":
                    n = TILES[i][1]
                    act.wait_ge(s_ke_mm, i + 1)
                    act.activation(kend[0:n, i].rearrange("p h d -> p (h d)"), ps[0:n, 4 + i % 4], ACT.Copy).then_inc(s_ke, 1)
                elif what == "gla":
                    n = TILES[i][1]
                    act.wait_ge(s_o, min(2 * i + 2, NCH))
                    for h in range(GH):
                        step(act.activation(sqa[0:n], ps[0:n, 5 + h // 2, DV * (h % 2):DV * (h % 2) + DV], ACT.Square,
                                            accum_out=stat[0:n, 16 + h:17 + h]))
                    if i:
                        act.wait_ge(s_og, i)
                    act.activation(stat[0:n, 20:24], stat[0:n, 16:20], ACT.Sqrt, bias=eps[0:n], scale=1.0 / DV).then_inc(s_osq, 1)
                elif what == "kout":
                    n, b = TILES[i][1], 3 + 2 * (i % 2)
                    act.wait_ge(s_kx, i + 1)
                    if i >= 2:
                        act.wait_ge(s_kst[i % 2], 16 * (i // 2))
                    for k in range(2):
                        act.activation(kb_rows[0:n, i % 2, 512 * k:512 * k + 512], ps[0:n, b + k], ACT.Copy).then_inc(s_krow, 1)
                elif what == "attn":
                    attention()
                elif what == "h2":
                    n = TILES[i][1]
                    emptied(act, last_wo[i])
                    step(act.activation(sq2[0:n], x2[0:n, i], ACT.Square, accum_out=stat[0:n, 40 + i:41 + i]))
                    act.activation(stat[0:n, 45 + i:46 + i], stat[0:n, 40 + i:41 + i], ACT.Sqrt, bias=eps[0:n], scale=1.0 / D).then_inc(s_2sq, 1)
                elif what == "router":
                    n = TILES[i][1]
                    act.wait_ge(s_h2x, i + 1)
                    if i:
                        act.wait_ge(s_lgm, i)
                    act.activation(h2T[:, :, 0:n], ps[:, 3:5].rearrange("p b (c t) -> p (b c) t", t=P)[:, :, 0:n], ACT.Copy).then_inc(s_h2T, 1)

            def attention():
                n_norm = [0]

                def head_norm(n, bank):
                    k = n_norm[0]
                    if k < DH:
                        act.wait_ge(s_pvq, 4 * (k + 1))
                    else:
                        act.wait_ge(s_hpv, 4 * (k - DH + 1))
                    if k:
                        act.wait_ge(s_bo, k)
                        act.wait_ge(s_bx, k)
                    act.activation(ob[0:n], ps[0:n, bank], ACT.Square).then_inc(s_sqr, 1)
                    act.wait_ge(s_brs, k + 1)
                    act.activation(stat[0:n, 28:32], stat[0:n, 24:28], ACT.Sqrt, bias=eps[0:n], scale=1.0 / DVB).then_inc(s_bsq, 1)
                    n_norm[0] += 1

                k = 0
                for h in range(DH):
                    for q in range(4):
                        w = P * (q + 1)
                        act.wait_ge(s_tt, 2 * k + 2)
                        act.activation(sc[:, k % 2, 0, 0:w], sc[:, k % 2, 0, 0:w], ACT.Exp, bias=att_st[:, k % 2, 0:1],
                                       scale=-1.0, accum_out=att_st[:, k % 2, 2:3])
                        act.activation(sc[:, k % 2, 1, 0:w], sc[:, k % 2, 1, 0:w], ACT.Exp, bias=att_st[:, k % 2, 1:2],
                                       scale=-1.0, accum_out=att_st[:, k % 2, 3:4]).then_inc(s_exp, 1)
                        if k >= 1:
                            probs_out(k - 1)
                        if q == 2 and h:
                            head_norm(P, 2 + 5 * ((h - 1) % 2))
                        k += 1
                probs_out(k - 1)
                head_norm(P, 7)
                for g in range(2):
                    for j in range(4):
                        h = 4 * g + j
                        for b in range(2):
                            act.wait_ge(s_kcx, 2 * h + b + 1)
                            if h >= 2:
                                act.wait_ge(s_ssc, h - 1)
                            act.activation(kcT[:, h % 2, 512 * b:512 * b + 512], ps[:, 6 + b], ACT.Copy).then_inc(s_kcT, 1)
                    act.wait_ge(s_stt, 2 * g + 2)
                    for b in range(2):
                        c = act.activation(scs[:, b], scs[:, b], ACT.Exp, bias=att_st[:, g, b:b + 1], scale=-1.0,
                                           accum_out=att_st[:, g, 2 + b:3 + b])
                    c.then_inc(s_sexp, 1)
                    if g == 0:
                        for b in range(2):
                            act.wait_ge(s_kst[b], 16 * ((NTILE + 1 - b) // 2))
                    for b in range(3):
                        nb = 4 if b < 2 else 1
                        rows = P if b < 2 else TS
                        act.wait_ge(s_spx, 3 * g + b + 1)
                        if b == 0 and g:
                            act.wait_ge(s_hpv, 4 * g)
                        act.activation(pTs_v[0:rows, 4 * b:4 * b + nb].rearrange("p c q -> p (c q)"),
                                       ps[0:rows, 6 + b % 2, 0:nb * P], ACT.Copy).then_inc(s_spT, 1)
                    head_norm(TS, 0)

            def probs_out(k):
                w = P * (k % 4 + 1)
                act.wait_ge(s_px, k + 1)
                if k >= 2:
                    act.wait_ge(s_pvq, k - 1)
                act.activation(pT[:, k % 2, 0:w], ps[:, k % 2, 0:w], ACT.Copy).then_inc(s_pT, 1)

            take_apart(0)
            take_apart(1)
            for u, d in enumerate(units):
                if d["eng"] == "A":
                    if u == first_qb or (u == first_qb + 1):
                        act.wait_ge(s_Sst, 32)
                    act.wait_ge(s_unit, u + 1)
                    kind, a, b, bank = d["kind"], d["a"], d["b"], bank_of[u]
                    if d["token_major"]:
                        dst, src = rows_of({"va": va, "ra": ra, "vb": vb}[kind], d, bank)
                        act.activation(dst, src, ACT.Silu if kind == "ra" else ACT.Copy).then_inc(s_ev["A"], 1)
                    else:
                        f = WC // P * d["nth"] + a
                        cols = slice(HALF * b, HALF * b + HALF)
                        dst = {"qa": fmA[:, f % 8, cols], "ka": fmA[:, (GH + f) % 8, cols], "ga": mixT[:, f, cols], "qb": qbT[:, f, cols],
                               "kb": kbT[:, f, cols], "gb": sgb[:, f, cols]}[kind]
                        if kind in ("ga", "gb"):
                            act.activation(dst, ps[:, bank, 0:HALF], ACT.Sigmoid).then_inc(s_ev["A"], 1)
                        elif kind == "qb":
                            act.activation(dst, ps[:, bank, 0:HALF], ACT.Copy, scale=-DQ ** -0.5).then_inc(s_ev["A"], 1)
                        else:
                            act.activation(dst, ps[:, bank, 0:HALF], ACT.Copy).then_inc(s_ev["A"], 1)
                if d["last"] and d["tile"] + RING in split_at:
                    take_apart(d["tile"] + RING)
                for what in hooks.get(u, []):
                    do(*what)
            act.wait_ge(s_gd, 1)
            act.activation(rt[:, 0, 0:NTILE * NG], rt[:, 0, 0:NTILE * NG], ACT.Exp).then_inc(s_ge, 1)
            act.wait_ge(s_ed, 1)
            act.activation(rs[:, 8], rs[:, 8], ACT.Exp).then_inc(s_ee, 1)

            def x_out(e, slot):
                act.wait_ge(s_xt, e + 1)
                act.activation(xgT[:, slot, 0:4].rearrange("p c t -> p (c t)"), ps[:, 4], ACT.Copy).then_inc(s_xtA, 1)

            def silu(e):
                act.wait_ge(s_gu, e + 1)
                act.activation(sg[:], ps[:, 0], ACT.Silu).then_inc(s_sg, 1)

            def h_out(e):
                act.wait_ge(s_at, e + 1)
                act.activation(hhT[:].rearrange("p c t -> p (c t)"), ps[:, 2], ACT.Copy).then_inc(s_hhT, 1)

            def y_out(e, slot):
                act.wait_ge(s_dn, e + 1)
                act.activation(yo[:, slot, 0:512], ps[:, 6], ACT.Copy).then_inc(s_yA, 1)
                act.wait_ge(s_yA, e + 1)
                act.wait_ge(s_yD, e + 1)

            act.wait_ge(s_slot, 1)
            x_out(0, 0)
            silu(0)
            x_out(1, 1)

            def y_of(e):
                return y_rows[bass.ds(e * CAP, CAP)]

            def body(e, odd, last=False):
                act.wait_ge(s_hh, e)
                silu(e)
                after(act, s_dn, e - 1)
                h_out(e - 1)
                if not last:
                    act.wait_ge(s_gu, e)
                    x_out(e + 1, 1 - odd)
                after(act, s_yst[1 - odd], store_count(e - 1, 1 - odd))
                y_out(e - 1, 1 - odd)
                act.dma_start(y_of(e - 1), yo[:, 1 - odd]).then_inc(s_yst[1 - odd], 16)

            def store_count(e, slot):
                return (e - slot) * 8

            body(1, 1)
            body(2, 0)
            with act.Fori(1, NE // 2 - 1) as it:
                body(it * 2 + 1, 1)
                body(it * 2 + 2, 0)
            body(NE - 1, 1, last=True)
            act.wait_ge(s_dn, NE - 1)
            h_out(NE - 1)
            act.wait_ge(s_yst[1], store_count(NE - 1, 1))
            y_out(NE - 1, 1)
            act.dma_start(y_of(NE - 1), yo[:, 1]).then_inc(s_yst[1], 16)
            act.wait_ge(s_zero, 16 * NOVF)
            n_ovf = act.value_load(ovi[0:1, 0:1], min_val=0, max_val=NOVF)
            for i in range(NOVF):
                with act.If(n_ovf > i):
                    e = NE + i
                    x_out(e, 0)
                    silu(e)
                    h_out(e)
                    act.wait_ge(s_yst[0], 16 * (NE // 2 + i))
                    y_out(e, 0)
                    act.dma_start(y_rows[CAP * e:CAP * (e + 1)], yo[:, 0]).then_inc(s_yst[0], 16)
                    act.wait_ge(s_yst[0], 16 * (NE // 2 + i + 1))
            act.activation(stat[:, 60:61], eps[:], ACT.Copy).then_inc(s_exdone, 1)
            for i, (t0, n) in enumerate(TILES):
                act.wait_ge(s_f, 2 * (i + 1))
                step(act.activation(sqf[0:n], x2[0:n, i], ACT.Square, accum_out=stat[0:n, 50 + i:51 + i]))
                act.activation(stat[0:n, 55 + i:56 + i], stat[0:n, 50 + i:51 + i], ACT.Sqrt, bias=eps[0:n], scale=1.0 / D).then_inc(s_fsq, 1)

        @block.tensor
        def _(pe):
            def transposes(ident_n, outs, done):
                for out, src in outs:
                    last = pe.transpose(out, src, ident[0:ident_n, 0:ident_n])
                last.then_inc(done, 1)

            pe.wait_ge(s_const, 1)
            for i, (t0, n) in enumerate(TILES):
                pe.wait_ge(s_h, i + 1)
                if i >= 2:
                    pe.wait_ge(s_hT, i - 1)
                b = 4 + 2 * (i % 2)
                transposes(n, [(ps[:, b + c // 4, P * (c % 4):P * (c % 4) + n], x0[0:n, i, P * c:P * c + P]) for c in range(KC)], s_hx)
            pe.wait_ge(s_hT, NTILE)

            def three_products(out, left, right, first, final):
                pe.matmul(out, left[0], right[0], start=first, stop=False)
                pe.matmul(out, left[0], right[1], start=False, stop=False)
                return pe.matmul(out, left[1], right[0], start=False, stop=final)

            def do(what, i=0):
                n = TILES[i][1] if i < NTILE else 0
                t0 = TILES[i][0] if i < NTILE else 0
                if what == "code":
                    pe.wait_ge(s_wc, 1)
                    for b in range(2):
                        cols = slice(HALF * b, HALF * b + HALF)
                        for c in range(KC):
                            last = three_products(ps[:, 4 + b, 0:HALF], (wc_hi[:, c], wc_lo[:, c]),
                                                  (h_hi[:, c, cols], h_lo[:, c, cols]), c == 0, c == KC - 1)
                    last.then_inc(s_code_mm, 1)
                elif what == "dec" and i < GH:
                    pe.wait_ge(s_code, 1)
                    if i >= 2:
                        pe.wait_ge(s_dec_rd, i - 1)
                        pe.wait_ge(s_ln, i - 1)
                    for b in range(2):
                        last = pe.matmul(ps[:, 4 + 2 * (i % 2) + b, 0:HALF], w_dec[:, P * i:P * i + P], code[:, HALF * b:HALF * b + HALF],
                                         start=True, stop=True)
                    last.then_inc(s_dec_mm, 1)
                elif what == "kend":
                    pe.wait_ge(s_qk, GH)
                    if i >= 4:
                        pe.wait_ge(s_ke, i - 3)
                    transposes(P, [(ps[0:n, 4 + i % 4, P * h:P * h + P], t2[:, h, t0:t0 + n]) for h in range(GH)], s_ke_mm)
                elif what == "gla":
                    gla_tile(i, t0, n)
                elif what == "kout":
                    b = 3 + 2 * (i % 2)
                    for u in units_of["kb"][-2:]:
                        emptied(pe, u)
                    if i >= 2:
                        pe.wait_ge(s_krow, 2 * (i - 1))
                    transposes(P, [(ps[0:n, b + h // 4, P * (h % 4):P * (h % 4) + P], kbT[:, h, t0:t0 + n]) for h in range(DH)], s_kx)
                elif what == "attn":
                    attention()
                elif what == "router":
                    pe.wait_ge(s_h2, i + 1)
                    if i:
                        pe.wait_ge(s_h2T, i)
                    transposes(n, [(ps[:, 3 + c // 4, P * (c % 4):P * (c % 4) + n], h2[0:n, i % 2, P * c:P * c + P]) for c in range(KC)], s_h2x)
                    pe.wait_ge(s_h2T, i + 1)
                    if i:
                        pe.wait_ge(s_lg, i)
                    for c in range(KC):
                        last = pe.matmul(ps[0:n, 5, 0:NG + NE], h2T[:, c, 0:n], wr[:, c], start=c == 0, stop=c == KC - 1)
                    last.then_inc(s_lgm, 1)

            def gla_tile(i, t0, n):
                chunks = [2 * i, 2 * i + 1] if i < NTILE - 1 else [NCH - 1]
                m = CHUNK if i < NTILE - 1 else TS
                pe.wait_ge(s_ke, NTILE)
                for u in units_of["va"][-2:]:
                    emptied(pe, u)
                if i:
                    pe.wait_ge(s_oaT, i)
                for c in chunks:
                    p0, tc = CHUNK * (c % 2) if i < NTILE - 1 else 0, CHUNK * c
                    rows = slice(p0, p0 + m)
                    if c >= 2:
                        pe.wait_ge(s_att, c - 1)
                    for h in range(GH):
                        last = pe.matmul(ps[rows, 4, CHUNK * h:CHUNK * h + m], fmA[:, GH + h, tc:tc + m], fmA[:, h, tc:tc + m],
                                         start=True, stop=True)
                    last.then_inc(s_att_mm, 1)
                    if c:
                        pe.wait_ge(s_S, c)
                    for h in range(GH):
                        last = pe.matmul(ps[:, 3 + 4 * (h // 2), DV * (h % 2):DV * (h % 2) + DV], kend[rows, i, h], va[rows, i, DV * h:DV * h + DV],
                                         start=True, stop=True)
                    last.then_inc(s_dS, 1)
                    if c == NCH - 1:
                        pe.wait_ge(s_sin, 16)
                    pe.wait_ge(s_att, c + 1)
                    for h in range(GH):
                        out = ps[rows, 5 + h // 2, DV * (h % 2):DV * (h % 2) + DV]
                        if c:
                            state = S_in[:, h] if c == NCH - 1 else S[:, c % 2, h]
                            pe.matmul(out, fmA[:, h, tc:tc + m], state, start=True, stop=False)
                        last = pe.matmul(out, att[rows, h, 0:m], va[rows, i, DV * h:DV * h + DV], start=c == 0, stop=True)
                    last.then_inc(s_o, 1)
                pe.wait_ge(s_og, i + 1)
                transposes(n, [(ps[:, 5 + c // 4, P * (c % 4):P * (c % 4) + n], ra[0:n, i, P * c:P * c + P]) for c in range(8)], s_ox)

            def attention():
                for u in units_of["qb"][-2:] + units_of["vb"][-2:]:
                    emptied(pe, u)
                emptied(pe, units_of["gb"][-1])
                pe.wait_ge(s_krow, 2 * NTILE)

                def scores(k):
                    h, q = k // 4, k % 4
                    w, b = P * (q + 1), 3 + 2 * (k % 2)
                    if k >= 2:
                        pe.wait_ge(s_tt, 2 * (k - 1))
                    for a in range(2):
                        r = slice(DQ * a, DQ * a + DQ)
                        last = pe.matmul(ps[:, b + a, 0:w], qbT[r, h, P * q:P * q + P], kbT[r, h, 0:w], start=True, stop=True)
                    last.then_inc(s_scm, 1)

                def probs_t(k):
                    pe.wait_ge(s_pr, k + 1)
                    if k >= 2:
                        pe.wait_ge(s_pT, k - 1)
                    transposes(P, [(ps[:, k % 2, P * c:P * c + P], sc[:, k % 2, 0, P * c:P * c + P]) for c in range(k % 4 + 1)], s_px)

                def values(k):
                    h, q = k // 4, k % 4
                    bank = 2 + 5 * (h % 2)
                    pe.wait_ge(s_pT, k + 1)
                    if q == 0 and h >= 2:
                        pe.wait_ge(s_obT, h - 1)
                    for c in range(q + 1):
                        last = pe.matmul(ps[:, bank, DVB * q:DVB * q + DVB], pT[:, k % 2, P * c:P * c + P], vb[:, c, DVB * h:DVB * h + DVB],
                                         start=c == 0, stop=c == q)
                    last.then_inc(s_pvq, 1)

                def out_t(h):
                    pe.wait_ge(s_bo, h + 1)
                    bank = 2 + 5 * (h % 2)
                    transposes(P, [(ps[:, bank, P * q:P * q + P], ob[:, P * q:P * q + P]) for q in range(4)], s_bx)

                NK = 4 * DH
                scores(0)
                scores(1)
                for k in range(NK):
                    probs_t(k)
                    if k + 2 < NK:
                        scores(k + 2)
                    values(k)
                    if k % 4 == 2 and k >= 6:
                        out_t(k // 4 - 1)
                out_t(DH - 1)
                pe.wait_ge(s_obT, DH)
                pe.wait_ge(s_pT, NK)
                for g in range(2):
                    for j in range(4):
                        h = 4 * g + j
                        pe.wait_ge(s_kc[h % 2], 16 * (h // 2 + 1))
                        for b in range(2):
                            if h:
                                pe.wait_ge(s_kcT, 2 * h - 1 + b)
                            if j == 0 and g:
                                pe.wait_ge(s_spT, 3 * g)
                            transposes(P, [(ps[:, 6 + b, P * c:P * c + P], kraw[:, h % 2, 4 * b + c]) for c in range(4)], s_kcx)
                        pe.wait_ge(s_kcT, 2 * h + 2)
                        if j == 0 and g:
                            pe.wait_ge(s_obT, DH + g)
                        rows = slice(32 * j, 32 * j + 32)
                        for a in range(2):
                            r = slice(DQ * a, DQ * a + DQ)
                            for b in range(2):
                                pe.matmul(ps[rows, 3 * a + b], qbT[r, h, TP:NT], kcT[r, h % 2, 512 * b:512 * b + 512], start=True, stop=True)
                            last = pe.matmul(ps[rows, 3 * a + 2, 0:TS], qbT[r, h, TP:NT], kbT[r, h, TP:NT], start=True, stop=True)
                        last.then_inc(s_ssc, 1)
                    pe.wait_ge(s_spr, g + 1)
                    for b in range(3):
                        if b == 2:
                            pe.wait_ge(s_spT, 3 * g + 1)
                        if b == 0:
                            pe.wait_ge(s_kcT, 8 * (g + 1))
                        if b < 2:
                            transposes(P, [(ps[:, 6 + b, P * c:P * c + P], scs[:, 0, 512 * b + P * c:512 * b + P * c + P]) for c in range(4)], s_spx)
                        else:
                            transposes(P, [(ps[0:TS, 6, 0:P], scs[:, 0, PAST:PAST + TS])], s_spx)
                    pe.wait_ge(s_spT, 3 * g + 3)
                    for j in range(4):
                        h = 4 * g + j
                        pe.wait_ge(s_vc[h % VBUF], 16 * (h // VBUF + 1))
                        for c in range(PAST // P + 1):
                            kk = P if c < PAST // P else TS
                            rhs = vc[:, h % VBUF, c] if c < PAST // P else vb[0:TS, 4, DVB * h:DVB * h + DVB]
                            last = pe.matmul(ps[0:TS, 0, DVB * j:DVB * j + DVB], pTs_v[0:kk, c, 32 * j:32 * j + 32], rhs,
                                             start=c == 0, stop=c == PAST // P)
                        last.then_inc(s_hpv, 1)
                    pe.wait_ge(s_bo, DH + g + 1)
                    transposes(TS, [(ps[:, 0, TS * j:TS * j + TS], ob[0:TS, P * j:P * j + P]) for j in range(4)], s_bx)

            for u, d in enumerate(units):
                n, kind, a, b, bank = d["tile"], d["kind"], d["a"], d["b"], bank_of[u]
                if d["first"]:
                    if n in split_at:
                        pe.wait_ge(s_lo, split_at[n] + 1)
                    else:
                        pe.wait_ge(s_w[n % RING], 16 * (n // RING + 1))
                    if kind == "pa":
                        pe.wait_ge(s_oaT, NTILE)
                    if kind == "pb":
                        pe.wait_ge(s_obT, DH + 2)
                    if kind == "wo" and d["nth"] == 0:
                        emptied(pe, units_of["pb"][-1])
                if u >= 3:
                    emptied(pe, u - 3)
                if n in split_at:
                    w = [part[:, split_at[n] % 2].rearrange("p (c n) -> p c n", c=KC) for part in (w_hi, w_lo)]
                else:
                    w = tile_ring(n).rearrange("p (c n) -> p c n", c=KC)
                    act_in = {"pa": fmA, "pb": obT, "wo": mixT}[kind]
                if d["token_major"]:
                    for k, (t0, m) in enumerate(TILES[a:a + 2]):
                        if n in split_at:
                            t0, m = t0 + m - P, P
                        out = ps[0:m, bank, WC * k:WC * k + WC]
                        for c in range(KC):
                            if n in split_at:
                                last = three_products(out, (h_hi[:, c, t0:t0 + m], h_lo[:, c, t0:t0 + m]), (w[0][:, c], w[1][:, c]),
                                                      c == 0, c == KC - 1)
                            else:
                                last = pe.matmul(out, act_in[:, c, t0:t0 + m], w[:, c], start=c == 0, stop=c == KC - 1)
                else:
                    feats, cols = slice(P * a, P * a + P), slice(HALF * b, HALF * b + HALF)
                    for c in range(KC):
                        if n in split_at:
                            last = three_products(ps[:, bank, 0:HALF], (w[0][:, c, feats], w[1][:, c, feats]),
                                                  (h_hi[:, c, cols], h_lo[:, c, cols]), c == 0, c == KC - 1)
                        else:
                            last = pe.matmul(ps[:, bank, 0:HALF], w[:, c, feats], act_in[:, c, cols], start=c == 0, stop=c == KC - 1)
                last.then_inc(s_unit, 1)
                for what in hooks.get(u, []):
                    do(*what)
            pe.wait_ge(s_A, 1)
            A = rt[:, 9].rearrange("p (i e) -> p i e", e=NE)
            for i, (t0, n) in enumerate(TILES):
                for j in range(i + 1):
                    k = TILES[j][1]
                    pe.matmul(ps[:, 0, NE * i:NE * i + NE], (upper if j == i else ones)[0:k, :], A[0:k, j], start=j == 0, stop=j == i)
            for j in range(NTILE):
                k = TILES[j][1]
                last = pe.matmul(ps[:, 0, NE * NTILE:NE * NTILE + NE], ones[0:k, :], A[0:k, j], start=j == 0, stop=j == NTILE - 1)
            last.then_inc(s_rank, 1)
            for i, (t0, n) in enumerate(TILES):
                pe.wait_ge(s_oh, i + 1)
                for j in range(NBLK):
                    last = pe.matmul(ps[:, 1, j:j + 1], onehot[0:n, i % 2, j], tok_id[0:n, i:i + 1], start=i == 0 and j == 0,
                                     stop=i == NTILE - 1, skip_group_check=True)
                last.then_inc(s_tok, 1)

            def XT(e, slot, count):
                pe.wait_ge(s_xg[slot], count)
                transposes(P, [(ps[:, 4 + c // 4, P * (c % 4):P * (c % 4) + P], xg[:, slot, P * c:P * c + P]) for c in range(KC)], s_xt)

            def GU(e, slot, count):
                pe.wait_ge(s_xtA, e + 1)
                pe.wait_ge(s_xtD, e + 1)
                for w, s, bank in ((wg, s_wg, 0), (wu, s_wu, 1)):
                    pe.wait_ge(s[slot], count)
                    for c in range(KC):
                        last = pe.matmul(ps[:, bank], xgT[:, slot, c], w[:, slot, c], start=c == 0, stop=c == KC - 1)
                last.then_inc(s_gu, 1)

            def AT(e, slot):
                pe.wait_ge(s_hh, e + 1)
                transposes(P, [(ps[:, 2, P * c:P * c + P], hh[:, slot, P * c:P * c + P]) for c in range(FE // P)], s_at)

            def Dn(e, slot, count):
                pe.wait_ge(s_hhT, e + 1)
                pe.wait_ge(s_wd[slot], count)
                for b in range(2):
                    for c in range(FE // P):
                        last = pe.matmul(ps[:, 6 + b], hhT[:, c], wd[:, slot, c, 512 * b:512 * b + 512], start=c == 0, stop=c == FE // P - 1)
                last.then_inc(s_dn, 1)

            def count(e, slot):
                return (e - slot) * 8 + 16

            pe.wait_ge(s_slot, 1)
            XT(0, 0, 16)
            GU(0, 0, 16)
            XT(1, 1, 16)

            def body(e, odd, last=False):
                pe.wait_ge(s_hh, e)
                GU(e, odd, count(e, odd))
                AT(e - 1, 1 - odd)
                if not last:
                    XT(e + 1, 1 - odd, count(e + 1, 1 - odd))
                after(pe, s_yA, e - 1)
                after(pe, s_yD, e - 1)
                Dn(e - 1, 1 - odd, count(e - 1, 1 - odd))

            body(1, 1)
            body(2, 0)
            with pe.Fori(1, NE // 2 - 1) as it:
                body(it * 2 + 1, 1)
                body(it * 2 + 2, 0)
            body(NE - 1, 1, last=True)
            AT(NE - 1, 1)
            pe.wait_ge(s_yA, NE - 1)
            pe.wait_ge(s_yD, NE - 1)
            Dn(NE - 1, 1, count(NE - 1, 1))
            n_ovf = pe.value_load(ovi[0:1, 0:1], min_val=0, max_val=NOVF)
            for i in range(NOVF):
                with pe.If(n_ovf > i):
                    e, c = NE + i, 16 * (NE // 2 + i + 1)
                    pe.wait_ge(s_yA, e)
                    pe.wait_ge(s_yD, e)
                    XT(e, 0, c)
                    GU(e, 0, c)
                    AT(e, 0)
                    Dn(e, 0, c)

        @block.vector
        def _(dve):
            steps = [0]

            def step(ins):
                steps[0] += 1
                ins.then_inc(s_dve, 1)
                dve.wait_ge(s_dve, steps[0])

            dve.memset(att[:], 0.0).then_inc(s_mz, 1)
            dve.wait_ge(s_small, 16 * 11)
            step(dve.tensor_tensor_reduce(lamt[:, 0], lamt[:, 0], lamt[:, 1], 1.0, 0.0, ALU.mult, ALU.add, lam[:, 0:1]))
            dve.tensor_tensor_reduce(lamt[:, 2], lamt[:, 2], lamt[:, 3], 1.0, 0.0, ALU.mult, ALU.add, lam[:, 1:2]).then_inc(s_lamp, 1)
            step(dve.tensor_scalar(g_diff_s, g_diff, 1.0 - LAM_INIT, None, ALU.mult))
            for i, (t0, n) in enumerate(TILES):
                dve.wait_ge(s_xsq, i + 1)
                step(dve.reciprocal(stat[0:n, 8 + i:9 + i], stat[0:n, 8 + i:9 + i]))
                dve.tensor_scalar(x0[0:n, i], x0[0:n, i], stat[0:n, 8 + i:9 + i], None, ALU.mult).then_inc(s_h, 1)
                dve.wait_ge(s_hx, i + 1)
                b = 4 + 2 * (i % 2)
                src = ps[:, b:b + 2].rearrange("p b (c t) -> p (b c) t", t=P)[:, :, 0:n]
                step(dve.tensor_tensor(h_hi[:, :, t0:t0 + n], src, rep(g_mix, 2, n), ALU.mult))
                for c in range(KC):
                    last = dve.scalar_tensor_tensor(h_lo[:, c, t0:t0 + n], src[:, c], g_mix[:, c:c + 1],
                                                    h_hi[:, c, t0:t0 + n].bitcast(F32), ALU.mult, ALU.subtract)
                last.then_inc(s_hT, 1)
            dve.wait_ge(s_lame, 1)
            step(dve.tensor_tensor(lam[:, 4:5], lam[:, 3:4], lam[:, 2:3], ALU.subtract))
            step(dve.tensor_scalar(lam[:, 4:5], lam[:, 4:5], LAM_INIT, None, ALU.subtract))
            dve.wait_ge(s_wc_hi, 1)
            dve.tensor_tensor(wc_lo[:, :, 0:RANK], w_code[:], wc_hi[:, :, 0:RANK].bitcast(F32), ALU.subtract).then_inc(s_wc, 1)
            dve.wait_ge(s_hT, NTILE)
            dve.wait_ge(s_const, 2)

            def take_apart(n):
                k = split_at[n]
                dve.wait_ge(s_hi, k + 1)
                dve.tensor_tensor(w_lo[:, k % 2], tile_ring(n), w_hi[:, k % 2].bitcast(F32), ALU.subtract).then_inc(s_lo, 1)

            def do(what, i=0):
                n = TILES[i][1] if i < NTILE else 0
                t0 = TILES[i][0] if i < NTILE else 0
                if what == "dec":
                    if i < GH:
                        dve.wait_ge(s_abs, i + 1)
                        src = ps[:, 4 + 2 * (i % 2):6 + 2 * (i % 2), 0:HALF]
                        dve.tensor_scalar(bT[:, i].rearrange("p (b t) -> p b t", b=2), src, b_dec[:, i:i + 1], 0.0, ALU.add, ALU.min).then_inc(s_dec_rd, 1)
                    if 1 <= i <= GH:
                        f = i - 1
                        dve.wait_ge(s_ln, f + 1)
                        dve.wait_ge(s_dec_rd, f + 1)
                        step(dve.tensor_tensor(t1[:, f], bT[:, f], t1[:, f], ALU.subtract))
                        step(dve.tensor_tensor_scan(bT[:, f], keep[:], t1[:, f], 0.0, ALU.mult, ALU.add))
                        bv = bT[:, f, 0:TP].rearrange("p (c t) -> p c t", t=CHUNK)
                        step(dve.tensor_tensor(t2[:, f, 0:TP].rearrange("p (c t) -> p c t", t=CHUNK),
                                               rep(bv[:, :, CHUNK - 1], 2, CHUNK), bv, ALU.subtract))
                        dve.tensor_scalar(t2[:, f, TP:NT], bT[:, f, TP:NT], bT[:, f, NT - 1:NT], -1.0, ALU.subtract, ALU.mult).then_inc(s_delta, 1)
                    if i >= 2:
                        f = i - 2
                        if f == 0:
                            for u in units_of["ka"][-2:] + units_of["qa"][-2:]:
                                emptied(dve, u)
                        dve.wait_ge(s_exps, f + 1)
                        step(dve.tensor_tensor(t2[:, f], t2[:, f], fmA[:, GH + f], ALU.mult))
                        step(dve.tensor_tensor(fmA[:, GH + f], fmA[:, GH + f], t3[:, f], ALU.mult))
                        dve.scalar_tensor_tensor(fmA[:, f], fmA[:, f], DK ** -0.5, t1[:, f], ALU.mult, ALU.mult).then_inc(s_qk, 1)
                elif what == "gla":
                    chunks = [2 * i, 2 * i + 1] if i < NTILE - 1 else [NCH - 1]
                    m = CHUNK if i < NTILE - 1 else TS
                    for c in chunks:
                        p0 = CHUNK * (c % 2) if i < NTILE - 1 else 0
                        rows = slice(p0, p0 + m)
                        dve.wait_ge(s_att_mm, c + 1)
                        dve.wait_ge(s_mz, 1)
                        dve.wait_ge(s_zero, 16 * NOVF)
                        if c >= 2:
                            dve.wait_ge(s_o, c - 1)
                        dve.copy_predicated(att[rows, :, 0:m], rep(trimask[rows, 0:m], 1, GH),
                                            ps[rows, 4, 0:GH * CHUNK].rearrange("p (h t) -> p h t", h=GH)[:, :, 0:m]).then_inc(s_att, 1)
                        dve.wait_ge(s_dS, c + 1)
                        if c:
                            dve.wait_ge(s_o, c)
                            dve.wait_ge(s_S, c)
                        if c == NCH - 1:
                            dve.wait_ge(s_sin, 16)
                        for h in range(GH):
                            dS = ps[:, 3 + 4 * (h // 2), DV * (h % 2):DV * (h % 2) + DV]
                            if c == 0:
                                last = dve.tensor_copy(S[:, 1, h], dS)
                            else:
                                last = dve.scalar_tensor_tensor(S[:, (c + 1) % 2, h], S_in[:, h] if c == NCH - 1 else S[:, c % 2, h],
                                                                ebl[:, h, c:c + 1], dS, ALU.mult, ALU.add)
                        last.then_inc(s_S, 1)
                    dve.wait_ge(s_osq, i + 1)
                    step(dve.reciprocal(stat[0:n, 32:36], stat[0:n, 20:24]))
                    if i == 0:
                        emptied(dve, units_of["ra"][-1])
                    for h in range(GH):
                        last = dve.scalar_tensor_tensor(ra[0:n, i, DV * h:DV * h + DV], ps[0:n, 5 + h // 2, DV * (h % 2):DV * (h % 2) + DV],
                                                        stat[0:n, 32 + h:33 + h], ra[0:n, i, DV * h:DV * h + DV], ALU.mult, ALU.mult)
                    last.then_inc(s_og, 1)
                    dve.wait_ge(s_ox, i + 1)
                    dve.tensor_tensor(fmA[:, :, t0:t0 + n], ps[:, 5:7].rearrange("p b (c t) -> p (b c) t", t=P)[:, :, 0:n],
                                      rep(g_gla, 2, n), ALU.mult).then_inc(s_oaT, 1)
                elif what == "attn":
                    attention()
                elif what == "h2":
                    dve.wait_ge(s_2sq, i + 1)
                    step(dve.reciprocal(stat[0:n, 45 + i:46 + i], stat[0:n, 45 + i:46 + i]))
                    if i == 0:
                        dve.wait_ge(s_g, 32)
                    if i >= 2:
                        dve.wait_ge(s_h2st[i % 2], 16 * (i // 2))
                        dve.wait_ge(s_h2x, i - 1)
                    dve.scalar_tensor_tensor(h2[0:n, i % 2], x2[0:n, i], stat[0:n, 45 + i:46 + i], gffn[0:n], ALU.mult, ALU.mult).then_inc(s_h2, 1)
                elif what == "router":
                    dve.wait_ge(s_lgm, i + 1)
                    if i == 0:
                        dve.wait_ge(s_c2, 1)
                    dve.tensor_tensor(lg[0:n, i], ps[0:n, 5, 0:NG + NE], br[0:n], ALU.add).then_inc(s_lg, 1)

            def attention():
                dve.wait_ge(s_dist, 1)
                step(dve.scalar_tensor_tensor(dist[:], dist[:], -1.0, dist[:], ALU.mult, ALU.max))
                step(dve.memset(dist[0:CHUNK, TP - CHUNK:TP], BIG))
                dve.scalar_tensor_tensor(dist_s[:], dist_s[:], -1.0, dist_s[:], ALU.mult, ALU.max).then_inc(s_bs, 1)

                def head_norm(n, k, bank):
                    dve.wait_ge(s_sqr, k + 1)
                    dve.tensor_reduce(stat[0:n, 24:28], ob[0:n].rearrange("p (q d) -> p q d", q=4), AX_X, ALU.add).then_inc(s_brs, 1)
                    dve.wait_ge(s_bsq, k + 1)
                    step(dve.reciprocal(stat[0:n, 36:40], stat[0:n, 28:32]))
                    if k:
                        dve.wait_ge(s_bx, k)
                    dve.tensor_tensor(ob[0:n].rearrange("p (q d) -> p q d", q=4), ps[0:n, bank].rearrange("p (q d) -> p q d", q=4),
                                      rep(stat[0:n, 36:40], 2, DVB), ALU.mult).then_inc(s_bo, 1)

                def head_out(k, bank, dst, src):
                    dve.wait_ge(s_bx, k + 1)
                    dve.tensor_scalar(dst, src, g_diff_s, None, ALU.mult).then_inc(s_obT, 1)

                def combine(k):
                    w = P * (k % 4 + 1)
                    st = att_st[:, k % 2]
                    dve.wait_ge(s_exp, k + 1)
                    step(dve.reciprocal(st[:, 4:6], st[:, 2:4]))
                    step(dve.tensor_tensor(st[:, 5:6], st[:, 5:6], lam[:, 4:5], ALU.mult))
                    step(dve.tensor_scalar(sc[:, k % 2, 1, 0:w], sc[:, k % 2, 1, 0:w], st[:, 5:6], None, ALU.mult))
                    dve.scalar_tensor_tensor(sc[:, k % 2, 0, 0:w], sc[:, k % 2, 0, 0:w], st[:, 4:5], sc[:, k % 2, 1, 0:w],
                                             ALU.mult, ALU.add).then_inc(s_pr, 1)

                k = 0
                for h in range(DH):
                    dve.wait_ge(s_bias, h + 1)
                    for q in range(4):
                        w, b = P * (q + 1), 3 + 2 * (k % 2)
                        dve.wait_ge(s_scm, k + 1)
                        if k >= 2:
                            dve.wait_ge(s_px, k - 1)
                        for a in range(2):
                            dve.tensor_tensor_reduce(sc[:, k % 2, a, 0:w], ps[:, b + a, 0:w], bias[:, h % 2, TP - w:TP], 1.0, 3.0e38,
                                                     ALU.add, ALU.min, att_st[:, k % 2, a:a + 1]).then_inc(s_tt, 1)
                        if k:
                            combine(k - 1)
                        if q == 2 and h:
                            head_norm(P, h - 1, 2 + 5 * ((h - 1) % 2))
                        if q == 3 and h:
                            head_out(h - 1, 0, qbT[:, h - 1, 0:TP], ps[:, 2 + 5 * ((h - 1) % 2)])
                        k += 1
                combine(k - 1)
                head_norm(P, DH - 1, 7)
                head_out(DH - 1, 0, qbT[:, DH - 1, 0:TP], ps[:, 7])
                dve.wait_ge(s_bs, 1)
                for g in range(2):
                    step(dve.tensor_scalar(bias_s, dist_s[:], slope[:, g:g + 1], None, ALU.mult))
                    dve.wait_ge(s_ssc, 4 * g + 4)
                    if g:
                        dve.wait_ge(s_spx, 3 * g)
                    for a in range(2):
                        dve.tensor_tensor_reduce(scs[:, a], ps[:, 3 * a:3 * a + 3].rearrange("p b n -> p (b n)")[:, 0:PAST + TS],
                                                 bias_s, 1.0, 3.0e38, ALU.add, ALU.min, att_st[:, g, a:a + 1]).then_inc(s_stt, 1)
                    st = att_st[:, g]
                    dve.wait_ge(s_sexp, g + 1)
                    step(dve.reciprocal(st[:, 4:6], st[:, 2:4]))
                    step(dve.tensor_tensor(st[:, 5:6], st[:, 5:6], lam[:, 4:5], ALU.mult))
                    step(dve.tensor_scalar(scs[:, 1], scs[:, 1], st[:, 5:6], None, ALU.mult))
                    dve.scalar_tensor_tensor(scs[:, 0], scs[:, 0], st[:, 4:5], scs[:, 1], ALU.mult, ALU.add).then_inc(s_spr, 1)
                    head_norm(TS, DH + g, 0)
                    head_out(DH + g, 0, qbT[:, 4 * g:4 * g + 4, TP:NT], ps[:, 0, 0:4 * TS].rearrange("p (j t) -> p j t", j=4))

            take_apart(0)
            take_apart(1)
            for u, d in enumerate(units):
                if d["eng"] == "D":
                    if u == first_qb or (u == first_qb + 1):
                        dve.wait_ge(s_Sst, 32)
                    dve.wait_ge(s_unit, u + 1)
                    kind, a, b, bank = d["kind"], d["a"], d["b"], bank_of[u]
                    if kind == "wo":
                        if d["nth"] == 0:
                            for k in range(a, min(a + 2, NTILE)):
                                dve.wait_ge(s_x2[k], 16)
                        dst, src = rows_of(x2, d, bank)
                        dve.tensor_tensor(dst, src, dst, ALU.add).then_inc(s_ev["D"], 1)
                    elif d["token_major"]:
                        dst, src = rows_of({"va": va, "ra": ra, "vb": vb}[kind], d, bank)
                        dve.tensor_copy(dst, src).then_inc(s_ev["D"], 1)
                    else:
                        f = WC // P * d["nth"] + a
                        cols = slice(HALF * b, HALF * b + HALF)
                        src = ps[:, bank, 0:HALF]
                        if kind == "pa":
                            emptied(dve, u_of("ga", d["nth"], a, b))
                            dve.tensor_tensor(mixT[:, f, cols], src, mixT[:, f, cols], ALU.mult).then_inc(s_ev["D"], 1)
                        elif kind == "pb":
                            emptied(dve, u_of("gb", d["nth"], a, b))
                            step(dve.tensor_tensor(tmpm[:, b], src, sgb[:, f, cols], ALU.mult))
                            dve.tensor_tensor(mixT[:, f, cols], mixT[:, f, cols], tmpm[:, b], ALU.add).then_inc(s_ev["D"], 1)
                        elif kind == "qb":
                            dve.tensor_scalar(qbT[:, f, cols], src, -DQ ** -0.5, None, ALU.mult).then_inc(s_ev["D"], 1)
                        else:
                            dst = {"qa": fmA[:, f % 8, cols], "ka": fmA[:, (GH + f) % 8, cols], "kb": kbT[:, f, cols]}[kind]
                            dve.tensor_copy(dst, src).then_inc(s_ev["D"], 1)
                if d["last"] and d["tile"] + RING in split_at:
                    take_apart(d["tile"] + RING)
                for what in hooks.get(u, []):
                    do(*what)

            def t3d(k, n):
                return rt[:, k, 0:NTILE * n].rearrange("p (i e) -> p i e", e=n)

            dve.wait_ge(s_lg, NTILE)
            gl, el = lg[:, :, 0:NG], lg[:, :, NG:NG + NE]
            step(dve.tensor_reduce(rs[:, 0], gl, AX_X, ALU.max))
            dve.tensor_tensor(t3d(0, NG), gl, rep(rs[:, 0], 2, NG), ALU.subtract).then_inc(s_gd, 1)

            def first_of(values, best, n, equal, cand, low, out):
                step(dve.tensor_tensor(equal, values, rep(best, 2, n), ALU.is_equal))
                step(dve.tensor_scalar(cand, equal, -64.0, None, ALU.mult))
                step(dve.tensor_tensor(cand, cand, rep(iota_e[:, 0:n], 1, NTILE), ALU.add))
                step(dve.tensor_reduce(low, cand, AX_X, ALU.min))
                step(dve.tensor_tensor(out, cand, rep(low, 2, n), ALU.is_equal))

            first_of(gl, rs[:, 0], NG, t3d(1, NG), t3d(2, NG), rs[:, 1], t3d(3, NG))
            step(dve.tensor_scalar(t3d(3, NG), t3d(3, NG), -1.0, BIG, ALU.add, ALU.mult))
            for i in range(NTILE):
                step(dve.tensor_tensor(t3d(4, NE)[:, i].rearrange("p (g e) -> p g e", g=NG), el[:, i].rearrange("p (g e) -> p g e", g=NG),
                                       rep(t3d(3, NG)[:, i], 2, EG), ALU.add))
            step(dve.tensor_reduce(rs[:, 2], t3d(4, NE), AX_X, ALU.max))
            first_of(t3d(4, NE), rs[:, 2], NE, t3d(5, NE), t3d(6, NE), rs[:, 3], t3d(7, NE))
            step(dve.scalar_tensor_tensor(t3d(4, NE), t3d(7, NE), -3.0 * BIG, t3d(4, NE), ALU.mult, ALU.add))
            step(dve.tensor_reduce(rs[:, 4], t3d(4, NE), AX_X, ALU.max))
            first_of(t3d(4, NE), rs[:, 4], NE, t3d(5, NE), t3d(6, NE), rs[:, 5], t3d(8, NE))
            dve.tensor_tensor(t3d(9, NE), t3d(7, NE), t3d(8, NE), ALU.add).then_inc(s_A, 1)
            dve.tensor_tensor(rs[:, 8], rs[:, 4], rs[:, 2], ALU.subtract).then_inc(s_ed, 1)
            dve.wait_ge(s_ge, 1)
            step(dve.tensor_reduce(rs[:, 6], t3d(0, NG), AX_X, ALU.add))
            step(dve.reciprocal(rs[:, 7], rs[:, 6]))
            dve.wait_ge(s_ee, 1)
            step(dve.tensor_scalar(rs[:, 9], rs[:, 8], 1.0, None, ALU.add))
            step(dve.reciprocal(rs[:, 10], rs[:, 9]))
            step(dve.tensor_tensor(rs[:, 11], rs[:, 10], rs[:, 7], ALU.mult))
            step(dve.tensor_tensor(rs[:, 12], rs[:, 11], rs[:, 8], ALU.mult))
            dve.wait_ge(s_rank, 1)
            dve.wait_ge(s_A, 1)
            rank = ps[:, 0, 0:NE * NTILE].rearrange("p (i e) -> p i e", e=NE)
            step(dve.tensor_copy(ov[:, 0], ps[:, 0, NE * NTILE:NE * NTILE + NE]))
            step(dve.scalar_tensor_tensor(t3d(10, NE), rank, 1.0, t3d(9, NE), ALU.add, ALU.mult))
            step(dve.tensor_scalar(rsel[:, :, 0:NE], t3d(10, NE), -1.0, None, ALU.add))
            step(dve.tensor_scalar(ov[:, 2], ov[:, 0], float(CAP), None, ALU.is_gt))
            for k in range(2, MORE + 1):
                step(dve.scalar_tensor_tensor(ov[:, 2], ov[:, 0], float(k * CAP), ov[:, 2], ALU.is_gt, ALU.add))
            step(dve.tensor_tensor_scan(ov[:, 3], ones[:, 0:NE], ov[:, 2], 0.0, ALU.mult, ALU.add))
            step(dve.tensor_tensor(ov[:, 4], ov[:, 3], ov[:, 2], ALU.subtract))
            step(dve.tensor_scalar(ov[:, 1], iota_e[:], float(CAP), None, ALU.mult))
            step(dve.tensor_scalar(ov[:, 6], ov[:, 4], NE - 1.0, float(CAP), ALU.add, ALU.mult))
            step(dve.tensor_tensor(ov[:, 6], ov[:, 6], ov[:, 1], ALU.subtract))
            step(dve.tensor_scalar(t3d(6, NE), rsel[:, :, 0:NE], float(CAP), None, ALU.is_ge))
            step(dve.tensor_tensor(t3d(6, NE), t3d(6, NE), rep(ov[:, 6], 1, NTILE), ALU.mult))
            step(dve.tensor_tensor(t3d(5, NE), rsel[:, :, 0:NE], rep(ov[:, 1], 1, NTILE), ALU.add))
            step(dve.tensor_tensor(t3d(5, NE), t3d(5, NE), t3d(6, NE), ALU.add))
            for k in range(2):
                step(dve.tensor_tensor(t3d(6, NE), t3d(5, NE), t3d(7 + k, NE), ALU.mult))
                step(dve.tensor_reduce(rs[:, 13], t3d(6, NE), AX_X, ALU.add))
                step(dve.tensor_copy(ysl[:, k], rs[:, 13]))
            ith = rep(iota_e[:, 0:NOVF], 2, NE)
            step(dve.tensor_tensor(ovm[:, :, 0], rep(ov[:, 4], 1, NOVF), ith, ALU.is_le))
            step(dve.tensor_tensor(ovm[:, :, 1], rep(ov[:, 3], 1, NOVF), ith, ALU.is_gt))
            step(dve.tensor_tensor(ovm[:, :, 0], ovm[:, :, 0], ovm[:, :, 1], ALU.mult))
            step(dve.tensor_tensor(ovm[:, :, 1], ovm[:, :, 0], rep(iota_e[:], 1, NOVF), ALU.mult))
            step(dve.tensor_reduce(ovb[:, :, 0], ovm[:, :, 1], AX_X, ALU.add))
            step(dve.tensor_tensor(ovm[:, :, 2], ith, rep(ov[:, 4], 1, NOVF), ALU.subtract))
            step(dve.tensor_tensor(ovm[:, :, 2], ovm[:, :, 2], ovm[:, :, 0], ALU.mult))
            step(dve.tensor_reduce(ovb[:, :, 1], ovm[:, :, 2], AX_X, ALU.add))
            step(dve.tensor_scalar(ovb[:, :, 1], ovb[:, :, 1], 1.0, float(CAP), ALU.add, ALU.mult))
            step(dve.tensor_copy(ovi[:, 1:1 + NOVF], ovb[:, :, 0]))
            step(dve.tensor_copy(ovi[:, 0:1], ov[:, 3, NE - 1:NE]))
            for i in range(NTILE):
                big = rt[:, 0:2].rearrange("p a b -> p (a b)")[:, 0:NOVF * NE].rearrange("p (a b) -> p a b", b=NE)
                step(dve.tensor_tensor(big, ovm[:, :, 0], rep(t3d(10, NE)[:, i], 1, NOVF), ALU.mult))
                step(dve.tensor_reduce(rsel[:, i, NE:NBLK], big, AX_X, ALU.add))
                step(dve.tensor_tensor(rsel[:, i, NE:NBLK], rsel[:, i, NE:NBLK], ovb[:, :, 1], ALU.subtract))
                step(dve.tensor_scalar(rsel[:, i, NE:NBLK], rsel[:, i, NE:NBLK], -1.0, None, ALU.add))
                if i >= 2:
                    dve.wait_ge(s_tok, i - 1)
                dve.tensor_tensor(onehot[:, i % 2], rep(iota_s[:], 1, NBLK), rep(rsel[:, i], 2, CAP), ALU.is_equal).then_inc(s_oh, 1)
            dve.wait_ge(s_tok, NTILE)
            dve.tensor_copy(slot_i[:], ps[:, 1, 0:NBLK]).then_inc(s_slot, 1)
            dve.wait_ge(s_slot, 1)

            def x_out(e, slot):
                dve.wait_ge(s_xt, e + 1)
                dve.tensor_copy(xgT[:, slot, 4:8].rearrange("p c t -> p (c t)"), ps[:, 5]).then_inc(s_xtD, 1)

            def gated(e, slot):
                dve.wait_ge(s_sg, e + 1)
                dve.tensor_tensor(hh[:, slot], ps[:, 1], sg[:], ALU.mult).then_inc(s_hh, 1)

            def y_out(e, slot):
                dve.wait_ge(s_dn, e + 1)
                dve.tensor_copy(yo[:, slot, 512:1024], ps[:, 7]).then_inc(s_yD, 1)

            def store_count(e, slot):
                return (e - slot) * 8

            def body(e, odd, last=False):
                after(dve, s_at, e - 1)
                gated(e, odd)
                if not last:
                    x_out(e + 1, 1 - odd)
                after(dve, s_yst[1 - odd], store_count(e - 1, 1 - odd))
                y_out(e - 1, 1 - odd)

            x_out(0, 0)
            gated(0, 0)
            x_out(1, 1)
            body(1, 1)
            body(2, 0)
            with dve.Fori(1, NE // 2 - 1) as it:
                body(it * 2 + 1, 1)
                body(it * 2 + 2, 0)
            body(NE - 1, 1, last=True)
            dve.wait_ge(s_yst[1], store_count(NE - 1, 1))
            y_out(NE - 1, 1)
            n_ovf = dve.value_load(ovi[0:1, 0:1], min_val=0, max_val=NOVF)
            for i in range(NOVF):
                with dve.If(n_ovf > i):
                    e = NE + i
                    x_out(e, 0)
                    gated(e, 0)
                    dve.wait_ge(s_yst[0], 16 * (NE // 2 + i))
                    y_out(e, 0)
            for i, (t0, n) in enumerate(TILES):
                dve.wait_ge(s_yg[i % 2], 32 * (i // 2 + 1))
                for k in range(2):
                    dve.scalar_tensor_tensor(x2[0:n, i], yg[0:n, i % 2, k], rs[0:n, 11 + k, i:i + 1], x2[0:n, i], ALU.mult, ALU.add).then_inc(s_f, 1)
                    dve.wait_ge(s_f, 2 * i + k + 1)
                dve.wait_ge(s_fsq, i + 1)
                step(dve.reciprocal(stat[0:n, 55 + i:56 + i], stat[0:n, 55 + i:56 + i]))
                if i >= 2:
                    dve.wait_ge(s_out[i % 2], 16 * (i // 2))
                dve.scalar_tensor_tensor(fo[0:n, i % 2], x2[0:n, i], stat[0:n, 55 + i:56 + i], gfin[0:n], ALU.mult, ALU.mult).then_inc(s_fo, 1)


_INS = ["x_prompt", "x_sample", "cache_k", "cache_v", "state_gla", "norm_mix", "w_in", "w_decay", "b_decay", "gla_norm",
        "w_proj_a", "lambda_q1", "lambda_k1", "lambda_q2", "lambda_k2", "diff_norm", "w_proj_b", "w_out", "norm_ffn",
        "w_router_group", "b_router_group", "w_router_expert", "b_router_expert", "w_gate", "w_up", "w_down", "norm_final"]
_OUTS = [(1, TP, D), (1, TS, D), (1, 1, TP, DH, 2 * DQ), (1, 1, TP, DH, DVB), (1, 1, GH, DK, DV),
         (1, 1, TS, DH, 2 * DQ), (1, 1, TS, DH, DVB), (1, 1, GH, DK, DV)]


def kernel(**inputs):
    import numpy as _np
    import concourse.bacc as _bacc
    from concourse import mybir as _mybir
    from concourse.bass_utils import run_bass_kernel_spmd as _run

    nc = _bacc.Bacc("TRN2", target_bir_lowering=False, num_devices=1)
    arrays, args = {}, []
    for name in _INS:
        a = _np.ascontiguousarray(inputs[name])
        arrays[f"in_{name}_dram"] = a
        args.append(nc.dram_tensor(f"in_{name}_dram", a.shape, _mybir.dt.from_np(a.dtype), kind="ExternalInput").ap())
    for i, shape in enumerate(_OUTS):
        args.append(nc.dram_tensor(f"out_{i}_dram", shape, F32, kind="ExternalOutput").ap())
    build(nc, *args)
    r = _run(nc, [arrays], core_ids=[0])
    return tuple(r.results[0][f"out_{i}_dram"] for i in range(len(_OUTS)))
```

```python
from contextlib import ExitStack

import concourse.bass as bass
from concourse import mybir

ALU = mybir.AluOpType
ACT = mybir.ActivationFunctionType
F32 = mybir.dt.float32
F16 = mybir.dt.float16
F32R = mybir.dt.float32r
I32 = mybir.dt.int32
AX_X = mybir.AxisListType.X

P = 128
D = 1024
KC = D // P
TP = 512
TS = 32
NT = TP + TS
TILES = [(i * P, P) for i in range(TP // P)] + [(TP, TS)]
NTILE = len(TILES)
HALF = NT // 2
PAST = 1024
VBUF = 3
EPS = 1e-6
CHUNK = 64
GH, DK, DV = 4, 128, 256
RANK = 16
TAU = 16.0
NCH = TP // CHUNK + 1
DH, DVB = 8, 128
DQ = 64
LAM_INIT = 0.2
NG, EG = 4, 4
NE = NG * EG
FE = 512
CAP = 128
MORE = (NT - 1) // CAP
NOVF = 2 * NT // CAP
NBLK = NE + NOVF
PARTS, PART, PBUF = 6, KC * FE // 2, 3
BIG = 1e30
WC = 256
RING = 2

C_QA, C_KA, C_VA, C_RA, C_CODE = 0, 512, 1024, 2048, 3072
C_QB, C_KB, C_VB, C_GA, C_GB = 3088, 4112, 5136, 6160, 7184


def layout_of_units():
    stages = [("qa", "w_in", C_QA, GH * DK), ("ka", "w_in", C_KA, GH * DK), ("va", "w_in", C_VA, GH * DV),
              ("ra", "w_in", C_RA, GH * DV), ("ga", "w_in", C_GA, D), ("pa", "w_proj_a", 0, D),
              ("qb", "w_in", C_QB, D), ("kb", "w_in", C_KB, D), ("vb", "w_in", C_VB, D), ("gb", "w_in", C_GB, D),
              ("pb", "w_proj_b", 0, D), ("wo", "w_out", 0, D)]
    tiles, kinds, nth = [], [], []
    for kind, name, col, width in stages:
        for n in range(width // WC):
            tiles.append((name, col + n * WC))
            kinds.append(kind)
            nth.append(n)
    units, emptied = [], {"A": 0, "D": 0}
    for n, kind in enumerate(kinds):
        token_major = kind in ("va", "ra", "vb", "wo")
        parts = [(i, 0) for i in range(0, NTILE, 2)] if token_major else [(f, h) for f in range(WC // P) for h in range(2)]
        for m, (a, b) in enumerate(parts):
            if kind in ("ra", "ga", "gb"):
                eng = "A"
            elif kind in ("pa", "pb", "wo"):
                eng = "D"
            else:
                eng = "AD"[len(units) % 2]
            emptied[eng] += 1
            units.append(dict(tile=n, kind=kind, nth=nth[n], a=a, b=b, first=m == 0, last=m == len(parts) - 1,
                              eng=eng, count=emptied[eng], token_major=token_major))
    return tiles, kinds, units


def build(nc, x_prompt, x_sample, cache_k, cache_v, state_gla, norm_mix, w_in, w_decay, b_decay, gla_norm, w_proj_a,
          lambda_q1, lambda_k1, lambda_q2, lambda_k2, diff_norm, w_proj_b, w_out, norm_ffn, w_router_group,
          b_router_group, w_router_expert, b_router_expert, w_gate, w_up, w_down, norm_final,
          y_prompt, y_sample, new_k_p, new_v_p, new_s_p, new_k_s, new_v_s, new_s_s):
    wtiles, wkinds, units = layout_of_units()
    bank_of = [u % 3 for u in range(len(units))]
    stage_units = {}
    for u, d in enumerate(units):
        stage_units.setdefault(d["tile"], []).append(u)
    units_of = {}
    for u, d in enumerate(units):
        units_of.setdefault(d["kind"], []).append(u)

    h2_rows = nc.dram_tensor("h2_rows", (NT, D), F32)
    y_rows = nc.dram_tensor("y_rows", (NBLK * CAP, D), F32)
    h2_rows, y_rows = h2_rows.ap(), y_rows.ap()

    ctx = ExitStack()
    with ctx:
        def sem(name):
            return ctx.enter_context(nc.semaphore(name))

        def sb(name, shape, dt=F32, stack=ctx):
            return stack.enter_context(nc.sbuf_tensor(name, shape, dt))

        ps = ctx.enter_context(nc.psum_tensor("ps", [P, 8, 512], F32))

        ident = sb("ident", [P, P])
        trimask = sb("trimask", [P, CHUNK], I32)
        trif = sb("trif", [P, CHUNK])
        eps = sb("eps", [P, 1])
        ones = sb("ones", [P, P])
        small = sb("small", [P, 64])
        g_mix, g_gla, g_diff, b_dec = small[:, 0:8], small[:, 8:16], small[:, 16:17], small[:, 17:21]
        g_diff_s = small[:, 21:22]
        lamt = sb("lamt", [P, 4, DQ])
        lam = sb("lam", [P, 8])
        stat = sb("stat", [P, 64])
        wr = sb("wr", [P, KC, NG + NE])
        br = sb("br", [P, NG + NE])
        w_code = sb("w_code", [P, KC, RANK])
        w_dec = sb("w_dec", [RANK, GH * DK])

        dense = ExitStack()
        ring = sb("ring", [P, RING, KC * WC], stack=dense)
        w_hi = sb("w_hi", [P, 2, KC * WC], F32R, stack=dense)
        w_lo = sb("w_lo", [P, 2, KC * WC], F32R, stack=dense)

        decay = ExitStack()
        bT = sb("bT", [P, GH, NT], stack=decay)
        t2 = sb("t2", [P, GH, NT], stack=decay)
        t1 = sb("t1", [P, GH, NT], stack=decay)
        t3 = sb("t3", [P, GH, NT], stack=decay)
        decay.close()
        mixT = sb("mixT", [P, KC, NT], stack=dense)

        low = ExitStack()
        S = sb("S", [P, 2, GH, DV], stack=low)
        S_in = sb("S_in", [P, GH, DV], stack=low)
        kend = sb("kend", [P, NTILE, GH, DK], stack=low)
        att = sb("att", [P, GH, CHUNK], stack=low)
        ebl = sb("ebl", [P, GH, NCH], stack=low)
        keep = sb("keep", [P, NT], stack=low)
        code = sb("code", [RANK, NT], stack=low)
        sqa = sb("sqa", [P, DV], stack=low)
        low.close()
        mix = ExitStack()
        m_hi = sb("m_hi", [P, KC, NT], F32R, stack=mix)
        m_lo = sb("m_lo", [P, KC, NT], F32R, stack=mix)
        mix.close()
        qbT = sb("qbT", [P, DH, NT], stack=dense)
        sgb = sb("sgb", [P, KC, NT], stack=dense)

        ht = ExitStack()
        h_hi = sb("h_hi", [P, KC, NT], F32R, stack=ht)
        h_lo = sb("h_lo", [P, KC, NT], F32R, stack=ht)

        gla = ExitStack()
        oa = ExitStack()
        oa_hi = sb("oa_hi", [P, KC, NT], F32R, stack=oa)
        oa_lo = sb("oa_lo", [P, KC, NT], F32R, stack=oa)
        oa.close()
        xa = ExitStack()
        x0 = sb("x0", [P, NTILE, D], stack=xa)
        sq0 = sb("sq0", [P, D], stack=xa)
        xa.close()
        va = sb("va", [P, NTILE, GH * DV], stack=gla)
        ra = sb("ra", [P, NTILE, GH * DV], stack=gla)
        fmA = sb("fmA", [P, 8, NT], stack=gla)
        wc_hi = sb("wc_hi", [P, KC, P], F32R, stack=gla)
        wc_lo = sb("wc_lo", [P, KC, P], F32R, stack=gla)
        gla.close()

        dif = ExitStack()
        kbT = sb("kbT", [P, DH, NT], stack=dif)
        vb = sb("vb", [P, NTILE, DH * DVB], stack=dif)
        kb_rows = sb("kb_rows", [P, 2, D], stack=dif)
        dist = sb("dist", [P, TP], stack=dif)
        bias = sb("bias", [P, 2, TP + TS // 2], stack=dif)
        slope = sb("slope", [P, 2], stack=dif)
        sc = sb("sc", [P, 2, 2, TP + 16], stack=dif)
        pT = sb("pT", [P, 2, TP], stack=dif)
        att_st = sb("att_st", [P, 4, 8], stack=dif)
        head_st = sb("head_st", [P, 3, 4 * DH], stack=dif)
        ob = sb("ob", [P, TP], stack=dif)
        dif.close()
        ht.close()

        smp = ExitStack()
        kraw = sb("kraw", [P, 2, PAST // P, P], stack=smp)
        kcT = sb("kcT", [P, 2, PAST], stack=smp)
        vc = sb("vc", [P, VBUF, PAST // P, P], stack=smp)
        dist_s = sb("dist_s", [P, PAST + TS], stack=smp)
        smp.close()

        o2 = ExitStack()
        ob_hi = sb("ob_hi", [P, KC, NT], F32R, stack=o2)
        ob_lo = sb("ob_lo", [P, KC, NT], F32R, stack=o2)
        tmpm = sb("tmpm", [P, 2, HALF], stack=o2)
        o2.close()
        merge = ExitStack()
        h2 = sb("h2", [P, 2, D], stack=merge)
        h2T = sb("h2T", [P, 2, KC, P], stack=merge)
        sq2 = sb("sq2", [P, D], stack=merge)
        merge.close()
        dense.close()

        ex = ExitStack()
        raw = sb("raw", [P, PARTS, PART], stack=ex)
        e_hi = sb("e_hi", [P, PBUF, PART], F32R, stack=ex)
        e_lo = sb("e_lo", [P, PBUF, PART], F32R, stack=ex)
        xg = sb("xg", [P, 2, D], stack=ex)
        x_hi = sb("x_hi", [P, 2, KC, P], F32R, stack=ex)
        x_lo = sb("x_lo", [P, 2, KC, P], F32R, stack=ex)
        sg = sb("sg", [P, FE], stack=ex)
        hh = sb("hh", [P, 2, FE], stack=ex)
        hh_hi = sb("hh_hi", [P, FE // P, P], F32R, stack=ex)
        hh_lo = sb("hh_lo", [P, FE // P, P], F32R, stack=ex)
        yo = sb("yo", [P, 2, D], stack=ex)
        x2 = sb("x2", [P, NTILE, D], stack=ex)
        gffn = sb("gffn", [P, D], stack=ex)
        gfin = sb("gfin", [P, D], stack=ex)
        lg = sb("lg", [P, NTILE, NG + NE], stack=ex)
        rt = sb("rt", [P, 12, NTILE * NE], stack=ex)
        rs = sb("rs", [P, 16, NTILE], stack=ex)
        iota_e = sb("iota_e", [P, NE], stack=ex)
        chosen = sb("chosen", [P, NTILE + 1, NE], stack=ex)
        ov = sb("ov", [P, 8, NE], stack=ex)
        iota_s = sb("iota_s", [P, CAP], stack=ex)
        tok_id = sb("tok_id", [P, NTILE], stack=ex)
        upper = sb("upper", [P, P], stack=ex)
        blk = sb("blk", [P, 2, NTILE, NBLK], stack=ex)
        iota_b = sb("iota_b", [P, 2, NBLK], stack=ex)
        in_block = sb("in_block", [P, 2, NTILE, NBLK], F16, stack=ex)
        slot_i = sb("slot_i", [P, NBLK], I32, stack=ex)
        ysl = sb("ysl", [P, 2, NTILE], I32, stack=ex)
        ovb = sb("ovb", [P, NOVF], stack=ex)
        ovi = sb("ovi", [P, NOVF + 1], I32, stack=ex)
        ovm = sb("ovm", [P, NOVF, 2, NE], stack=ex)
        at_slot = sb("at_slot", [P, 2, NTILE, CAP], F16, stack=ex)

        ex.close()
        fin = ExitStack()
        yg = sb("yg", [P, NTILE, 2, D], stack=fin)
        fo = sb("fo", [P, NTILE, D], stack=fin)
        sqf = sb("sqf", [P, D], stack=fin)
        fin.close()
        def rep(ap, axis, n):
            a = ap.unsqueeze(axis)
            shape = list(a.shape)
            shape[axis] = n
            return a.broadcast_to(shape)

        def after(eng, s, value):
            if not (isinstance(value, int) and value <= 0):
                eng.wait_ge(s, value)

        kept = [sc[:, 0, :, 0:TP], sc[:, 1, :, 0:TP]] + [kb_rows[:, i].rearrange("p (a n) -> p a n", a=2) for i in range(2)]
        bias_s = bias[:].rearrange("p a n -> p (a n)")
        scs = sc[:].rearrange("p k a n -> p k (a n)")
        pTs_v = kb_rows[:].rearrange("p a n -> p (a n)")[:, 0:(PAST // P + 1) * P].rearrange("p (c q) -> p c q", q=P)

        def u_of(kind, nth, a, b):
            return next(u for u, d in enumerate(units) if (d["kind"], d["nth"], d["a"], d["b"]) == (kind, nth, a, b))

        s_x = [sem(f"s_x{i}") for i in range(NTILE)]
        s_gmix, s_small = sem("s_gmix"), sem("s_small")
        s_wcode = sem("s_wcode")
        s_const = sem("s_const")
        s_pool = sem("s_pool")
        s_dve = sem("s_dve")
        s_act = sem("s_act")
        s_lamp, s_lame = sem("s_lamp"), sem("s_lame")
        s_xsq, s_xrs = sem("s_xsq"), sem("s_xrs")
        s_h = sem("s_h")
        s_hx = sem("s_hx")
        s_hT = sem("s_hT")
        s_w = [sem(f"s_w{i}") for i in range(RING)]
        s_hi, s_lo = sem("s_hi"), sem("s_lo")
        s_wc_hi, s_wc = sem("s_wc_hi"), sem("s_wc")
        s_ohi, s_olo = sem("s_ohi"), sem("s_olo")
        s_sum, s_mhi = sem("s_sum"), sem("s_mhi")
        s_unit = sem("s_unit")
        s_ev = {"A": sem("s_evA"), "D": sem("s_evD")}
        s_code_mm, s_code = sem("s_code_mm"), sem("s_code")
        s_dec_mm, s_dec_rd = sem("s_dec_mm"), sem("s_dec_rd")
        s_abs, s_ln = sem("s_abs"), sem("s_ln")
        s_delta, s_exps = sem("s_delta"), sem("s_exps")
        s_qk = sem("s_qk")
        s_ke_mm, s_ke = sem("s_ke_mm"), sem("s_ke")
        s_sin = sem("s_sin")
        s_att_mm, s_att = sem("s_att_mm"), sem("s_att")
        s_dS, s_S, s_o = sem("s_dS"), sem("s_S"), sem("s_o")
        s_osq, s_og = sem("s_osq"), sem("s_og")
        s_ox, s_oaT = sem("s_ox"), sem("s_oaT")
        s_Sst = sem("s_Sst")
        s_mz = sem("s_mz")
        s_dist, s_dist_s = sem("s_dist"), sem("s_dist_s")
        s_bs = sem("s_bs")
        s_bias = sem("s_bias")
        s_kx, s_krow = sem("s_kx"), sem("s_krow")
        s_kst, s_vst = [sem("s_kst0"), sem("s_kst1")], sem("s_vst")
        s_scm, s_tt, s_exp = sem("s_scm"), sem("s_tt"), sem("s_exp")
        s_pr, s_px, s_pT = sem("s_pr"), sem("s_px"), sem("s_pT")
        s_pvq = sem("s_pvq")
        s_sqr, s_row = sem("s_sqr"), sem("s_row")
        s_brs, s_bsq = sem("s_brs"), sem("s_bsq")
        s_bo, s_bx, s_obT = sem("s_bo"), sem("s_bx"), sem("s_obT")
        s_kc = [sem("s_kc0"), sem("s_kc1")]
        s_vc = [sem(f"s_vc{i}") for i in range(VBUF)]
        s_kcx, s_kcT = sem("s_kcx"), sem("s_kcT")
        s_ssc, s_stt = sem("s_ssc"), sem("s_stt")
        s_sexp, s_spr = sem("s_sexp"), sem("s_spr")
        s_spx, s_spT, s_hpv = sem("s_spx"), sem("s_spT"), sem("s_hpv")
        s_x2 = [sem(f"s_x2_{i}") for i in range(NTILE)]
        s_g = sem("s_g")
        s_c2 = sem("s_c2")
        s_2sq, s_h2 = sem("s_2sq"), sem("s_h2")
        s_h2st = [sem("s_h2st0"), sem("s_h2st1")]
        s_h2x, s_h2T, s_lgm = sem("s_h2x"), sem("s_h2T"), sem("s_lgm")
        s_gd, s_ge = sem("s_gd"), sem("s_ge")
        s_ed, s_ee = sem("s_ed"), sem("s_ee")
        s_A, s_rank = sem("s_A"), sem("s_rank")
        s_oh, s_tok = sem("s_oh"), sem("s_tok")
        s_slot, s_ovi = sem("s_slot"), sem("s_ovi")
        s_raw = [sem(f"s_raw{i}") for i in range(PARTS)]
        s_ehi, s_elo = sem("s_ehi"), sem("s_elo")
        s_part = sem("s_part")
        s_xg = [sem("s_xg0"), sem("s_xg1")]
        s_xt, s_xhi, s_xlo = sem("s_xt"), sem("s_xhi"), sem("s_xlo")
        s_sg, s_hh = sem("s_sg"), sem("s_hh")
        s_at, s_hhi, s_hlo = sem("s_at"), sem("s_hhi"), sem("s_hlo")
        s_y = sem("s_y")
        s_yst = [sem("s_yst0"), sem("s_yst1")]
        s_zero = sem("s_zero")
        s_exdone = sem("s_exdone")
        s_yg = [sem(f"s_yg{i}") for i in range(NTILE)]
        s_f, s_fsq, s_fo = sem("s_f"), sem("s_fsq"), sem("s_fo")
        s_out = [sem("s_out0"), sem("s_out1")]

        hooks = {}

        def hook(u, *what):
            hooks.setdefault(u, []).append(what)

        hook(units_of["ka"][-1], "code")
        for f in range(GH + 2):
            hook(units_of["va"][2 * f], "dec", f)
        for i in range(NTILE):
            hook(units_of["ra"][6 + i], "kend", i)
            hook(units_of["ga"][3 * i - 1] if i else units_of["ra"][-1], "gla", i)
            hook(units_of["ga"][3 * i + 1], "gla_out", i)
            hook(units_of["vb"][2 * i + 1], "kout", i)
        hook(units_of["ga"][-2], "oa")
        hook(units_of["vb"][-1], "dist")
        hook(units_of["gb"][-1], "attn")
        last_wo = [units_of["wo"][-len(TILES[::2]) + i // 2] for i in range(NTILE)]
        for u, steps in zip(sorted(set(last_wo)), (
                (("h2", 0), ("h2", 1)),
                (("turn", 0), ("h2", 2), ("turn", 1), ("logits", 0), ("h2", 3)),
                (("turn", 2), ("logits", 1), ("h2", 4), ("turn", 3), ("logits", 2), ("turn", 4), ("logits", 3), ("logits", 4)))):
            for what, i in steps:
                hook(u, what, i)
        first_qb, last_unit = units_of["qb"][0], len(units) - 1
        last_pa = units_of["pa"][-1]

        def kind_of(u):
            return units[u]["kind"]

        def tile_ring(n):
            return ring[:, n % RING]

        def rows_of(dst, d, bank):
            a, cols = d["a"], slice(WC * d["nth"], WC * d["nth"] + WC)
            if a < NTILE - 1:
                return dst[:, a:a + 2, cols], ps[:, bank].rearrange("p (i n) -> p i n", n=WC)
            return dst[0:TS, a, cols], ps[P - TS:P, bank, 0:WC]

        def part_of(r, j):
            if not isinstance(r, int):
                return r * PARTS + (j - 2), (j + 1) % PBUF, j, r * 16 + (16 if j < 4 else 0)
            seq = j if r == 0 else PARTS * r - 2 + j - (4 if r == NE else 0) if r <= NE else PARTS * (r - 1) + j
            loads = r + (1 if j < 4 else 0) if r <= NE else r
            return seq, seq % PBUF, j, 16 * loads

        def third_after(r, j):
            if isinstance(r, int) and r == 0:
                return part_of(0, 3) if j == 0 else part_of(1, j - 1)
            if j < 3:
                return part_of(r, j + 3)
            if isinstance(r, int) and r == NE - 1:
                return part_of(NE, 4 + j - 3) if j < 5 else None
            return part_of(r + 1, j - 3)

        def emptied(eng, u):
            eng.wait_ge(s_ev[units[u]["eng"]], units[u]["count"])

        block = ctx.enter_context(nc.Block())

        @block.sync
        def _(sp):
            dram = {"w_in": w_in, "w_proj_a": w_proj_a, "w_proj_b": w_proj_b, "w_out": w_out}

            def small_loads():
                with nc.allow_non_contiguous_dma("a few parameter columns"):
                    for h in range(GH):
                        sp.dma_start(g_gla[:, 2 * h:2 * h + 2], gla_norm[0].rearrange("(c p) -> p c", p=P)).then_inc(s_small, 16)
                    sp.dma_start(g_diff, diff_norm[0].rearrange("(c p) -> p c", p=P)).then_inc(s_small, 16)
                    sp.dma_start(b_dec, b_decay[0].rearrange("(c p) -> p c", p=P)).then_inc(s_small, 16)
                    for k, l in enumerate((lambda_q1, lambda_k1, lambda_q2, lambda_k2)):
                        sp.dma_start(lamt[:, k], l.broadcast_to([P, DQ])).then_inc(s_small, 16)
                    sp.dma_start(w_code[:], w_in[0, :, C_CODE:C_CODE + RANK].rearrange("(c p) n -> p c n", p=P)).then_inc(s_wcode, 16)
                    sp.dma_start(w_dec[:], w_decay[0]).then_inc(s_wcode, 16)
                    sp.dma_start(wr[:, :, 0:NG], w_router_group[0].rearrange("(c p) n -> p c n", p=P)).then_inc(s_wcode, 16)
                    sp.dma_start(wr[:, :, NG:NG + NE], w_router_expert[0].rearrange("(c p) n -> p c n", p=P)).then_inc(s_wcode, 16)
                    sp.dma_start(br[:, 0:NG], b_router_group.broadcast_to([P, NG])).then_inc(s_wcode, 16)
                    sp.dma_start(br[:, NG:NG + NE], b_router_expert.broadcast_to([P, NE])).then_inc(s_wcode, 16)

            with nc.allow_non_contiguous_dma("a few parameter columns"):
                sp.dma_start(g_mix, norm_mix[0].rearrange("(c p) -> p c", p=P)).then_inc(s_gmix, 16)
            sp.wait_ge(s_x[2], 16)
            for n, (name, col) in enumerate(wtiles):
                if n == RING:
                    small_loads()
                if n >= RING:
                    sp.wait_ge(s_lo, n - RING + 1)
                src = dram[name][0, :, col:col + WC].rearrange("(c p) n -> p c n", p=P)
                sp.dma_start(ring[:, n % RING, :].rearrange("p (c n) -> p c n", c=KC), src).then_inc(s_w[n % RING], 16)
            sp.wait_ge(s_unit, last_unit + 1)

            def load_part(e, j):
                w, n = ((w_gate, FE), (w_up, FE), (w_down, D))[j // 2]
                c = PART // n
                src = w[0, bass.ds(e, 1)].rearrange("a (c p) n -> p (a c) n", p=P)[:, c * (j % 2):c * (j % 2) + c]
                sp.dma_start(raw[:, j].rearrange("p (c n) -> p c n", c=c), src).then_inc(s_raw[j], 16)

            for j in range(PARTS):
                load_part(0, j)
            for j in range(4):
                sp.wait_ge(s_elo, part_of(0, j)[0] + 1)
                load_part(1, j)
            with sp.Fori(2, NE) as r:
                for j in range(PARTS):
                    before = part_of(r - 1, j)[0]
                    sp.wait_ge(s_elo, before + 1)
                    load_part(r if j < 4 else r - 1, j)
            for j in (4, 5):
                sp.wait_ge(s_elo, part_of(NE - 1, j)[0] + 1)
                load_part(NE - 1, j)
            sp.wait_ge(s_ovi, 1)
            n_ovf = sp.value_load(ovi[0:1, 0:1], min_val=0, max_val=NOVF)
            for i in range(NOVF):
                e = sp.value_load(ovi[0:1, 1 + i:2 + i], min_val=0, max_val=NE - 1)
                with sp.If(n_ovf > i):
                    sp.wait_ge(s_elo, PARTS * (NE + i))
                    for j in range(PARTS):
                        load_part(e, j)
            for i, (t0, n) in enumerate(TILES):
                sp.wait_ge(s_fo, i + 1)
                dst = y_prompt[0, t0:t0 + n] if i < NTILE - 1 else y_sample[0]
                sp.dma_start(dst, fo[0:n, i]).then_inc(s_out[i % 2], 16)
            sp.wait_ge(s_out[0], 48)
            sp.wait_ge(s_out[1], 32)
            for i in range(2):
                sp.wait_ge(s_kst[i], 16 * ((NTILE + 1 - i) // 2))
                sp.wait_ge(s_h2st[i], 16 * ((NTILE + 1 - i) // 2))
            sp.wait_ge(s_vst, 32)
            sp.wait_ge(s_Sst, 32)

        @block.gpsimd
        def _(pool):
            steps = [0]

            def step(ins):
                steps[0] += 1
                ins.then_inc(s_pool, 1)
                pool.wait_ge(s_pool, steps[0])

            step(pool.memset(ident[:], 0.0))
            step(pool.affine_select(out=ident[:], in_=ident[:], compare_op=ALU.not_equal, fill=1.0, base=0,
                                    pattern=[[-1, P]], channel_multiplier=1))
            step(pool.memset(ones[:], 1.0))
            step(pool.memset(wc_hi[:].bitcast(F32), 0.0))
            step(pool.memset(wc_lo[:].bitcast(F32), 0.0))
            step(pool.memset(eps[:], EPS))
            step(pool.memset(trif[:], 1.0))
            for a in range(2):
                t = trif[64 * a:64 * a + 64, :]
                step(pool.affine_select(out=t, in_=t, compare_op=ALU.is_ge, fill=0.0, base=0,
                                        pattern=[[1, CHUNK]], channel_multiplier=-1))
            pool.tensor_copy(trimask[:], trif[:]).then_inc(s_const, 1)
            step(pool.memset(keep[:], 1.0))
            step(pool.memset(keep[:, 0:TP].rearrange("p (c t) -> p c t", t=CHUNK)[:, :, 0:1], 0.0))
            pool.memset(keep[:, TP:TP + 1], 0.0).then_inc(s_const, 1)
            for n in range(2):
                pool.wait_ge(s_hi, n + 1)
                pool.tensor_tensor(w_lo[:, n % 2], tile_ring(n), w_hi[:, n % 2].bitcast(F32), ALU.subtract).then_inc(s_lo, 1)
                pool.wait_ge(s_lo, n + 1)
            pool.wait_ge(s_mz, 1)
            pool.wait_ge(s_hT, NTILE)
            for i in range(NOVF):
                pool.dma_start(y_rows[CAP * (NE + i):CAP * (NE + i + 1)].rearrange("p (a n) -> p a n", n=256),
                               rep(att[:].rearrange("p h t -> p (h t)"), 1, D // 256)).then_inc(s_zero, 16)
            pool.wait_ge(s_ke_mm, NTILE)
            pool.dma_start(S_in[:], state_gla[0, 0].rearrange("h k v -> k h v")).then_inc(s_sin, 16)
            pool.wait_ge(s_S, NCH - 1)
            pool.dma_start(new_s_p[0, 0].rearrange("h k v -> k h v"), S[:, 0]).then_inc(s_Sst, 16)
            pool.wait_ge(s_S, NCH)
            pool.dma_start(new_s_s[0, 0].rearrange("h k v -> k h v"), S[:, 1]).then_inc(s_Sst, 16)
            pool.wait_ge(s_unit, last_pa + 1)
            emptied(pool, last_pa)
            pool.wait_ge(s_Sst, 32)
            step(pool.iota(dist[:], pattern=[[-1, TP]], base=TP - P, channel_multiplier=1,
                           allow_small_or_imprecise_dtypes=True))
            for j in range(4):
                for g in range(2):
                    step(pool.memset(slope[32 * j:32 * j + 32, g:g + 1], 2.0 ** -(4 * g + j + 1)))
            pool.memset(att_st[:], 0.0).then_inc(s_dist, 1)
            for i, (t0, n) in enumerate(TILES):
                pool.wait_ge(s_krow, 2 * (i + 1))
                dst = new_k_p[0, 0, t0:t0 + n] if i < NTILE - 1 else new_k_s[0, 0]
                pool.dma_start(dst.rearrange("t h d -> t (h d)"), kb_rows[0:n, i % 2]).then_inc(s_kst[i % 2], 16)
            emptied(pool, units_of["vb"][-1])
            emptied(pool, units_of["vb"][-2])
            pool.dma_start(new_v_p[0, 0].rearrange("(i p) h d -> p i (h d)", p=P), vb[:, 0:4]).then_inc(s_vst, 16)
            pool.dma_start(new_v_s[0, 0].rearrange("t h d -> t (h d)"), vb[0:TS, 4]).then_inc(s_vst, 16)
            def head_bias(h):
                pool.tensor_scalar(bias[:, h % 2, 0:TP], dist[:], 2.0 ** -(h + 1), None, ALU.mult).then_inc(s_bias, 1)

            pool.wait_ge(s_bs, 1)
            head_bias(0)
            head_bias(1)
            pool.wait_ge(s_bias, 2)
            pool.wait_ge(s_unit, units_of["gb"][-1] + 1)
            for j in range(4):
                last = pool.iota(dist_s[32 * j:32 * j + 32], pattern=[[-1, PAST + TS]], base=PAST,
                                 channel_multiplier=1, allow_small_or_imprecise_dtypes=True)
            last.then_inc(s_dist_s, 1)
            pool.wait_ge(s_dist_s, 1)

            def load_cache(h):
                pool.dma_start(kraw[:, h % 2], cache_k[0, 0, :, h, :].rearrange("(c p) d -> p c d", p=P)).then_inc(s_kc[h % 2], 16)
                if h >= VBUF:
                    pool.wait_ge(s_hpv, h - VBUF + 1)
                pool.dma_start(vc[:, h % VBUF], cache_v[0, 0, :, h, :].rearrange("(c p) d -> p c d", p=P)).then_inc(s_vc[h % VBUF], 16)

            for h in range(2):
                load_cache(h)
            for h in range(2, DH):
                pool.wait_ge(s_tt, 8 * (h - 1))
                head_bias(h)
            for h in range(2, DH):
                pool.wait_ge(s_kcx, 2 * (h - 1))
                load_cache(h)
            pool.wait_ge(s_obT, DH + 2)
            for i in range(2):
                pool.wait_ge(s_kst[i], 16 * ((NTILE + 1 - i) // 2))
            pool.wait_ge(s_vst, 32)
            for i, (t0, n) in enumerate(TILES):
                src = x_prompt[0, t0:t0 + n] if i < NTILE - 1 else x_sample[0]
                pool.dma_start(x2[0:n, i], src).then_inc(s_x2[i], 16)
            pool.dma_start(gffn[:], norm_ffn.broadcast_to([P, D])).then_inc(s_g, 16)
            pool.dma_start(gfin[:], norm_final.unsqueeze(0).broadcast_to([P, D])).then_inc(s_g, 16)
            step(pool.iota(iota_e[:], pattern=[[1, NE]], base=0, channel_multiplier=0, allow_small_or_imprecise_dtypes=True))
            step(pool.iota(iota_s[:], pattern=[[1, CAP]], base=0, channel_multiplier=0, allow_small_or_imprecise_dtypes=True))
            step(pool.iota(iota_b[:, 0], pattern=[[1, NBLK]], base=1, channel_multiplier=0, allow_small_or_imprecise_dtypes=True))
            step(pool.iota(iota_b[:, 1], pattern=[[CAP, NBLK]], base=0, channel_multiplier=0, allow_small_or_imprecise_dtypes=True))
            step(pool.iota(tok_id[:], pattern=[[P, NTILE]], base=0, channel_multiplier=1, allow_small_or_imprecise_dtypes=True))
            step(pool.memset(upper[:], 1.0))
            step(pool.affine_select(out=upper[:], in_=upper[:], compare_op=ALU.is_gt, fill=0.0, base=0,
                                    pattern=[[1, P]], channel_multiplier=-1))
            step(pool.memset(chosen[:], 0.0))
            pool.memset(lg[:], 0.0).then_inc(s_c2, 1)

            def rows_in(i):
                n = TILES[i][1]
                pool.wait_ge(s_h2, i + 1)
                pool.dma_start(h2_rows[TILES[i][0]:TILES[i][0] + n], h2[0:n, i % 2]).then_inc(s_h2st[i % 2], 16)

            for i in range(NTILE):
                rows_in(i)
            pool.wait_ge(s_h2st[0], 48)
            pool.wait_ge(s_h2st[1], 32)
            for j in range(2):
                seq, buf, slot, _ = part_of(0, j)
                pool.wait_ge(s_ehi, seq + 1)
                pool.tensor_tensor(e_lo[:, buf], raw[:, slot], e_hi[:, buf].bitcast(F32), ALU.subtract).then_inc(s_elo, 1)
            pool.wait_ge(s_slot, 1)

            def gather(j, slot):
                pool.indirect_dma_start(xg[:, slot], None, h2_rows,
                                        bass.IndirectOffsetOnAxis(slot_i[:, j:j + 1], 0)).then_inc(s_xg[slot], 16)

            for e in range(NE):
                if e >= 2:
                    pool.wait_ge(s_xt, e - 1)
                gather(e, e % 2)
            pool.wait_ge(s_ovi, 1)
            n_ovf = pool.value_load(ovi[0:1, 0:1], min_val=0, max_val=NOVF)
            for i in range(NOVF):
                with pool.If(n_ovf > i):
                    pool.wait_ge(s_xt, NE + i)
                    gather(NE + i, 0)
            pool.wait_ge(s_yst[0], 16 * NE // 2)
            pool.wait_ge(s_yst[1], 16 * NE // 2)
            pool.wait_ge(s_exdone, 1)
            for i, (t0, n) in enumerate(TILES):
                for k in range(2):
                    pool.indirect_dma_start(yg[0:n, i, k], None, y_rows,
                                            bass.IndirectOffsetOnAxis(ysl[0:n, k, i:i + 1], 0)).then_inc(s_yg[i], 16)

        @block.scalar
        def _(act):
            steps = [0]

            def step(ins):
                steps[0] += 1
                ins.then_inc(s_act, 1)
                act.wait_ge(s_act, steps[0])

            for i, (t0, n) in enumerate(TILES):
                src = x_prompt[0, t0:t0 + n] if i < NTILE - 1 else x_sample[0]
                act.dma_start(x0[0:n, i], src).then_inc(s_x[i], 16)
            act.wait_ge(s_const, 1)

            def take_apart(n):
                act.wait_ge(s_w[n % RING], 16 * (n // RING + 1))
                if n >= 2:
                    act.wait_ge(s_unit, stage_units[n - 2][-1] + 1)
                act.activation(w_hi[:, n % 2], tile_ring(n), ACT.Copy).then_inc(s_hi, 1)

            def scale_x(i):
                n = TILES[i][1]
                act.wait_ge(s_xrs, i + 1)
                act.activation(x0[0:n, i], x0[0:n, i], ACT.Copy, scale=stat[0:n, 8 + i:9 + i]).then_inc(s_h, 1)

            for i, (t0, n) in enumerate(TILES):
                act.wait_ge(s_x[i], 16)
                step(act.activation(sq0[0:n], x0[0:n, i], ACT.Square, accum_out=stat[0:n, i:i + 1]))
                act.activation(stat[0:n, 8 + i:9 + i], stat[0:n, i:i + 1], ACT.Sqrt, bias=eps[0:n], scale=1.0 / D).then_inc(s_xsq, 1)
                if i:
                    scale_x(i - 1)
                if i == 3:
                    take_apart(0)
            scale_x(NTILE - 1)

            def output_apart(hi, src):
                for c in range(0, KC, 2):
                    act.activation(hi[:, c:c + 2], src[:, c:c + 2], ACT.Copy).then_inc(s_ohi, 1)

            def do(what, i=0):
                if what == "code":
                    act.wait_ge(s_code_mm, 1)
                    act.activation(code[:].rearrange("r (b t) -> r b t", b=2), ps[0:RANK, 4:6, 0:HALF], ACT.Copy).then_inc(s_code, 1)
                elif what == "dec":
                    if i < GH:
                        act.wait_ge(s_dec_mm, i + 1)
                        act.activation(t1[:, i].rearrange("p (b t) -> p b t", b=2), ps[:, 4 + 2 * (i % 2):6 + 2 * (i % 2), 0:HALF],
                                       ACT.Abs, bias=b_dec[:, i:i + 1]).then_inc(s_abs, 1)
                        act.wait_ge(s_abs, i + 1)
                        step(act.activation(t1[:, i], t1[:, i], ACT.Exp, scale=-1.0))
                        act.activation(t1[:, i], t1[:, i], ACT.Ln, bias=ones[:, 0:1]).then_inc(s_ln, 1)
                    if 1 <= i <= GH:
                        f = i - 1
                        act.wait_ge(s_delta, f + 1)
                        act.activation(t2[:, f], t2[:, f], ACT.Exp, scale=1.0 / TAU)
                        act.activation(t1[:, f], bT[:, f], ACT.Exp, scale=1.0 / TAU)
                        act.activation(t3[:, f], bT[:, f], ACT.Exp, scale=-1.0 / TAU)
                        act.activation(ebl[:, f, 0:8], bT[:, f, 0:TP].rearrange("p (c t) -> p c t", t=CHUNK)[:, :, CHUNK - 1],
                                       ACT.Exp, scale=1.0 / TAU)
                        act.activation(ebl[:, f, 8:9], bT[:, f, NT - 1:NT], ACT.Exp, scale=1.0 / TAU).then_inc(s_exps, 1)
                elif what == "kend":
                    n = TILES[i][1]
                    act.wait_ge(s_ke_mm, i + 1)
                    act.activation(kend[0:n, i].rearrange("p h d -> p (h d)"), ps[0:n, 4 + i % 4], ACT.Copy).then_inc(s_ke, 1)
                elif what == "gla":
                    n = TILES[i][1]
                    act.wait_ge(s_o, min(2 * i + 2, NCH))
                    for h in range(GH):
                        step(act.activation(sqa[0:n], ps[0:n, 5 + h // 2, DV * (h % 2):DV * (h % 2) + DV], ACT.Square,
                                            accum_out=stat[0:n, 16 + h:17 + h]))
                    if i:
                        act.wait_ge(s_og, i)
                    act.activation(stat[0:n, 20:24], stat[0:n, 16:20], ACT.Sqrt, bias=eps[0:n], scale=1.0 / DV).then_inc(s_osq, 1)
                elif what == "kout":
                    n, b = TILES[i][1], 3 + 2 * (i % 2)
                    act.wait_ge(s_kx, i + 1)
                    if i >= 2:
                        act.wait_ge(s_kst[i % 2], 16 * (i // 2))
                    for k in range(2):
                        act.activation(kb_rows[0:n, i % 2, 512 * k:512 * k + 512], ps[0:n, b + k], ACT.Copy).then_inc(s_krow, 1)
                elif what == "attn":
                    attention()
                    act.wait_ge(s_obT, DH + 2)
                    output_apart(ob_hi, qbT)
                elif what == "oa":
                    act.wait_ge(s_oaT, NTILE)
                    output_apart(oa_hi, fmA)
                elif what == "h2":
                    n = TILES[i][1]
                    emptied(act, last_wo[i])
                    step(act.activation(sq2[0:n], x2[0:n, i], ACT.Square, accum_out=stat[0:n, 40 + i:41 + i]))
                    act.activation(stat[0:n, 45 + i:46 + i], stat[0:n, 40 + i:41 + i], ACT.Sqrt, bias=eps[0:n], scale=1.0 / D).then_inc(s_2sq, 1)
                elif what == "turn":
                    n, b = TILES[i][1], 3 + 3 * (i % 2)
                    act.wait_ge(s_h2x, i + 1)
                    if i >= 2:
                        act.wait_ge(s_lgm, i - 1)
                    act.activation(h2T[:, i % 2, :, 0:n], ps[:, b:b + 2].rearrange("p b (c t) -> p (b c) t", t=P)[:, :, 0:n], ACT.Copy).then_inc(s_h2T, 1)

            def attention():
                def squares(h):
                    act.wait_ge(s_pvq, 4 * (h + 1))
                    if h:
                        act.wait_ge(s_row, h)
                    act.activation(ob[:], ps[:, 2 + 5 * (h % 2)], ACT.Square).then_inc(s_sqr, 1)

                def sample_roots(g):
                    act.wait_ge(s_hpv, 4 * (g + 1))
                    if g:
                        act.wait_ge(s_bx, DH + g)
                    act.activation(ob[0:TS], ps[0:TS, 0], ACT.Square).then_inc(s_sqr, 1)
                    act.wait_ge(s_brs, g + 1)
                    act.activation(stat[0:TS, 28:32], stat[0:TS, 24:28], ACT.Sqrt, bias=eps[0:TS], scale=1.0 / DVB).then_inc(s_bsq, 1)

                k = 0
                for h in range(DH):
                    for q in range(4):
                        w = P * (q + 1)
                        act.wait_ge(s_tt, 2 * k + 2)
                        for a in range(2):
                            last = act.activation(kept[q][:, a, 0:w], kept[q][:, a, 0:w], ACT.Exp, bias=att_st[:, q, a:a + 1],
                                                  scale=-1.0, accum_out=att_st[:, q, 2 + a:3 + a])
                        last.then_inc(s_exp, 1)
                        if k >= 1:
                            probs_out(k - 1)
                        if q == 2 and h:
                            squares(h - 1)
                        k += 1
                probs_out(k - 1)
                squares(DH - 1)
                act.wait_ge(s_row, DH)
                act.activation(head_st[:, 1], head_st[:, 0], ACT.Sqrt, bias=eps[:], scale=1.0 / DVB).then_inc(s_bsq, 1)
                for h in range(0, DH, 2):
                    act.wait_ge(s_bx, h + 1)
                    act.activation(qbT[:, h, 0:TP], ps[:, h], ACT.Copy, scale=g_diff_s).then_inc(s_obT, 1)
                for g in range(2):
                    for j in range(4):
                        h = 4 * g + j
                        for b in range(2):
                            act.wait_ge(s_kcx, 2 * h + b + 1)
                            if h >= 2:
                                act.wait_ge(s_ssc, h - 1)
                            act.activation(kcT[:, h % 2, 512 * b:512 * b + 512], ps[:, 6 + b], ACT.Copy).then_inc(s_kcT, 1)
                    act.wait_ge(s_stt, 2 * g + 2)
                    for b in range(2):
                        c = act.activation(scs[:, b], scs[:, b], ACT.Exp, bias=att_st[:, g, b:b + 1], scale=-1.0,
                                           accum_out=att_st[:, g, 2 + b:3 + b])
                    c.then_inc(s_sexp, 1)
                    if g == 0:
                        for b in range(2):
                            act.wait_ge(s_kst[b], 16 * ((NTILE + 1 - b) // 2))
                    for b in range(3):
                        nb = 4 if b < 2 else 1
                        rows = P if b < 2 else TS
                        act.wait_ge(s_spx, 3 * g + b + 1)
                        if b == 0 and g:
                            act.wait_ge(s_hpv, 4 * g)
                        act.activation(pTs_v[0:rows, 4 * b:4 * b + nb].rearrange("p c q -> p (c q)"),
                                       ps[0:rows, 6 + b % 2, 0:nb * P], ACT.Copy).then_inc(s_spT, 1)
                    sample_roots(g)

            def probs_out(k):
                w = P * (k % 4 + 1)
                act.wait_ge(s_px, k + 1)
                if k >= 2:
                    act.wait_ge(s_pvq, k - 1)
                act.activation(pT[:, k % 2, 0:w], ps[:, k % 2, 0:w], ACT.Copy).then_inc(s_pT, 1)

            take_apart(1)
            act.wait_ge(s_wcode, 96)
            act.activation(wc_hi[:, :, 0:RANK], w_code[:], ACT.Copy).then_inc(s_wc_hi, 1)
            act.wait_ge(s_lamp, 1)
            act.activation(lam[:, 2:4], lam[:, 0:2], ACT.Exp).then_inc(s_lame, 1)
            for u, d in enumerate(units):
                if d["eng"] == "A":
                    if u == first_qb or (u == first_qb + 1):
                        act.wait_ge(s_Sst, 32)
                    act.wait_ge(s_unit, u + 1)
                    kind, a, b, bank = d["kind"], d["a"], d["b"], bank_of[u]
                    if d["token_major"]:
                        dst, src = rows_of({"va": va, "ra": ra, "vb": vb}[kind], d, bank)
                        act.activation(dst, src, ACT.Silu if kind == "ra" else ACT.Copy).then_inc(s_ev["A"], 1)
                    else:
                        f = WC // P * d["nth"] + a
                        cols = slice(HALF * b, HALF * b + HALF)
                        dst = {"qa": fmA[:, f % 8, cols], "ka": fmA[:, (GH + f) % 8, cols], "ga": mixT[:, f, cols], "qb": qbT[:, f, cols],
                               "kb": kbT[:, f, cols], "gb": sgb[:, f, cols]}[kind]
                        if kind in ("ga", "gb"):
                            act.activation(dst, ps[:, bank, 0:HALF], ACT.Sigmoid).then_inc(s_ev["A"], 1)
                        elif kind == "qb":
                            act.activation(dst, ps[:, bank, 0:HALF], ACT.Copy, scale=-DQ ** -0.5).then_inc(s_ev["A"], 1)
                        else:
                            act.activation(dst, ps[:, bank, 0:HALF], ACT.Copy).then_inc(s_ev["A"], 1)
                if kind_of(u) == "pb":
                    a, b = d["a"], d["b"]
                    f = WC // P * d["nth"] + a
                    act.wait_ge(s_sum, u - units_of["pb"][0] + 1)
                    act.activation(m_hi[:, f, HALF * b:HALF * b + HALF], tmpm[:, b], ACT.Copy).then_inc(s_mhi, 1)
                if d["last"] and d["tile"] + RING < len(wtiles):
                    take_apart(d["tile"] + RING)
                for what in hooks.get(u, []):
                    do(*what)
            def part_hi(part):
                if part:
                    seq, buf, slot, loads = part
                    act.wait_ge(s_raw[slot], loads)
                    after(act, s_part, seq - (PBUF - 1))
                    act.activation(e_hi[:, buf], raw[:, slot], ACT.Copy).then_inc(s_ehi, 1)

            part_hi(part_of(0, 0))
            act.wait_ge(s_gd, 1)
            act.activation(rt[:, 0, 0:NTILE * NG], rt[:, 0, 0:NTILE * NG], ACT.Exp).then_inc(s_ge, 1)
            part_hi(part_of(0, 1))
            act.wait_ge(s_ed, 1)
            act.activation(rs[:, 8], rs[:, 8], ACT.Exp).then_inc(s_ee, 1)
            part_hi(part_of(0, 2))


            def x_out(e, slot):
                act.wait_ge(s_xt, e + 1)
                act.activation(x_hi[:, slot].rearrange("p c t -> p (c t)"), ps[:, 4:6].rearrange("p b n -> p (b n)"), ACT.Copy).then_inc(s_xhi, 1)

            def silu(e, up):
                act.wait_ge(s_part, up[0] + 1)
                after(act, s_hh, e)
                act.activation(sg[:], ps[:, 0], ACT.Silu).then_inc(s_sg, 1)

            def h_out(e):
                act.wait_ge(s_at, e + 1)
                act.activation(hh_hi[:].rearrange("p c t -> p (c t)"), ps[:, 2], ACT.Copy).then_inc(s_hhi, 1)

            def y_out(e, slot, down):
                act.wait_ge(s_part, down[0] + 1)
                act.activation(yo[:, slot], ps[:, 6:8].rearrange("p b n -> p (b n)"), ACT.Copy).then_inc(s_y, 1)
                act.wait_ge(s_y, e + 1)
                act.dma_start(y_of(e), yo[:, slot]).then_inc(s_yst[slot], 16)

            def y_of(e):
                return y_rows[bass.ds(e * CAP, CAP)]

            def store_count(e, slot):
                return (e - slot) * 8

            def body(r, odd, last=False):
                part_hi(third_after(r, 0))
                h_out(r - 1)
                part_hi(third_after(r, 1))
                if not last:
                    x_out(r + 1, 1 - odd)
                part_hi(third_after(r, 2))
                part_hi(third_after(r, 3))
                silu(r, part_of(r, 3))
                part_hi(third_after(r, 4))
                part_hi(third_after(r, 5))
                after(act, s_yst[1 - odd], store_count(r - 1, 1 - odd))
                y_out(r - 1, 1 - odd, part_of(r, 5))

            x_out(0, 0)
            part_hi(third_after(0, 0))
            x_out(1, 1)
            for j in range(1, 4):
                part_hi(third_after(0, j))
            silu(0, part_of(0, 3))
            body(1, 1)
            body(2, 0)
            with act.Fori(1, NE // 2 - 1) as it:
                body(it * 2 + 1, 1)
                body(it * 2 + 2, 0)
            body(NE - 1, 1, last=True)
            h_out(NE - 1)
            act.wait_ge(s_yst[1], store_count(NE - 1, 1))
            y_out(NE - 1, 1, part_of(NE, 5))
            act.wait_ge(s_zero, 16 * NOVF)
            act.wait_ge(s_ovi, 1)
            n_ovf = act.value_load(ovi[0:1, 0:1], min_val=0, max_val=NOVF)
            for i in range(NOVF):
                with act.If(n_ovf > i):
                    e = NE + i
                    x_out(e, 0)
                    for j in range(PARTS - 2):
                        part_hi(part_of(e + 1, j))
                    silu(e, part_of(e + 1, 3))
                    for j in range(PARTS - 2, PARTS):
                        part_hi(part_of(e + 1, j))
                    h_out(e)
                    act.wait_ge(s_yst[0], 16 * (NE // 2 + i))
                    y_out(e, 0, part_of(e + 1, 5))
                    act.wait_ge(s_yst[0], 16 * (NE // 2 + i + 1))
            act.activation(stat[:, 60:61], eps[:], ACT.Sqrt).then_inc(s_exdone, 1)
            for i, (t0, n) in enumerate(TILES):
                act.wait_ge(s_f, 2 * (i + 1))
                step(act.activation(sqf[0:n], x2[0:n, i], ACT.Square, accum_out=stat[0:n, 50 + i:51 + i]))
                act.activation(stat[0:n, 55 + i:56 + i], stat[0:n, 50 + i:51 + i], ACT.Sqrt, bias=eps[0:n], scale=1.0 / D).then_inc(s_fsq, 1)

        @block.tensor
        def _(pe):
            def transposes(ident_n, outs, done):
                for out, src in outs:
                    last = pe.transpose(out, src, ident[0:ident_n, 0:ident_n])
                last.then_inc(done, 1)

            pe.wait_ge(s_const, 1)
            for i, (t0, n) in enumerate(TILES):
                pe.wait_ge(s_h, i + 1)
                if i >= 2:
                    pe.wait_ge(s_hT, i - 1)
                b = 4 + 2 * (i % 2)
                transposes(n, [(ps[:, b + c // 4, P * (c % 4):P * (c % 4) + n], x0[0:n, i, P * c:P * c + P]) for c in range(KC)], s_hx)
            pe.wait_ge(s_hT, NTILE)

            def three_products(out, left, right, first, final):
                pe.matmul(out, left[0], right[0], start=first, stop=False)
                pe.matmul(out, left[0], right[1], start=False, stop=False)
                return pe.matmul(out, left[1], right[0], start=False, stop=final)

            def do(what, i=0):
                n = TILES[i][1] if i < NTILE else 0
                t0 = TILES[i][0] if i < NTILE else 0
                if what == "code":
                    pe.wait_ge(s_wc, 1)
                    for b in range(2):
                        cols = slice(HALF * b, HALF * b + HALF)
                        for c in range(KC):
                            last = three_products(ps[:, 4 + b, 0:HALF], (wc_hi[:, c], wc_lo[:, c]),
                                                  (h_hi[:, c, cols], h_lo[:, c, cols]), c == 0, c == KC - 1)
                    last.then_inc(s_code_mm, 1)
                elif what == "dec" and i < GH:
                    pe.wait_ge(s_code, 1)
                    if i >= 2:
                        pe.wait_ge(s_dec_rd, i - 1)
                        pe.wait_ge(s_ln, i - 1)
                    for b in range(2):
                        last = pe.matmul(ps[:, 4 + 2 * (i % 2) + b, 0:HALF], w_dec[:, P * i:P * i + P], code[:, HALF * b:HALF * b + HALF],
                                         start=True, stop=True)
                    last.then_inc(s_dec_mm, 1)
                elif what == "kend":
                    pe.wait_ge(s_qk, GH)
                    if i >= 4:
                        pe.wait_ge(s_ke, i - 3)
                    transposes(P, [(ps[0:n, 4 + i % 4, P * h:P * h + P], t2[:, h, t0:t0 + n]) for h in range(GH)], s_ke_mm)
                elif what == "gla":
                    gla_tile(i, t0, n)
                elif what == "gla_out":
                    pe.wait_ge(s_og, i + 1)
                    transposes(n, [(ps[:, 5 + c // 4, P * (c % 4):P * (c % 4) + n], ra[0:n, i, P * c:P * c + P]) for c in range(8)], s_ox)
                elif what == "kout":
                    b = 3 + 2 * (i % 2)
                    for u in units_of["kb"][-2:]:
                        emptied(pe, u)
                    if i >= 2:
                        pe.wait_ge(s_krow, 2 * (i - 1))
                    transposes(P, [(ps[0:n, b + h // 4, P * (h % 4):P * (h % 4) + P], kbT[:, h, t0:t0 + n]) for h in range(DH)], s_kx)
                elif what == "attn":
                    attention()
                elif what == "turn":
                    b = 3 + 3 * (i % 2)
                    pe.wait_ge(s_h2, i + 1)
                    if i >= 2:
                        pe.wait_ge(s_h2T, i - 1)
                    transposes(n, [(ps[:, b + c // 4, P * (c % 4):P * (c % 4) + n], h2[0:n, i % 2, P * c:P * c + P]) for c in range(KC)], s_h2x)
                elif what == "logits":
                    pe.wait_ge(s_h2T, i + 1)
                    for c in range(KC):
                        last = pe.matmul(ps[0:n, 5, (NG + NE) * i:(NG + NE) * (i + 1)], h2T[:, i % 2, c, 0:n], wr[:, c], start=c == 0, stop=c == KC - 1)
                    last.then_inc(s_lgm, 1)

            def gla_tile(i, t0, n):
                chunks = [2 * i, 2 * i + 1] if i < NTILE - 1 else [NCH - 1]
                m = CHUNK if i < NTILE - 1 else TS
                pe.wait_ge(s_ke, NTILE)
                for u in units_of["va"][-2:]:
                    emptied(pe, u)
                if i:
                    pe.wait_ge(s_oaT, i)
                for c in chunks:
                    p0, tc = CHUNK * (c % 2) if i < NTILE - 1 else 0, CHUNK * c
                    rows = slice(p0, p0 + m)
                    if c >= 2:
                        pe.wait_ge(s_att, c - 1)
                    for h in range(GH):
                        last = pe.matmul(ps[rows, 4, CHUNK * h:CHUNK * h + m], fmA[:, GH + h, tc:tc + m], fmA[:, h, tc:tc + m],
                                         start=True, stop=True)
                    last.then_inc(s_att_mm, 1)
                    if c:
                        pe.wait_ge(s_S, c)
                    for h in range(GH):
                        last = pe.matmul(ps[:, 3 + 4 * (h // 2), DV * (h % 2):DV * (h % 2) + DV], kend[rows, i, h], va[rows, i, DV * h:DV * h + DV],
                                         start=True, stop=True)
                    last.then_inc(s_dS, 1)
                    if c == NCH - 1:
                        pe.wait_ge(s_sin, 16)
                    pe.wait_ge(s_att, c + 1)
                    for h in range(GH):
                        out = ps[rows, 5 + h // 2, DV * (h % 2):DV * (h % 2) + DV]
                        if c:
                            state = S_in[:, h] if c == NCH - 1 else S[:, c % 2, h]
                            pe.matmul(out, fmA[:, h, tc:tc + m], state, start=True, stop=False)
                        last = pe.matmul(out, att[rows, h, 0:m], va[rows, i, DV * h:DV * h + DV], start=c == 0, stop=True)
                    last.then_inc(s_o, 1)
            def attention():
                for u in units_of["qb"][-2:] + units_of["vb"][-2:]:
                    emptied(pe, u)
                emptied(pe, units_of["gb"][-1])
                pe.wait_ge(s_krow, 2 * NTILE)

                def scores(k):
                    h, q = k // 4, k % 4
                    w, b = P * (q + 1), 3 + 2 * (k % 2)
                    if k >= 2:
                        pe.wait_ge(s_tt, 2 * (k - 1))
                    for a in range(2):
                        r = slice(DQ * a, DQ * a + DQ)
                        last = pe.matmul(ps[:, b + a, 0:w], qbT[r, h, P * q:P * q + P], kbT[r, h, 0:w], start=True, stop=True)
                    last.then_inc(s_scm, 1)

                def probs_t(k):
                    pe.wait_ge(s_pr, k + 1)
                    if k >= 2:
                        pe.wait_ge(s_pT, k - 1)
                    transposes(P, [(ps[:, k % 2, P * c:P * c + P], kept[k % 4][:, 0, P * c:P * c + P]) for c in range(k % 4 + 1)], s_px)

                def values(k):
                    h, q = k // 4, k % 4
                    bank = 2 + 5 * (h % 2)
                    pe.wait_ge(s_pT, k + 1)
                    if q == 0 and h >= 2:
                        pe.wait_ge(s_row, h - 1)
                    for c in range(q + 1):
                        last = pe.matmul(ps[:, bank, DVB * q:DVB * q + DVB], pT[:, k % 2, P * c:P * c + P], vb[:, c, DVB * h:DVB * h + DVB],
                                         start=c == 0, stop=c == q)
                    last.then_inc(s_pvq, 1)

                NK = 4 * DH
                scores(0)
                scores(1)
                for k in range(NK):
                    if k + 2 < NK:
                        scores(k + 2)
                    probs_t(k)
                    if k:
                        values(k - 1)
                values(NK - 1)
                pe.wait_ge(s_pT, NK)
                for h in range(DH):
                    pe.wait_ge(s_bo, h + 1)
                    transposes(P, [(ps[:, h, P * q:P * q + P], vb[:, q, DVB * h:DVB * h + DVB]) for q in range(4)], s_bx)
                pe.wait_ge(s_obT, DH)
                pe.wait_ge(s_pT, NK)
                for g in range(2):
                    for j in range(4):
                        h = 4 * g + j
                        pe.wait_ge(s_kc[h % 2], 16 * (h // 2 + 1))
                        for b in range(2):
                            if h:
                                pe.wait_ge(s_kcT, 2 * h - 1 + b)
                            if j == 0 and g:
                                pe.wait_ge(s_spT, 3 * g)
                            transposes(P, [(ps[:, 6 + b, P * c:P * c + P], kraw[:, h % 2, 4 * b + c]) for c in range(4)], s_kcx)
                        pe.wait_ge(s_kcT, 2 * h + 2)
                        if j == 0 and g:
                            pe.wait_ge(s_obT, DH + g)
                        rows = slice(32 * j, 32 * j + 32)
                        for a in range(2):
                            r = slice(DQ * a, DQ * a + DQ)
                            for b in range(2):
                                pe.matmul(ps[rows, 3 * a + b], qbT[r, h, TP:NT], kcT[r, h % 2, 512 * b:512 * b + 512], start=True, stop=True)
                            last = pe.matmul(ps[rows, 3 * a + 2, 0:TS], qbT[r, h, TP:NT], kbT[r, h, TP:NT], start=True, stop=True)
                        last.then_inc(s_ssc, 1)
                    pe.wait_ge(s_spr, g + 1)
                    for b in range(3):
                        if b == 2:
                            pe.wait_ge(s_spT, 3 * g + 1)
                        if b == 0:
                            pe.wait_ge(s_kcT, 8 * (g + 1))
                        if b < 2:
                            transposes(P, [(ps[:, 6 + b, P * c:P * c + P], scs[:, 0, 512 * b + P * c:512 * b + P * c + P]) for c in range(4)], s_spx)
                        else:
                            transposes(P, [(ps[0:TS, 6, 0:P], scs[:, 0, PAST:PAST + TS])], s_spx)
                    pe.wait_ge(s_spT, 3 * g + 3)
                    for j in range(4):
                        h = 4 * g + j
                        pe.wait_ge(s_vc[h % VBUF], 16 * (h // VBUF + 1))
                        for c in range(PAST // P + 1):
                            kk = P if c < PAST // P else TS
                            rhs = vc[:, h % VBUF, c] if c < PAST // P else vb[0:TS, 4, DVB * h:DVB * h + DVB]
                            last = pe.matmul(ps[0:TS, 0, DVB * j:DVB * j + DVB], pTs_v[0:kk, c, 32 * j:32 * j + 32], rhs,
                                             start=c == 0, stop=c == PAST // P)
                        last.then_inc(s_hpv, 1)
                    pe.wait_ge(s_bo, DH + g + 1)
                    transposes(TS, [(ps[:, 0, TS * j:TS * j + TS], ob[0:TS, P * j:P * j + P]) for j in range(4)], s_bx)

            for u, d in enumerate(units):
                n, kind, a, b, bank = d["tile"], d["kind"], d["a"], d["b"], bank_of[u]
                if d["first"]:
                    pe.wait_ge(s_lo, n + 1)
                    if kind == "wo" and d["nth"] == 0:
                        emptied(pe, units_of["pb"][-1])
                if u >= 3:
                    emptied(pe, u - 3)
                w = [part[:, n % 2].rearrange("p (c n) -> p c n", c=KC) for part in (w_hi, w_lo)]
                x = {"pa": (oa_hi, oa_lo), "pb": (ob_hi, ob_lo), "wo": (m_hi, m_lo)}.get(kind, (h_hi, h_lo))
                if d["token_major"]:
                    for k, (t0, m) in enumerate(TILES[a:a + 2]):
                        toks = slice(t0 + m - P, t0 + m)
                        for c in range(KC):
                            last = three_products(ps[:, bank, WC * k:WC * k + WC], (x[0][:, c, toks], x[1][:, c, toks]),
                                                  (w[0][:, c], w[1][:, c]), c == 0, c == KC - 1)
                else:
                    feats, cols = slice(P * a, P * a + P), slice(HALF * b, HALF * b + HALF)
                    for c in range(KC):
                        if u == units_of["pa"][0] and c % 2 == 0:
                            pe.wait_ge(s_olo, c // 2 + 1)
                        if u == units_of["pb"][0] and c % 2 == 0:
                            pe.wait_ge(s_olo, KC // 2 + c // 2 + 1)
                        last = three_products(ps[:, bank, 0:HALF], (w[0][:, c, feats], w[1][:, c, feats]),
                                              (x[0][:, c, cols], x[1][:, c, cols]), c == 0, c == KC - 1)
                last.then_inc(s_unit, 1)
                for what in hooks.get(u, []):
                    do(*what)
            pe.wait_ge(s_A, 1)
            pe.matmul(ps[:, 0, 0:NE * (NTILE + 1)], upper[:], chosen[:].rearrange("p i e -> p (i e)"), start=True, stop=False)
            for j in range(NTILE):
                last = pe.matmul(ps[:, 0, NE * (j + 1):NE * (NTILE + 1)].rearrange("p (i e) -> p i e", e=NE), ones[:],
                                 rep(chosen[:, j], 1, NTILE - j), start=False, stop=j == NTILE - 1)
            last.then_inc(s_rank, 1)
            for k in range(2):
                pe.wait_ge(s_oh, k + 1)
                for i, (t0, n) in enumerate(TILES):
                    last = pe.matmul(ps[:, 1, 0:NBLK], at_slot[0:n, k, i], in_block[0:n, k, i], start=k == 0 and i == 0,
                                     stop=k == 1 and i == NTILE - 1)
            last.then_inc(s_tok, 1)

            def XT(e, slot, count):
                pe.wait_ge(s_xg[slot], count)
                transposes(P, [(ps[:, 4 + c // 4, P * (c % 4):P * (c % 4) + P], xg[:, slot, P * c:P * c + P]) for c in range(KC)], s_xt)

            def GU(part, slot):
                seq, buf, j, _ = part
                pe.wait_ge(s_elo, seq + 1)
                for i in range(KC // 2):
                    c, w = KC // 2 * (j % 2) + i, slice(FE * i, FE * i + FE)
                    last = three_products(ps[:, j // 2], (x_hi[:, slot, c], x_lo[:, slot, c]), (e_hi[:, buf, w], e_lo[:, buf, w]),
                                          c == 0, c == KC - 1)
                last.then_inc(s_part, 1)

            def AT(e, slot):
                pe.wait_ge(s_hh, e + 1)
                transposes(P, [(ps[:, 2, P * c:P * c + P], hh[:, slot, P * c:P * c + P]) for c in range(FE // P)], s_at)

            def Dn(part):
                seq, buf, j, _ = part
                pe.wait_ge(s_elo, seq + 1)
                for i in range(2):
                    c = 2 * (j % 2) + i
                    for b in range(2):
                        w = slice(D * i + 512 * b, D * i + 512 * b + 512)
                        last = three_products(ps[:, 6 + b], (hh_hi[:, c], hh_lo[:, c]), (e_hi[:, buf, w], e_lo[:, buf, w]),
                                              c == 0, c == FE // P - 1)
                last.then_inc(s_part, 1)

            def count(e, slot):
                return (e - slot) * 8 + 16

            XT(0, 0, 16)
            pe.wait_ge(s_xlo, 1)
            GU(part_of(0, 0), 0)
            GU(part_of(0, 1), 0)
            XT(1, 1, 16)
            GU(part_of(0, 2), 0)
            GU(part_of(0, 3), 0)

            def body(r, odd, last=False):
                pe.wait_ge(s_hh, r)
                pe.wait_ge(s_xlo, r + 1)
                GU(part_of(r, 0), odd)
                AT(r - 1, 1 - odd)
                GU(part_of(r, 1), odd)
                if not last:
                    XT(r + 1, 1 - odd, count(r + 1, 1 - odd))
                GU(part_of(r, 2), odd)
                GU(part_of(r, 3), odd)
                after(pe, s_y, r - 1)
                pe.wait_ge(s_hlo, r)
                Dn(part_of(r, 4))
                Dn(part_of(r, 5))

            body(1, 1)
            body(2, 0)
            with pe.Fori(1, NE // 2 - 1) as it:
                body(it * 2 + 1, 1)
                body(it * 2 + 2, 0)
            body(NE - 1, 1, last=True)
            AT(NE - 1, 1)
            pe.wait_ge(s_y, NE - 1)
            pe.wait_ge(s_hlo, NE)
            Dn(part_of(NE, 4))
            Dn(part_of(NE, 5))
            pe.wait_ge(s_ovi, 1)
            n_ovf = pe.value_load(ovi[0:1, 0:1], min_val=0, max_val=NOVF)
            for i in range(NOVF):
                with pe.If(n_ovf > i):
                    e = NE + i
                    pe.wait_ge(s_y, e)
                    XT(e, 0, 16 * (NE // 2 + i + 1))
                    pe.wait_ge(s_xlo, e + 1)
                    for j in range(PARTS - 2):
                        GU(part_of(e + 1, j), 0)
                    AT(e, 0)
                    pe.wait_ge(s_hlo, e + 1)
                    for j in range(PARTS - 2, PARTS):
                        Dn(part_of(e + 1, j))

        @block.vector
        def _(dve):
            steps = [0]

            def step(ins):
                steps[0] += 1
                ins.then_inc(s_dve, 1)
                dve.wait_ge(s_dve, steps[0])

            dve.memset(att[:], 0.0).then_inc(s_mz, 1)
            def over_x_root(i):
                n = TILES[i][1]
                dve.wait_ge(s_xsq, i + 1)
                dve.reciprocal(stat[0:n, 8 + i:9 + i], stat[0:n, 8 + i:9 + i]).then_inc(s_xrs, 1)

            over_x_root(0)
            over_x_root(1)
            dve.wait_ge(s_gmix, 16)
            for i, (t0, n) in enumerate(TILES):
                if i + 2 < NTILE:
                    over_x_root(i + 2)
                dve.wait_ge(s_hx, i + 1)
                b = 4 + 2 * (i % 2)
                src = ps[:, b:b + 2].rearrange("p b (c t) -> p (b c) t", t=P)[:, :, 0:n]
                step(dve.tensor_tensor(h_hi[:, :, t0:t0 + n], src, rep(g_mix, 2, n), ALU.mult))
                for c in range(KC):
                    last = dve.scalar_tensor_tensor(h_lo[:, c, t0:t0 + n], src[:, c], g_mix[:, c:c + 1],
                                                    h_hi[:, c, t0:t0 + n].bitcast(F32), ALU.mult, ALU.subtract)
                last.then_inc(s_hT, 1)

            def take_apart(n):
                dve.wait_ge(s_hi, n + 1)
                dve.tensor_tensor(w_lo[:, n % 2], tile_ring(n), w_hi[:, n % 2].bitcast(F32), ALU.subtract).then_inc(s_lo, 1)

            def output_apart(lo, src, hi, done):
                for c in range(0, KC, 2):
                    dve.wait_ge(s_ohi, done + c // 2 + 1)
                    dve.tensor_tensor(lo[:, c:c + 2], src[:, c:c + 2], hi[:, c:c + 2].bitcast(F32), ALU.subtract).then_inc(s_olo, 1)

            def do(what, i=0):
                n = TILES[i][1] if i < NTILE else 0
                t0 = TILES[i][0] if i < NTILE else 0
                if what == "dec":
                    if i < GH:
                        dve.wait_ge(s_abs, i + 1)
                        src = ps[:, 4 + 2 * (i % 2):6 + 2 * (i % 2), 0:HALF]
                        dve.tensor_scalar(bT[:, i].rearrange("p (b t) -> p b t", b=2), src, b_dec[:, i:i + 1], 0.0, ALU.add, ALU.min).then_inc(s_dec_rd, 1)
                    if 1 <= i <= GH:
                        f = i - 1
                        dve.wait_ge(s_ln, f + 1)
                        dve.wait_ge(s_dec_rd, f + 1)
                        step(dve.tensor_tensor(t1[:, f], bT[:, f], t1[:, f], ALU.subtract))
                        step(dve.tensor_tensor_scan(bT[:, f], keep[:], t1[:, f], 0.0, ALU.mult, ALU.add))
                        bv = bT[:, f, 0:TP].rearrange("p (c t) -> p c t", t=CHUNK)
                        step(dve.tensor_tensor(t2[:, f, 0:TP].rearrange("p (c t) -> p c t", t=CHUNK),
                                               rep(bv[:, :, CHUNK - 1], 2, CHUNK), bv, ALU.subtract))
                        dve.tensor_scalar(t2[:, f, TP:NT], bT[:, f, TP:NT], bT[:, f, NT - 1:NT], -1.0, ALU.subtract, ALU.mult).then_inc(s_delta, 1)
                    if i >= 2:
                        f = i - 2
                        if f == 0:
                            for u in units_of["ka"][-2:] + units_of["qa"][-2:]:
                                emptied(dve, u)
                        dve.wait_ge(s_exps, f + 1)
                        step(dve.tensor_tensor(t2[:, f], t2[:, f], fmA[:, GH + f], ALU.mult))
                        step(dve.tensor_tensor(fmA[:, GH + f], fmA[:, GH + f], t3[:, f], ALU.mult))
                        dve.scalar_tensor_tensor(fmA[:, f], fmA[:, f], DK ** -0.5, t1[:, f], ALU.mult, ALU.mult).then_inc(s_qk, 1)
                elif what == "gla":
                    chunks = [2 * i, 2 * i + 1] if i < NTILE - 1 else [NCH - 1]
                    m = CHUNK if i < NTILE - 1 else TS
                    for c in chunks:
                        p0 = CHUNK * (c % 2) if i < NTILE - 1 else 0
                        rows = slice(p0, p0 + m)
                        dve.wait_ge(s_att_mm, c + 1)
                        dve.wait_ge(s_mz, 1)
                        dve.wait_ge(s_zero, 16 * NOVF)
                        if c >= 2:
                            dve.wait_ge(s_o, c - 1)
                        dve.copy_predicated(att[rows, :, 0:m], rep(trimask[rows, 0:m], 1, GH),
                                            ps[rows, 4, 0:GH * CHUNK].rearrange("p (h t) -> p h t", h=GH)[:, :, 0:m]).then_inc(s_att, 1)
                        dve.wait_ge(s_dS, c + 1)
                        if c:
                            dve.wait_ge(s_o, c)
                            dve.wait_ge(s_S, c)
                        if c == NCH - 1:
                            dve.wait_ge(s_sin, 16)
                        for h in range(GH):
                            dS = ps[:, 3 + 4 * (h // 2), DV * (h % 2):DV * (h % 2) + DV]
                            if c == 0:
                                last = dve.tensor_copy(S[:, 1, h], dS)
                            else:
                                last = dve.scalar_tensor_tensor(S[:, (c + 1) % 2, h], S_in[:, h] if c == NCH - 1 else S[:, c % 2, h],
                                                                ebl[:, h, c:c + 1], dS, ALU.mult, ALU.add)
                        last.then_inc(s_S, 1)
                    dve.wait_ge(s_osq, i + 1)
                    step(dve.reciprocal(stat[0:n, 32:36], stat[0:n, 20:24]))
                    if i == 0:
                        emptied(dve, units_of["ra"][-1])
                    for h in range(GH):
                        last = dve.scalar_tensor_tensor(ra[0:n, i, DV * h:DV * h + DV], ps[0:n, 5 + h // 2, DV * (h % 2):DV * (h % 2) + DV],
                                                        stat[0:n, 32 + h:33 + h], ra[0:n, i, DV * h:DV * h + DV], ALU.mult, ALU.mult)
                    last.then_inc(s_og, 1)
                elif what == "gla_out":
                    dve.wait_ge(s_ox, i + 1)
                    dve.tensor_tensor(fmA[:, :, t0:t0 + n], ps[:, 5:7].rearrange("p b (c t) -> p (b c) t", t=P)[:, :, 0:n],
                                      rep(g_gla, 2, n), ALU.mult).then_inc(s_oaT, 1)
                elif what == "dist":
                    dve.wait_ge(s_dist, 1)
                    step(dve.scalar_tensor_tensor(dist[:], dist[:], -1.0, dist[:], ALU.mult, ALU.max))
                    dve.memset(dist[0:CHUNK, TP - CHUNK:TP], BIG).then_inc(s_bs, 1)
                elif what == "attn":
                    attention()
                    output_apart(ob_lo, qbT, ob_hi, KC // 2)
                elif what == "oa":
                    output_apart(oa_lo, fmA, oa_hi, 0)
                elif what == "h2":
                    dve.wait_ge(s_2sq, i + 1)
                    step(dve.reciprocal(stat[0:n, 45 + i:46 + i], stat[0:n, 45 + i:46 + i]))
                    if i == 0:
                        dve.wait_ge(s_g, 32)
                    if i >= 2:
                        dve.wait_ge(s_h2st[i % 2], 16 * (i // 2))
                        dve.wait_ge(s_h2x, i - 1)
                    dve.scalar_tensor_tensor(h2[0:n, i % 2], x2[0:n, i], stat[0:n, 45 + i:46 + i], gffn[0:n], ALU.mult, ALU.mult).then_inc(s_h2, 1)

            def attention():
                def head_rows(h):
                    dve.wait_ge(s_sqr, h + 1)
                    dve.tensor_reduce(head_st[:, 0, 4 * h:4 * h + 4], ob[:].rearrange("p (q d) -> p q d", q=4), AX_X, ALU.add)
                    dve.tensor_copy(vb[:, 0:4, DVB * h:DVB * h + DVB],
                                    ps[:, 2 + 5 * (h % 2)].rearrange("p (q d) -> p q d", q=4)).then_inc(s_row, 1)

                def head_normed(h):
                    rows = vb[:, 0:4, DVB * h:DVB * h + DVB]
                    dve.tensor_tensor(rows, rows, rep(head_st[:, 2, 4 * h:4 * h + 4], 2, DVB), ALU.mult).then_inc(s_bo, 1)

                def sample_normed(g):
                    dve.wait_ge(s_sqr, DH + g + 1)
                    dve.tensor_reduce(stat[0:TS, 24:28], ob[0:TS].rearrange("p (q d) -> p q d", q=4), AX_X, ALU.add).then_inc(s_brs, 1)
                    dve.wait_ge(s_bsq, g + 2)
                    step(dve.reciprocal(stat[0:TS, 36:40], stat[0:TS, 28:32]))
                    dve.tensor_tensor(ob[0:TS].rearrange("p (q d) -> p q d", q=4), ps[0:TS, 0].rearrange("p (q d) -> p q d", q=4),
                                      rep(stat[0:TS, 36:40], 2, DVB), ALU.mult).then_inc(s_bo, 1)

                def head_out(k, dst, src):
                    dve.wait_ge(s_bx, k + 1)
                    dve.tensor_scalar(dst, src, g_diff_s, None, ALU.mult).then_inc(s_obT, 1)

                def combine(k):
                    w = P * (k % 4 + 1)
                    st, p = att_st[:, k % 4], kept[k % 4]
                    dve.wait_ge(s_exp, k + 1)
                    step(dve.reciprocal(st[:, 4:6], st[:, 2:4]))
                    step(dve.tensor_tensor(st[:, 5:6], st[:, 5:6], lam[:, 4:5], ALU.mult))
                    step(dve.tensor_scalar(p[:, 1, 0:w], p[:, 1, 0:w], st[:, 5:6], None, ALU.mult))
                    dve.scalar_tensor_tensor(p[:, 0, 0:w], p[:, 0, 0:w], st[:, 4:5], p[:, 1, 0:w], ALU.mult, ALU.add).then_inc(s_pr, 1)

                dve.wait_ge(s_vst, 32)
                for i in range(2):
                    dve.wait_ge(s_kst[i], 16 * ((NTILE + 1 - i) // 2))
                k = 0
                for h in range(DH):
                    dve.wait_ge(s_bias, h + 1)
                    for q in range(4):
                        w, b = P * (q + 1), 3 + 2 * (k % 2)
                        if q == 3:
                            combine(k - 1)
                        dve.wait_ge(s_scm, k + 1)
                        if k >= 4:
                            dve.wait_ge(s_px, k - 3)
                        for a in range(2):
                            dve.tensor_tensor_reduce(kept[q][:, a, 0:w], ps[:, b + a, 0:w], bias[:, h % 2, TP - w:TP], 1.0, 3.0e38,
                                                     ALU.add, ALU.min, att_st[:, q, a:a + 1]).then_inc(s_tt, 1)
                        if k and q < 3:
                            combine(k - 1)
                        if q == 3 and h:
                            head_rows(h - 1)
                        k += 1
                combine(k - 1)
                head_rows(DH - 1)
                dve.wait_ge(s_row, DH)
                dve.wait_ge(s_bsq, 1)
                step(dve.reciprocal(head_st[:, 2], head_st[:, 1]))
                for h in range(4):
                    head_normed(h)
                for h in range(1, DH, 2):
                    head_out(h, qbT[:, h, 0:TP], ps[:, h])
                    if h < 5:
                        head_normed(h + 3)
                        head_normed(h + 4)
                dve.wait_ge(s_dist_s, 1)
                step(dve.scalar_tensor_tensor(dist_s[:], dist_s[:], -1.0, dist_s[:], ALU.mult, ALU.max))
                for g in range(2):
                    step(dve.tensor_scalar(bias_s, dist_s[:], slope[:, g:g + 1], None, ALU.mult))
                    dve.wait_ge(s_ssc, 4 * g + 4)
                    if g:
                        dve.wait_ge(s_spx, 3 * g)
                    for a in range(2):
                        dve.tensor_tensor_reduce(scs[:, a], ps[:, 3 * a:3 * a + 3].rearrange("p b n -> p (b n)")[:, 0:PAST + TS],
                                                 bias_s, 1.0, 3.0e38, ALU.add, ALU.min, att_st[:, g, a:a + 1]).then_inc(s_stt, 1)
                    st = att_st[:, g]
                    dve.wait_ge(s_sexp, g + 1)
                    step(dve.reciprocal(st[:, 4:6], st[:, 2:4]))
                    step(dve.tensor_tensor(st[:, 5:6], st[:, 5:6], lam[:, 4:5], ALU.mult))
                    step(dve.tensor_scalar(scs[:, 1], scs[:, 1], st[:, 5:6], None, ALU.mult))
                    dve.scalar_tensor_tensor(scs[:, 0], scs[:, 0], st[:, 4:5], scs[:, 1], ALU.mult, ALU.add).then_inc(s_spr, 1)
                    sample_normed(g)
                    head_out(DH + g, qbT[:, 4 * g:4 * g + 4, TP:NT], ps[:, 0, 0:4 * TS].rearrange("p (j t) -> p j t", j=4))

            dve.wait_ge(s_small, 16 * 10)
            step(dve.tensor_tensor_reduce(lamt[:, 0], lamt[:, 0], lamt[:, 1], 1.0, 0.0, ALU.mult, ALU.add, lam[:, 0:1]))
            dve.tensor_tensor_reduce(lamt[:, 2], lamt[:, 2], lamt[:, 3], 1.0, 0.0, ALU.mult, ALU.add, lam[:, 1:2]).then_inc(s_lamp, 1)
            step(dve.tensor_scalar(g_diff_s, g_diff, 1.0 - LAM_INIT, None, ALU.mult))
            dve.wait_ge(s_wc_hi, 1)
            dve.tensor_tensor(wc_lo[:, :, 0:RANK], w_code[:], wc_hi[:, :, 0:RANK].bitcast(F32), ALU.subtract).then_inc(s_wc, 1)
            dve.wait_ge(s_lame, 1)
            step(dve.tensor_tensor(lam[:, 4:5], lam[:, 3:4], lam[:, 2:3], ALU.subtract))
            step(dve.tensor_scalar(lam[:, 4:5], lam[:, 4:5], LAM_INIT, None, ALU.subtract))
            dve.wait_ge(s_const, 2)
            dve.wait_ge(s_lo, 2)
            for u, d in enumerate(units):
                if d["eng"] == "D":
                    if u == first_qb or (u == first_qb + 1):
                        dve.wait_ge(s_Sst, 32)
                    dve.wait_ge(s_unit, u + 1)
                    kind, a, b, bank = d["kind"], d["a"], d["b"], bank_of[u]
                    if kind == "wo":
                        if d["nth"] == 0:
                            for k in range(a, min(a + 2, NTILE)):
                                dve.wait_ge(s_x2[k], 16)
                        dst, src = rows_of(x2, d, bank)
                        dve.tensor_tensor(dst, src, dst, ALU.add).then_inc(s_ev["D"], 1)
                    elif d["token_major"]:
                        dst, src = rows_of({"va": va, "ra": ra, "vb": vb}[kind], d, bank)
                        dve.tensor_copy(dst, src).then_inc(s_ev["D"], 1)
                    else:
                        f = WC // P * d["nth"] + a
                        cols = slice(HALF * b, HALF * b + HALF)
                        src = ps[:, bank, 0:HALF]
                        if kind == "pa":
                            emptied(dve, u_of("ga", d["nth"], a, b))
                            dve.tensor_tensor(mixT[:, f, cols], src, mixT[:, f, cols], ALU.mult).then_inc(s_ev["D"], 1)
                        elif kind == "pb":
                            emptied(dve, u_of("gb", d["nth"], a, b))
                            k = u - units_of["pb"][0]
                            step(dve.tensor_tensor(tmpm[:, b], src, sgb[:, f, cols], ALU.mult))
                            dve.tensor_tensor(tmpm[:, b], mixT[:, f, cols], tmpm[:, b], ALU.add).then_inc(s_sum, 1)
                            dve.wait_ge(s_mhi, k + 1)
                            dve.tensor_tensor(m_lo[:, f, cols], tmpm[:, b], m_hi[:, f, cols].bitcast(F32), ALU.subtract).then_inc(s_ev["D"], 1)
                        elif kind == "qb":
                            dve.tensor_scalar(qbT[:, f, cols], src, -DQ ** -0.5, None, ALU.mult).then_inc(s_ev["D"], 1)
                        else:
                            dst = {"qa": fmA[:, f % 8, cols], "ka": fmA[:, (GH + f) % 8, cols], "kb": kbT[:, f, cols]}[kind]
                            dve.tensor_copy(dst, src).then_inc(s_ev["D"], 1)
                if d["last"] and d["tile"] + RING < len(wtiles):
                    take_apart(d["tile"] + RING)
                for what in hooks.get(u, []):
                    do(*what)

            def t3d(k, n):
                return rt[:, k, 0:NTILE * n].rearrange("p (i e) -> p i e", e=n)

            dve.wait_ge(s_lgm, NTILE)
            dve.wait_ge(s_c2, 1)
            logits = ps[:, 5, 0:NTILE * (NG + NE)].rearrange("p (i e) -> p i e", i=NTILE)
            dve.tensor_tensor(lg[:, 0:NTILE - 1], logits[:, 0:NTILE - 1], rep(br[:], 1, NTILE - 1), ALU.add)
            step(dve.tensor_tensor(lg[0:TS, NTILE - 1], logits[0:TS, NTILE - 1], br[0:TS], ALU.add))
            gl, el = lg[:, :, 0:NG], lg[:, :, NG:NG + NE]
            step(dve.tensor_reduce(rs[:, 0], gl, AX_X, ALU.max))
            dve.tensor_tensor(t3d(0, NG), gl, rep(rs[:, 0], 2, NG), ALU.subtract).then_inc(s_gd, 1)

            def first_of(values, best, n, equal, cand, low, out):
                step(dve.tensor_tensor(equal, values, rep(best, 2, n), ALU.is_equal))
                step(dve.tensor_scalar(cand, equal, -64.0, None, ALU.mult))
                step(dve.tensor_tensor(cand, cand, rep(iota_e[:, 0:n], 1, NTILE), ALU.add))
                step(dve.tensor_reduce(low, cand, AX_X, ALU.min))
                step(dve.tensor_tensor(out, cand, rep(low, 2, n), ALU.is_equal))

            first_of(gl, rs[:, 0], NG, t3d(1, NG), t3d(2, NG), rs[:, 1], t3d(3, NG))
            step(dve.tensor_scalar(t3d(3, NG), t3d(3, NG), -1.0, BIG, ALU.add, ALU.mult))
            for i in range(NTILE):
                step(dve.tensor_tensor(t3d(4, NE)[:, i].rearrange("p (g e) -> p g e", g=NG), el[:, i].rearrange("p (g e) -> p g e", g=NG),
                                       rep(t3d(3, NG)[:, i], 2, EG), ALU.add))
            step(dve.tensor_reduce(rs[:, 2], t3d(4, NE), AX_X, ALU.max))
            first_of(t3d(4, NE), rs[:, 2], NE, t3d(5, NE), t3d(6, NE), rs[:, 3], t3d(7, NE))
            step(dve.scalar_tensor_tensor(t3d(4, NE), t3d(7, NE), -3.0 * BIG, t3d(4, NE), ALU.mult, ALU.add))
            step(dve.tensor_reduce(rs[:, 4], t3d(4, NE), AX_X, ALU.max))
            first_of(t3d(4, NE), rs[:, 4], NE, t3d(5, NE), t3d(6, NE), rs[:, 5], t3d(8, NE))
            dve.tensor_tensor(chosen[:, 0:NTILE - 1], t3d(7, NE)[:, 0:NTILE - 1], t3d(8, NE)[:, 0:NTILE - 1], ALU.add)
            dve.tensor_tensor(chosen[0:TS, NTILE - 1], t3d(7, NE)[0:TS, NTILE - 1], t3d(8, NE)[0:TS, NTILE - 1], ALU.add).then_inc(s_A, 1)
            dve.tensor_tensor(rs[:, 8], rs[:, 4], rs[:, 2], ALU.subtract).then_inc(s_ed, 1)
            dve.wait_ge(s_ge, 1)
            step(dve.tensor_reduce(rs[:, 6], t3d(0, NG), AX_X, ALU.add))
            step(dve.reciprocal(rs[:, 7], rs[:, 6]))
            dve.wait_ge(s_ee, 1)
            step(dve.tensor_scalar(rs[:, 9], rs[:, 8], 1.0, None, ALU.add))
            step(dve.reciprocal(rs[:, 10], rs[:, 9]))
            step(dve.tensor_tensor(rs[:, 11], rs[:, 10], rs[:, 7], ALU.mult))
            step(dve.tensor_tensor(rs[:, 12], rs[:, 11], rs[:, 8], ALU.mult))
            dve.wait_ge(s_rank, 1)
            dve.wait_ge(s_A, 1)
            rank = ps[:, 0, 0:NE * NTILE].rearrange("p (i e) -> p i e", e=NE)
            step(dve.tensor_copy(ov[:, 0], ps[:, 0, NE * NTILE:NE * NTILE + NE]))
            step(dve.scalar_tensor_tensor(t3d(10, NE), rank, 1.0, chosen[:, 0:NTILE], ALU.add, ALU.mult))
            step(dve.tensor_scalar(t3d(11, NE), t3d(10, NE), -1.0, None, ALU.add))
            step(dve.tensor_scalar(ov[:, 2], ov[:, 0], float(CAP), None, ALU.is_gt))
            for k in range(2, MORE + 1):
                step(dve.scalar_tensor_tensor(ov[:, 2], ov[:, 0], float(k * CAP), ov[:, 2], ALU.is_gt, ALU.add))
            step(dve.tensor_tensor_scan(ov[:, 3], ones[:, 0:NE], ov[:, 2], 0.0, ALU.mult, ALU.add))
            step(dve.tensor_tensor(ov[:, 4], ov[:, 3], ov[:, 2], ALU.subtract))
            step(dve.tensor_scalar(ov[:, 1], iota_e[:], float(CAP), None, ALU.mult))
            step(dve.tensor_scalar(ov[:, 6], ov[:, 4], NE - 1.0, float(CAP), ALU.add, ALU.mult))
            step(dve.tensor_tensor(ov[:, 6], ov[:, 6], ov[:, 1], ALU.subtract))
            step(dve.tensor_scalar(t3d(6, NE), t3d(11, NE), float(CAP), None, ALU.is_ge))
            step(dve.tensor_tensor(t3d(6, NE), t3d(6, NE), rep(ov[:, 6], 1, NTILE), ALU.mult))
            step(dve.tensor_tensor(t3d(5, NE), t3d(11, NE), rep(ov[:, 1], 1, NTILE), ALU.add))
            step(dve.tensor_tensor(t3d(5, NE), t3d(5, NE), t3d(6, NE), ALU.add))
            for k in range(2):
                step(dve.tensor_tensor(t3d(6, NE), t3d(5, NE), t3d(7 + k, NE), ALU.mult))
                step(dve.tensor_reduce(rs[:, 13 + k], t3d(6, NE), AX_X, ALU.add))
                step(dve.tensor_tensor(blk[:, k], rep(rs[:, 13 + k], 2, NBLK), rep(iota_b[:, 1], 1, NTILE), ALU.is_ge))
                step(dve.tensor_reduce(rs[:, 15], blk[:, k], AX_X, ALU.add))
                step(dve.tensor_tensor(blk[:, k], rep(rs[:, 15], 2, NBLK), rep(iota_b[:, 0], 1, NTILE), ALU.is_equal))
                dve.tensor_tensor(in_block[:, k], blk[:, k], rep(tok_id[:], 2, NBLK), ALU.mult)
                step(dve.tensor_scalar(rs[:, 15], rs[:, 15], 1.0, float(CAP), ALU.subtract, ALU.mult))
                step(dve.tensor_tensor(rs[:, 15], rs[:, 13 + k], rs[:, 15], ALU.subtract))
                step(dve.tensor_tensor(at_slot[:, k], rep(iota_s[:], 1, NTILE), rep(rs[:, 15], 2, CAP), ALU.is_equal))
                dve.tensor_copy(ysl[:, k], rs[:, 13 + k]).then_inc(s_oh, 1)
            dve.wait_ge(s_tok, 1)
            dve.tensor_copy(slot_i[:], ps[:, 1, 0:NBLK]).then_inc(s_slot, 1)
            ith = rep(iota_e[:, 0:NOVF], 2, NE)
            step(dve.tensor_tensor(ovm[:, :, 0], rep(ov[:, 4], 1, NOVF), ith, ALU.is_le))
            step(dve.tensor_tensor(ovm[:, :, 1], rep(ov[:, 3], 1, NOVF), ith, ALU.is_gt))
            step(dve.tensor_tensor(ovm[:, :, 0], ovm[:, :, 0], ovm[:, :, 1], ALU.mult))
            step(dve.tensor_tensor(ovm[:, :, 1], ovm[:, :, 0], rep(iota_e[:], 1, NOVF), ALU.mult))
            step(dve.tensor_reduce(ovb[:], ovm[:, :, 1], AX_X, ALU.add))
            step(dve.tensor_copy(ovi[:, 1:1 + NOVF], ovb[:]))
            dve.tensor_copy(ovi[:, 0:1], ov[:, 3, NE - 1:NE]).then_inc(s_ovi, 1)
            dve.wait_ge(s_ovi, 1)

            def part_lo(part):
                if part:
                    seq, buf, slot, _ = part
                    dve.wait_ge(s_ehi, seq + 1)
                    dve.tensor_tensor(e_lo[:, buf], raw[:, slot], e_hi[:, buf].bitcast(F32), ALU.subtract).then_inc(s_elo, 1)

            def x_out(e, slot):
                dve.wait_ge(s_xhi, e + 1)
                dve.tensor_tensor(x_lo[:, slot].rearrange("p c t -> p (c t)"), ps[:, 4:6].rearrange("p b n -> p (b n)"),
                                  x_hi[:, slot].bitcast(F32).rearrange("p c t -> p (c t)"), ALU.subtract).then_inc(s_xlo, 1)

            def gated(e, slot):
                dve.wait_ge(s_sg, e + 1)
                dve.tensor_tensor(hh[:, slot], ps[:, 1], sg[:], ALU.mult).then_inc(s_hh, 1)

            def h_out(e):
                dve.wait_ge(s_hhi, e + 1)
                dve.tensor_tensor(hh_lo[:].rearrange("p c t -> p (c t)"), ps[:, 2],
                                  hh_hi[:].bitcast(F32).rearrange("p c t -> p (c t)"), ALU.subtract).then_inc(s_hlo, 1)

            def body(r, odd, last=False):
                part_lo(third_after(r, 0))
                h_out(r - 1)
                part_lo(third_after(r, 1))
                if not last:
                    x_out(r + 1, 1 - odd)
                part_lo(third_after(r, 2))
                part_lo(third_after(r, 3))
                gated(r, odd)
                part_lo(third_after(r, 4))
                part_lo(third_after(r, 5))

            dve.wait_ge(s_elo, 2)
            part_lo(part_of(0, 2))
            x_out(0, 0)
            part_lo(third_after(0, 0))
            x_out(1, 1)
            for j in range(1, 4):
                part_lo(third_after(0, j))
            gated(0, 0)
            body(1, 1)
            body(2, 0)
            with dve.Fori(1, NE // 2 - 1) as it:
                body(it * 2 + 1, 1)
                body(it * 2 + 2, 0)
            body(NE - 1, 1, last=True)
            h_out(NE - 1)
            n_ovf = dve.value_load(ovi[0:1, 0:1], min_val=0, max_val=NOVF)
            for i in range(NOVF):
                with dve.If(n_ovf > i):
                    e = NE + i
                    x_out(e, 0)
                    for j in range(PARTS - 2):
                        part_lo(part_of(e + 1, j))
                    gated(e, 0)
                    for j in range(PARTS - 2, PARTS):
                        part_lo(part_of(e + 1, j))
                    h_out(e)
            def finish(i):
                n = TILES[i][1]
                dve.wait_ge(s_fsq, i + 1)
                step(dve.reciprocal(stat[0:n, 55 + i:56 + i], stat[0:n, 55 + i:56 + i]))
                dve.scalar_tensor_tensor(fo[0:n, i], x2[0:n, i], stat[0:n, 55 + i:56 + i], gfin[0:n], ALU.mult, ALU.mult).then_inc(s_fo, 1)

            for i, (t0, n) in enumerate(TILES):
                dve.wait_ge(s_yg[i], 32)
                for k in range(2):
                    dve.scalar_tensor_tensor(x2[0:n, i], yg[0:n, i, k], rs[0:n, 11 + k, i:i + 1], x2[0:n, i], ALU.mult, ALU.add).then_inc(s_f, 1)
                    dve.wait_ge(s_f, 2 * i + k + 1)
                if i:
                    finish(i - 1)
            finish(NTILE - 1)


_INS = ["x_prompt", "x_sample", "cache_k", "cache_v", "state_gla", "norm_mix", "w_in", "w_decay", "b_decay", "gla_norm",
        "w_proj_a", "lambda_q1", "lambda_k1", "lambda_q2", "lambda_k2", "diff_norm", "w_proj_b", "w_out", "norm_ffn",
        "w_router_group", "b_router_group", "w_router_expert", "b_router_expert", "w_gate", "w_up", "w_down", "norm_final"]
_OUTS = [(1, TP, D), (1, TS, D), (1, 1, TP, DH, 2 * DQ), (1, 1, TP, DH, DVB), (1, 1, GH, DK, DV),
         (1, 1, TS, DH, 2 * DQ), (1, 1, TS, DH, DVB), (1, 1, GH, DK, DV)]


def kernel(**inputs):
    import numpy as _np
    import concourse.bacc as _bacc
    from concourse import mybir as _mybir
    from concourse.bass_utils import run_bass_kernel_spmd as _run

    nc = _bacc.Bacc("TRN2", target_bir_lowering=False, num_devices=1)
    arrays, args = {}, []
    for name in _INS:
        a = _np.ascontiguousarray(inputs[name])
        arrays[f"in_{name}_dram"] = a
        args.append(nc.dram_tensor(f"in_{name}_dram", a.shape, _mybir.dt.from_np(a.dtype), kind="ExternalInput").ap())
    for i, shape in enumerate(_OUTS):
        args.append(nc.dram_tensor(f"out_{i}_dram", shape, F32, kind="ExternalOutput").ap())
    build(nc, *args)
    r = _run(nc, [arrays], core_ids=[0])
    return tuple(r.results[0][f"out_{i}_dram"] for i in range(len(_OUTS)))
```
